# Optimizing a Trainium2 kernel written in Bass

```python
import math
import jax, jax.numpy as jnp
from jax import lax
import numpy as np

D_MODEL = 2048
BATCH = 1
SEQ = 512
DEPTH = 1
DEC_BATCH = 8
DEC_SEQ = 1
PAST_LEN = 1024
PAGE_SIZE = 128

HEAD_DIM = 128
MIX_WIDTH = D_MODEL
W_DIFF = MIX_WIDTH // 2
DK_DIFF = HEAD_DIM
DV_DIFF = 2 * HEAD_DIM
H_DIFF = W_DIFF // DV_DIFF
W_DIL = MIX_WIDTH // 4
H_DIL = W_DIL // HEAD_DIM
DILATIONS = ((128, 1), (512, 4), (2048, 16))
MAX_WINDOW = 2048
W_MEM = MIX_WIDTH // 4
H_MEM = W_MEM // HEAD_DIM
N_MEM = 256

IN_WIDTH = 4 * W_DIFF + 4 * W_DIL + 2 * W_MEM
Q_BLOCK = 128
EPS = 1e-6
NEG_INF = -1e30

kernel_name = 'hymba_diff_dilated_mem_decoder_step'

def rms_norm(x, g):
    xf = x.astype(jnp.float32)
    y = xf * lax.rsqrt(jnp.mean(xf * xf, axis=-1, keepdims=True) + EPS)
    return (y * g.astype(jnp.float32)).astype(x.dtype)

def alibi_slopes():
    n = H_DIFF + H_DIL
    s = 2.0 ** (-8.0 * np.arange(1, n + 1) / n)
    return jnp.asarray(s[0::2][:H_DIFF], jnp.float32), jnp.asarray(s[1::2][:H_DIL], jnp.float32)

def diff_lambda(lq1, lk1, lq2, lk2, layer):
    lam_init = 0.8 - 0.6 * math.exp(-0.3 * layer)
    f = jnp.float32
    lam = (jnp.exp(jnp.sum(lq1.astype(f) * lk1.astype(f)))
           - jnp.exp(jnp.sum(lq2.astype(f) * lk2.astype(f))) + lam_init)
    return lam, lam_init

def split_projection(h, w_in):
    B, S = h.shape[:2]
    z = jnp.einsum('bsd,de->bse', h, w_in)
    widths = (W_DIFF, W_DIFF, W_DIFF, W_DIFF, W_DIL, W_DIL, W_DIL, W_DIL, W_MEM, W_MEM)
    cuts = [int(c) for c in np.cumsum(widths)[:-1]]
    qd, kd, vd, gd, qw, kw, vw, gw, qm, gm = jnp.split(z, cuts, axis=-1)
    qd = qd.reshape(B, S, H_DIFF, 2, DK_DIFF)
    kd = kd.reshape(B, S, H_DIFF, 2, DK_DIFF)
    vd = vd.reshape(B, S, H_DIFF, DV_DIFF)
    qw = qw.reshape(B, S, H_DIL, HEAD_DIM)
    kw = kw.reshape(B, S, H_DIL, HEAD_DIM)
    vw = vw.reshape(B, S, H_DIL, HEAD_DIM)
    qm = qm.reshape(B, S, H_MEM, HEAD_DIM)
    return qd, kd, vd, gd, qw, kw, vw, gw, qm, gm

def diff_attn_prompt(q, k, v, lam, slopes):
    B, S = q.shape[:2]
    nb = S // Q_BLOCK
    scale = DK_DIFF ** -0.5
    qb = q.reshape(B, nb, Q_BLOCK, H_DIFF, 2, DK_DIFF).transpose(1, 0, 2, 3, 4, 5)
    kpos = jnp.arange(S)

    def block(args):
        qblk, b = args
        qpos = b * Q_BLOCK + jnp.arange(Q_BLOCK)
        s = jnp.einsum('bqhcd,bkhcd->bhcqk', qblk, k, preferred_element_type=jnp.float32) * scale
        dist = (qpos[:, None] - kpos[None, :]).astype(jnp.float32)
        s = s - slopes[:, None, None, None] * dist
        s = jnp.where(dist >= 0, s, NEG_INF)
        p = jax.nn.softmax(s, axis=-1)
        a = p[:, :, 0] - lam * p[:, :, 1]
        return jnp.einsum('bhqk,bkhd->bqhd', a, v)

    o = lax.map(block, (qb, jnp.arange(nb)))
    return o.transpose(1, 0, 2, 3, 4).reshape(B, S, H_DIFF, DV_DIFF)

def diff_attn_sample(q, k_new, v_new, k_pool, v_pool, page_table, lam, slopes):
    DB, DS = q.shape[:2]
    past = page_table.shape[1] * PAGE_SIZE
    scale = DK_DIFF ** -0.5
    k_past = k_pool[page_table].reshape(DB, past, H_DIFF, 2, DK_DIFF)
    v_past = v_pool[page_table].reshape(DB, past, H_DIFF, DV_DIFF)
    qpos = past + jnp.arange(DS)
    d_past = (qpos[:, None] - jnp.arange(past)[None, :]).astype(jnp.float32)
    d_new = (qpos[:, None] - qpos[None, :]).astype(jnp.float32)
    s_past = jnp.einsum('bqhcd,bkhcd->bhcqk', q, k_past, preferred_element_type=jnp.float32) * scale
    s_past = s_past - slopes[:, None, None, None] * d_past
    s_new = jnp.einsum('bqhcd,bkhcd->bhcqk', q, k_new, preferred_element_type=jnp.float32) * scale
    s_new = jnp.where(d_new >= 0, s_new - slopes[:, None, None, None] * d_new, NEG_INF)
    p = jax.nn.softmax(jnp.concatenate([s_past, s_new], axis=-1), axis=-1)
    a = p[:, :, 0] - lam * p[:, :, 1]
    return (jnp.einsum('bhqk,bkhd->bqhd', a[..., :past], v_past)
            + jnp.einsum('bhqk,bkhd->bqhd', a[..., past:], v_new))

def dilated_branch_prompt(q, k, v, window, r, slopes):
    B, S, H, Dh = q.shape
    n_steps = window // r
    L = S // r
    nb = -(-L // Q_BLOCK)
    Lp = nb * Q_BLOCK
    scale = Dh ** -0.5

    def to_blocks(t):
        t = t.reshape(B, L, r, H, Dh).transpose(0, 2, 1, 3, 4)
        t = jnp.pad(t, ((0, 0), (0, 0), (0, Lp - L), (0, 0), (0, 0)))
        return t.reshape(B, r, nb, Q_BLOCK, H, Dh)

    def with_prev(t):
        prev = jnp.pad(t, ((0, 0), (0, 0), (1, 0), (0, 0), (0, 0), (0, 0)))[:, :, :-1]
        return jnp.concatenate([prev, t], axis=3)

    qb = to_blocks(q)
    kk = with_prev(to_blocks(k))
    vv = with_prev(to_blocks(v))
    s = jnp.einsum('brnqhd,brnkhd->brnhqk', qb, kk, preferred_element_type=jnp.float32) * scale
    qi = jnp.arange(nb)[:, None] * Q_BLOCK + jnp.arange(Q_BLOCK)[None, :]
    ki = jnp.arange(nb)[:, None] * Q_BLOCK - Q_BLOCK + jnp.arange(2 * Q_BLOCK)[None, :]
    steps = qi[:, :, None] - ki[:, None, :]
    valid = (steps >= 0) & (steps <= n_steps) & (ki[:, None, :] >= 0)
    s = s - slopes[:, None, None] * (r * steps).astype(jnp.float32)[:, None]
    s = jnp.where(valid[:, None], s, NEG_INF)
    lse = jax.nn.logsumexp(s, axis=-1)
    p = jnp.exp(s - lse[..., None])
    o = jnp.einsum('brnhqk,brnkhd->brnqhd', p, vv)
    o = o.reshape(B, r, Lp, H, Dh)[:, :, :L].transpose(0, 2, 1, 3, 4).reshape(B, S, H, Dh)
    lse = lse.transpose(0, 1, 2, 4, 3).reshape(B, r, Lp, H)[:, :, :L]
    lse = lse.transpose(0, 2, 1, 3).reshape(B, S, H)
    return o, lse

def combine_by_denominator(outs, lses):
    w = jax.nn.softmax(jnp.stack(lses, axis=0), axis=0)
    return jnp.sum(w[..., None] * jnp.stack(outs, axis=0), axis=0)

def dilated_prompt(q, k, v, slopes):
    outs, lses = [], []
    for window, r in DILATIONS:
        o, lse = dilated_branch_prompt(q, k, v, window, r, slopes)
        outs.append(o)
        lses.append(lse)
    return combine_by_denominator(outs, lses)

def dilated_sample(q, k_new, v_new, k_buf, v_buf, slopes):
    DB, DS, H, Dh = q.shape
    WB = k_buf.shape[1]
    scale = Dh ** -0.5
    kc = jnp.concatenate([k_buf, k_new], axis=1)
    vc = jnp.concatenate([v_buf, v_new], axis=1)
    outs, lses = [], []
    for window, r in DILATIONS:
        j = jnp.arange(window // r + 1)
        idx = WB + jnp.arange(DS)[:, None] - r * j[None, :]
        valid = idx >= 0
        idx = jnp.maximum(idx, 0)
        kg = kc[:, idx]
        vg = vc[:, idx]
        s = jnp.einsum('bqhd,bqjhd->bhqj', q, kg, preferred_element_type=jnp.float32) * scale
        s = s - slopes[:, None, None] * (r * j).astype(jnp.float32)[None, None, :]
        s = jnp.where(valid, s, NEG_INF)
        lse = jax.nn.logsumexp(s, axis=-1)
        p = jnp.exp(s - lse[..., None])
        outs.append(jnp.einsum('bhqj,bqjhd->bqhd', p, vg))
        lses.append(lse.transpose(0, 2, 1))
    return combine_by_denominator(outs, lses)

def memory_kv(mem, g_mem, w_mem_kv):
    B = mem.shape[0]
    m = rms_norm(mem, g_mem)
    kv = jnp.einsum('bmd,de->bme', m, w_mem_kv).reshape(B, N_MEM, 2, H_MEM, HEAD_DIM)
    return kv[:, :, 0], kv[:, :, 1]

def memory_attn(q, mk, mv):
    s = jnp.einsum('bshd,bmhd->bhsm', q, mk, preferred_element_type=jnp.float32) * HEAD_DIM ** -0.5
    p = jax.nn.softmax(s, axis=-1)
    return jnp.einsum('bhsm,bmhd->bshd', p, mv)

def gated_merge(od, gd, ow, gw, om, gm, g_sub, lam_init, w_out, dtype):
    B, S = gd.shape[:2]
    od = rms_norm(od, g_sub) * (1.0 - lam_init)
    cat = jnp.concatenate([
        od.reshape(B, S, W_DIFF) * jax.nn.silu(gd),
        ow.reshape(B, S, W_DIL) * jax.nn.silu(gw),
        om.reshape(B, S, W_MEM) * jax.nn.silu(gm)], axis=-1).astype(dtype)
    return jnp.einsum('bse,ed->bsd', cat, w_out)

def setup_inputs(seed: int = 0) -> dict:
    key = jax.random.key(seed)
    ks = jax.random.split(key, 24)
    f = jnp.float32
    n_pages = PAST_LEN // PAGE_SIZE
    n_used = DEC_BATCH * n_pages
    n_pool = n_used + n_used // 4
    win_buf = min(MAX_WINDOW, PAST_LEN)
    nrm = jax.random.normal
    return {
        'x_prompt': nrm(ks[0], (BATCH, SEQ, D_MODEL), f),
        'x_sample': nrm(ks[1], (DEC_BATCH, DEC_SEQ, D_MODEL), f),
        'mem_prompt': nrm(ks[2], (BATCH, N_MEM, D_MODEL), f),
        'cache_k_diff': nrm(ks[3], (DEPTH, n_pool, PAGE_SIZE, H_DIFF, 2, DK_DIFF), f),
        'cache_v_diff': nrm(ks[4], (DEPTH, n_pool, PAGE_SIZE, H_DIFF, DV_DIFF), f),
        'page_table': jax.random.permutation(ks[5], n_pool)[:n_used].reshape(DEC_BATCH, n_pages).astype(jnp.int32),
        'cache_k_win': nrm(ks[6], (DEPTH, DEC_BATCH, win_buf, H_DIL, HEAD_DIM), f),
        'cache_v_win': nrm(ks[7], (DEPTH, DEC_BATCH, win_buf, H_DIL, HEAD_DIM), f),
        'cache_mem_k': nrm(ks[8], (DEPTH, DEC_BATCH, N_MEM, H_MEM, HEAD_DIM), f),
        'cache_mem_v': nrm(ks[9], (DEPTH, DEC_BATCH, N_MEM, H_MEM, HEAD_DIM), f),
        'g_norm': 1.0 + 0.02 * nrm(ks[10], (DEPTH, D_MODEL), f),
        'w_in': nrm(ks[11], (DEPTH, D_MODEL, IN_WIDTH), f) * D_MODEL ** -0.5,
        'lambda_q1': 0.1 * nrm(ks[12], (DEPTH, DK_DIFF), f),
        'lambda_k1': 0.1 * nrm(ks[13], (DEPTH, DK_DIFF), f),
        'lambda_q2': 0.1 * nrm(ks[14], (DEPTH, DK_DIFF), f),
        'lambda_k2': 0.1 * nrm(ks[15], (DEPTH, DK_DIFF), f),
        'g_subln': 1.0 + 0.02 * nrm(ks[16], (DEPTH, DV_DIFF), f),
        'g_mem_norm': 1.0 + 0.02 * nrm(ks[17], (DEPTH, D_MODEL), f),
        'w_mem_kv': nrm(ks[18], (DEPTH, D_MODEL, 2 * W_MEM), f) * D_MODEL ** -0.5,
        'w_out': nrm(ks[19], (DEPTH, MIX_WIDTH, D_MODEL), f) * MIX_WIDTH ** -0.5,
        'g_final': 1.0 + 0.02 * nrm(ks[20], (D_MODEL,), f),
    }

def reference(x_prompt, x_sample, mem_prompt, cache_k_diff, cache_v_diff, page_table,
              cache_k_win, cache_v_win, cache_mem_k, cache_mem_v, g_norm, w_in,
              lambda_q1, lambda_k1, lambda_q2, lambda_k2, g_subln, g_mem_norm, w_mem_kv,
              w_out, g_final):
    slopes_diff, slopes_dil = alibi_slopes()
    yp, ys = x_prompt, x_sample
    kdp, vdp, kwp, vwp, mkp, mvp = [], [], [], [], [], []
    kds, vds, kws, vws = [], [], [], []
    for l in range(DEPTH):
        lam, lam_init = diff_lambda(lambda_q1[l], lambda_k1[l], lambda_q2[l], lambda_k2[l], l)
        hp = rms_norm(yp, g_norm[l])
        qd, kd, vd, gd, qw, kw, vw, gw, qm, gm = split_projection(hp, w_in[l])
        od = diff_attn_prompt(qd, kd, vd, lam, slopes_diff)
        ow = dilated_prompt(qw, kw, vw, slopes_dil)
        mk, mv = memory_kv(mem_prompt, g_mem_norm[l], w_mem_kv[l])
        om = memory_attn(qm, mk, mv)
        yp = yp + gated_merge(od, gd, ow, gw, om, gm, g_subln[l], lam_init, w_out[l], yp.dtype)
        keep = min(MAX_WINDOW, kw.shape[1])
        kdp.append(kd); vdp.append(vd)
        kwp.append(kw[:, -keep:]); vwp.append(vw[:, -keep:])
        mkp.append(mk); mvp.append(mv)
        hs = rms_norm(ys, g_norm[l])
        qd, kd, vd, gd, qw, kw, vw, gw, qm, gm = split_projection(hs, w_in[l])
        od = diff_attn_sample(qd, kd, vd, cache_k_diff[l], cache_v_diff[l], page_table, lam, slopes_diff)
        ow = dilated_sample(qw, kw, vw, cache_k_win[l], cache_v_win[l], slopes_dil)
        om = memory_attn(qm, cache_mem_k[l], cache_mem_v[l])
        ys = ys + gated_merge(od, gd, ow, gw, om, gm, g_subln[l], lam_init, w_out[l], ys.dtype)
        kds.append(kd); vds.append(vd); kws.append(kw); vws.append(vw)
    y_prompt = rms_norm(yp, g_final)
    y_sample = rms_norm(ys, g_final)
    return (y_prompt, y_sample,
            jnp.stack(kdp), jnp.stack(vdp), jnp.stack(kwp), jnp.stack(vwp),
            jnp.stack(mkp), jnp.stack(mvp),
            jnp.stack(kds), jnp.stack(vds), jnp.stack(kws), jnp.stack(vws))


_drawn_inputs = setup_inputs


def setup_inputs(seed=0):
    import zlib

    import numpy as np

    out = dict(_drawn_inputs(seed))
    spreads = {}
    factors = {'g_norm': 2.81, 'g_subln': 8.0, 'g_mem_norm': 2.825, 'g_final': 2.868}
    for name, (base, spread) in spreads.items():
        noise = np.random.default_rng([zlib.crc32(name.encode()), seed]).standard_normal(out[name].shape)
        drawn = base * np.exp(spread * noise) if base else spread * noise
        out[name] = __import__('jax').numpy.asarray(drawn.astype(out[name].dtype))
    for name, factor in factors.items():
        out[name] = (out[name] * factor).astype(out[name].dtype)
    return out
```

```python
import math
from contextlib import ExitStack

import numpy as np

import concourse.bass as bass
from concourse import mybir

F32 = mybir.dt.float32
F32R = mybir.dt.float32r
I32 = mybir.dt.int32
ALU = mybir.AluOpType
ACT = mybir.ActivationFunctionType
AX_X = mybir.AxisListType.X

P = 128
D_MODEL = 2048
KT = D_MODEL // P
SEQ = 512
NBLK = SEQ // P
DB = 8
TOK = SEQ + DB
HALF = TOK // 2
N_MEM = 256
H = 4
PAGES = 8
PAST = PAGES * P
SCALE = P ** -0.5
EPS = 1e-6
LAM_INIT = 0.8 - 0.6 * math.exp(-0.3 * 0)
MASKED = -1e30
LOWEST = -3e38

WIN_RING = 8
SPLIT_RING = 4
AHEAD = 3
PAGE_RING = 6

COL = dict(qd=0, kd=1024, vd=2048, gd=3072, qw=4096, kw=4608, vw=5120, gw=5632, qm=6144, gm=6656)


def slopes():
    s = 2.0 ** (-8.0 * np.arange(1, 2 * H + 1) / (2 * H))
    return s[0::2], s[1::2]


def branch_count(dist):
    n = np.zeros(dist.shape)
    for window, r in ((128, 1), (512, 4), (2048, 16)):
        n += (dist >= 0) & (dist <= window) & (dist % r == 0)
    return n


def log_count(n):
    return np.where(n > 0, np.log(np.maximum(n, 1)), MASKED)


def constants():
    sd, sw = slopes()
    dist = 3 * P + np.arange(P)[:, None] - np.arange(SEQ)[None, :]
    out = np.zeros((2 * H, P, SEQ))
    for h in range(H):
        out[h] = np.where(dist >= 0, -sd[h] * dist, MASKED)
        out[H + h] = np.where(branch_count(dist) > 0, -sw[h] * dist + log_count(branch_count(dist)), MASKED)
    key = np.arange(P)
    bd = -(PAST - (np.arange(PAGES)[None, :, None] * P + key[:, None, None])) * sd[None, None, :]
    far = np.concatenate([PAST - np.arange(512, 896, 4), PAST - np.arange(0, 512, 16)])
    bw = np.zeros((P, 2, 2, H))
    for t, d in enumerate((PAST - (896 + key), far)):
        bw[:, t, 0] = -d[:, None] * sw[None, :] + log_count(branch_count(d))[:, None]
    bn = np.zeros((2, 2, DB, H))
    bn[1, 0] = math.log(3.0)
    bn[1, 1] = MASKED
    small = np.concatenate([bd.reshape(P, -1), bw.reshape(P, -1), np.broadcast_to(bn.reshape(1, -1), (P, 128))], axis=1)
    return ((out / SCALE).astype(np.float32), (small / SCALE).astype(np.float32), np.eye(P, dtype=np.float32))


def tiles():
    out = [("mk", j, 0) for j in range(H)] + [("mv", j, 0) for j in range(H)]
    out += [("qd", h, c) for h in range(H) for c in range(2)]
    for h in range(H):
        out += [(kind, h, c) for kind in ("kd", "vd", "gd") for c in range(2)]
    out += [("qw", j, 0) for j in range(H)] + [("qm", j, 0) for j in range(H)] + [("kw", j, 0) for j in range(H)]
    out += [(kind, j, 0) for j in range(H) for kind in ("vw", "gw")]
    out += [("gm", j, 0) for j in range(H)]
    out += [("y", e, 0) for e in range(KT)]
    return out


TILES = tiles()
AT = {t: n for n, t in enumerate(TILES)}
N_TILES = len(TILES)
QUARTERS = 4 * N_TILES
FIRST_IN = AT["qd", 0, 0]
FIRST_OUT = AT["y", 0, 0]
IN_END = 4 * FIRST_OUT
KEEP = KT
N_PREP = KT // 2


def cat_slot(kind, h, c):
    return {"qd": 2 * h + c, "qw": 2 * H + h, "qm": 3 * H + h, "gm": 3 * H + h}[kind]


def att_steps():
    out = []
    for h in range(H):
        s0 = 4 * (AT["gd", h, 1] + 1) + 2
        period = 6 if h < H - 1 else 4
        out += [("diff", h, i, s0 + period * i) for i in range(NBLK)]
    s = out[-1][3] + 5
    for j in range(H):
        s = max(s, 4 * (AT["qm", j, 0] + 1) + 1)
        for pair in range(2):
            out.append(("mem", j, pair, s))
            s += 2
    s += 1
    for j in range(H):
        s = max(s, 4 * (AT["gw", j, 0] + 1) + 2)
        for i in range(NBLK):
            out.append(("dil", j, i, s))
            s += 2
    return out


STEPS = att_steps()


def plan():
    n_slots = QUARTERS + 8
    slots = [[] for _ in range(n_slots)]
    load = [0.65] * n_slots

    def put(s, kind, what=None, cost=0.0):
        slots[s].append((kind, what))
        load[s] += cost

    for u in range(N_PREP):
        put(2 + u, "prep", (1, u), 0.7)
    put(11, "prep_sample", None, 0.7)
    for u in range(N_PREP):
        put(31 if u < 4 else 32, "prep", (2, u), 0.7)
    for n, (kind, h, c) in enumerate(TILES):
        s = 4 * n + 4
        put(s, "evac", n, 0.65 if kind in ("gd", "gw") else 1.3 if kind == "gm" else 0.0)
        if kind in ("mk", "mv", "kd", "kw", "vd", "vw"):
            put(s + 1, "nat", n)
        if kind == "y":
            put(s + 1, "ynat", n, 0.8)
    put(4 * (AT["qd", 3, 1] + 1) + 1, "qrows", 0)
    put(4 * (AT["qm", 3, 0] + 1) + 1, "qrows", 1)
    put(4 * (AT["vw", 3, 0] + 1) + 3, "kvrows", 0)
    put(4 * (AT["vw", 3, 0] + 1) + 4, "kvrows", 1)
    for t, (kind, h, i, s) in enumerate(STEPS):
        w = (i + 1) * P
        put(s, "A", t, {"diff": 3.5 * w * 1.04e-3 + 0.4, "mem": 1.0, "dil": w * 1.04e-3 + 0.3}[kind])
        put(s + 1, "P", t, 0.0)
        put(s + 2, "B", t)
        put(s + 3, "C", t, {"diff": 0.35, "mem": 0.35, "dil": 0.2}[kind])
        if kind == "diff":
            put(s + 4, "D", t, 0.45)
    seq = []
    summed = {}
    BUDGET = 2.8
    K0 = 4 * (AT["qd", 3, 1] + 1) + 4
    seq += [("dk", u, K0, 0.83) for u in range(128)]
    seq += [("soft", (0, k), 4 * (AT["kd", 3, 1] + 1) + 2 + k, 1.6) for k in range(4)]
    for u in range(128):
        seq.append(("dv", u, 0, 0.70))
        if u % 8 == 7:
            seq.append(("do", u // 8, 0, 0.1))
    W0 = 4 * (AT["qm", 3, 0] + 1) + 4
    seq += [("dk", u, W0, 0.83) for u in range(128, 160)]
    seq += [("soft", (1, k), 4 * (AT["kw", 3, 0] + 1) + 2 + k, 1.0) for k in range(4)]
    for u in range(128, 160):
        seq.append(("dv", u, 0, 0.83))
        if u % 2:
            seq.append(("do", 16 + (u - 128) // 2, 0, 0.1))
    seq += [("fin", k, 4 * (AT["gw", 3, 0] + 1) + 2 + k, 0.8) for k in range(3)]
    s = 0
    for kind, what, least, cost in seq:
        s = max(s, least)
        if kind == "dv":
            i = what // 8 if what < 128 else 16 + (what - 128) // 2
            s = max(s, summed.get(i - 2, 0))
        while sum(load[s - 3:s + 1]) + cost > 4 * BUDGET and not (kind in ("soft", "fin", "do")):
            s += 1
        if what == 0 and kind == "fin":
            s += 2
        put(s + (kind == "do"), kind, what, cost)
        if kind == "do":
            summed[what] = s + 1
        if kind in ("soft", "fin"):
            s += 1
    assert summed[31] < 4 * AT["gm", 0, 0] + 4 and s < IN_END, s
    rank = {"evac": 0, "P": 1, "B": 2, "D": 3, "C": 4, "A": 5}
    used = {"tb": 0, "ob": 0, "sb": 0}
    bank = {"nat": "tb", "ynat": "tb ob", "qrows": "tb", "kvrows": "tb", "A": "sb", "B": "tb", "C": "ob", "D": "tb", "do": "ob"}
    out = []
    for jobs in slots:
        row = []
        for kind, what in sorted(jobs, key=lambda j: rank.get(j[0], 6)):
            banks = bank.get(kind, "")
            if kind == "soft":
                banks = ("tb", "ob", "ob", "")[what[1]]
            if kind == "fin":
                banks = "ob" if what == 1 else ""
            use = {}
            for b in banks.split():
                use[b] = used[b]
                used[b] += 1
            row.append((kind, what, use))
        out.append(row)
    return out, used


PLAN, USED = plan()
USE = {(kind, what): use for jobs in PLAN for kind, what, use in jobs}
SLOT = {(kind, what): s for s, jobs in enumerate(PLAN) for kind, what, _ in jobs}
LAST_STEP = {}
for _t, (_kind, _h, _i, _s) in enumerate(STEPS):
    LAST_STEP[_kind, _h] = _t
NAT_K = [n for n, t in enumerate(TILES) if t[0] in ("mk", "kd", "kw")]
NAT_V = [n for n, t in enumerate(TILES) if t[0] in ("mv", "vd", "vw")]
PAIRS = 3


ORDER_OF = {0: 0, 1: 1, 2: 2, 3: 3, 6: 4, 4: 5, 5: 6}
KEPT_KINDS = ("qd", "qw", "qm", "kd", "kw", "vd", "vw", "gd", "gw")
KEPT = {}
for _tile in TILES:
    if _tile[0] in KEPT_KINDS:
        KEPT[_tile] = len(KEPT) + 1
TANHS = {n: i for i, n in enumerate(n for n, t in enumerate(TILES) if t[0][0] == "g")}
RECS, SCORES_READ = {}, {}
for _t, _step in enumerate(STEPS):
    if _step[0] != "diff":
        RECS[_t] = len(RECS)
    SCORES_READ[_t] = sum(x[0] != "mem" for x in STEPS[:_t + 1])


def unit(u):
    if u < 128:
        return 0, u // 64, u // 8 % 8, u % 8
    u -= 128
    return 1, u // 16, u // 2 % 8, u % 2


UNITS = [(s, kind == "dv", what) for s, jobs in enumerate(PLAN) for kind, what, _ in jobs if kind in ("dk", "dv")]
UNIT_AT = {(value, u): i for i, (_, value, u) in enumerate(UNITS)}
LANDED = []
for _i, (_, _value, _u) in enumerate(UNITS):
    _g, _c, _b, _tile = unit(_u)
    _before = LANDED[_i - PAGE_RING] if _i >= PAGE_RING else 0
    LANDED.append(_before + (32 if (_g, _c, _tile) == (1, 0, 1) else 16))


def hybrid_decoder(nc, x_prompt, x_sample, mem_prompt, cache_k_diff, cache_v_diff, page_table, cache_k_win,
                   cache_v_win, cache_mem_k, cache_mem_v, g_norm, w_in, lambda_q1, lambda_k1, lambda_q2, lambda_k2,
                   g_subln, g_mem_norm, w_mem_kv, w_out, g_final, bias_tables, bias_small, identity,
                   y_prompt, y_sample, k_diff_prompt, v_diff_prompt, k_win_prompt, v_win_prompt, mem_k_prompt,
                   mem_v_prompt, k_diff_sample, v_diff_sample, k_win_sample, v_win_sample, q_rows_dram):
    with ExitStack() as ctx:
        def sb(name, shape, dt=F32):
            return ctx.enter_context(nc.sbuf_tensor(name, shape, dt))

        def sem(name):
            return ctx.enter_context(nc.semaphore(name))

        act_hi = sb("act_hi", [P, KT, TOK], F32R)
        act_lo = sb("act_lo", [P, KT, TOK], F32R)
        w_raw = sb("w_raw", [P, WIN_RING, 4 * P])
        w_hi = sb("w_hi", [P, SPLIT_RING, 4 * P], F32R)
        w_lo = sb("w_lo", [P, SPLIT_RING, 4 * P], F32R)
        cat = sb("cat", [P, KT * TOK])
        cat_t = cat[:, :].rearrange("p (k t) -> p k t", k=KT)
        nat = cat[:, 0:NBLK * D_MODEL].rearrange("p (t f) -> p t f", t=NBLK)
        kT = sb("kT", [P, 4 * TOK])
        kT_t = kT[:, :].rearrange("p (k t) -> p k t", k=4)
        gate = sb("gate", [P, 4 * TOK])
        gate_t = gate[:, :].rearrange("p (k t) -> p k t", k=4)
        v_nat = sb("v_nat", [P, 2, NBLK, 2 * P])
        k_nat = sb("k_nat", [P, NBLK, P])
        tall = sb("tall", [P, TOK])
        mk_T = sb("mk_T", [P, H, N_MEM])
        mv_nat = sb("mv_nat", [P, 2, H * P])
        bias = sb("bias", [P, 2, SEQ])
        probs = sb("probs", [P, 2, SEQ])
        probs_T = sb("probs_T", [P, SEQ])
        o_nat = sb("o_nat", [P, 2 * P])
        pages = sb("pages", [P, PAGE_RING, 512])
        q_bc = sb("q_bc", [P, 2, 512])
        v_acc = sb("v_acc", [P, 2, 512])
        dec_s = sb("dec_s", [P, 512])
        dec_a = sb("dec_a", [P, PAGES, DB * H])
        ident = sb("ident", [P, P])
        ones = sb("ones", [P, P])
        b_small = sb("b_small", [P, PAGES * H + 4 * H + P])
        rows = sb("rows", [P, 2, P])
        q_s = sb("q_s", [P, KT, DB])
        k_s = sb("k_s", [P, 12, DB])
        v_s = sb("v_s", [P, 12, DB])
        g_s = sb("g_s", [P, 12, DB])
        o_s = sb("o_s", [P, 16, DB])
        gn = sb("gn", [P, KT])
        gmn = sb("gmn", [P, KT])
        gsub = sb("gsub", [P, 2])
        gsub_c = sb("gsub_c", [P, 2])
        lam_in = sb("lam_in", [P, 4])
        lam_w = sb("lam_w", [P, 8])
        power = sb("power", [P, 32])
        ids = sb("ids", [1, DB * PAGES], I32)
        tok_ss = sb("tok_ss", [P, 8])
        tok_r = sb("tok_r", [P, 8])
        tok_s = sb("tok_s", [P, KT, DB])
        a_new = sb("a_new", [P, 2, DB * H])
        tmp = sb("tmp", [P, H, DB])
        y_ss = sb("y_ss", [P, 5, KT])
        y_sum = sb("y_sum", [P, 5])
        y_r = sb("y_r", [P, 5])
        st_m = sb("st_m", [P, 2, 2])
        st_n = sb("st_n", [P, 2, 2])
        st_l = sb("st_l", [P, 2, 2])
        st_r = sb("st_r", [P, 2, 3])
        st_q = sb("st_q", [P, 2, 2])
        dc = sb("dc", [P, 8, 64])
        z = [ctx.enter_context(nc.psum_tensor(f"z{i}", [P, 2, 512], F32)) for i in range(2)]
        s_ps = ctx.enter_context(nc.psum_tensor("s_ps", [P, 2, 512], F32))
        t_ps = ctx.enter_context(nc.psum_tensor("t_ps", [P, 512], F32))
        o_ps = ctx.enter_context(nc.psum_tensor("o_ps", [P, 512], F32))

        SMALL = ["ident", "bsmall", "gn", "gmn", "gsub", "lam", "ids"]
        s_const = sem("const_loaded")
        s_tok = [sem(f"tokens_loaded{i}") for i in range(7)]
        s_ss = sem("token_squares")
        s_r1 = sem("token_mean")
        s_rr = sem("token_rstd")
        s_scaled = sem("tokens_scaled")
        s_pfull = sem("prep_full")
        s_phi = sem("prep_hi")
        s_plo = sem("prep_lo")
        s_raw = [sem(f"weights_loaded{i}") for i in range(WIN_RING)]
        s_hi = sem("weights_hi")
        s_lo = sem("weights_lo")
        s_quarter = sem("quarter_multiplied")
        s_zfree = [sem("z0_free"), sem("z1_free")]
        s_tanh = sem("gate_tanh")
        s_bias = [sem("bias_loaded0"), sem("bias_loaded1")]
        s_sfull, s_sfree = sem("scores_full"), sem("scores_free")
        s_tfull, s_tfree = sem("turned_full"), sem("turned_free")
        s_ofull, s_ofree = sem("out_full"), sem("out_free")
        s_max, s_exp, s_rec, s_probs = sem("row_max"), sem("probs_exp"), sem("probs_rec"), sem("probs_ready")
        s_osq, s_opow1, s_orstd = sem("o_squares"), sem("o_mean"), sem("o_rstd")
        s_kout, s_vout = sem("k_stored"), [sem("v_stored0"), sem("v_stored1")]
        s_mvout = sem("mv_stored")
        s_keep = sem("sample_columns_kept")
        s_lam, s_lamp, s_lame = sem("lambda_products"), sem("lambda_sums"), sem("lambda_exp")
        s_neglam = sem("lambda_ready")
        s_init = sem("constants_set")
        s_qrow, s_qdram = sem("q_rows_ready"), sem("q_rows_stored")
        s_kvrow, s_kvout = sem("kv_rows_ready"), [sem("k_rows_stored"), sem("v_rows_stored")]
        s_qbc = [sem("q_bc_loaded0"), sem("q_bc_loaded1")]
        s_page = [sem(f"page_loaded{i}") for i in range(PAGE_RING)]
        s_unit = sem("unit_done")
        s_dsm, s_dexp = sem("decode_softmax_dve"), sem("decode_exp")
        s_dprod = sem("new_key_products")
        s_fin, s_finp = sem("decode_out_dve"), sem("decode_out_rstd")
        s_gated = sem("memory_gated")
        s_chi, s_clo = sem("cat_hi"), sem("cat_lo")
        s_res = [sem(f"residual_loaded{i}") for i in range(5)]
        s_gf = sem("g_final_loaded")
        s_ysq = sem("y_squares")
        s_yr, s_yrp = sem("y_mean"), sem("y_rstd")
        s_ydone = [sem(f"y_done{i}") for i in range(5)]
        s_yout = sem("y_stored")
        s_chain = sem("vector_chain")
        s_pchain = sem("pool_chain")
        s_achain = sem("scalar_chain")

        x_t = x_prompt.rearrange("a (t p) f -> (a t) p f", p=P)
        m_t = mem_prompt.rearrange("a (t p) f -> (a t) p f", p=P)
        xs = x_sample.rearrange("b a f -> (b a) f")
        w_dram = {"m": w_mem_kv, "i": w_in, "o": w_out}
        w_view = {k: v.rearrange("a (r k p) f -> (a r) p k f", r=4, p=P) for k, v in w_dram.items()}
        kpages = cache_k_diff.rearrange("a n p h c d -> (a n) p (h c d)")
        vpages = cache_v_diff.rearrange("a n p h d -> (a n) p (h d)")
        kwin = cache_k_win.rearrange("a b w h d -> (a b) w (h d)")
        vwin = cache_v_win.rearrange("a b w h d -> (a b) w (h d)")
        kmem = cache_mem_k.rearrange("a b w h d -> (a b) w (h d)")
        vmem = cache_mem_v.rearrange("a b w h d -> (a b) w (h d)")
        out_nat = {
            "kd": k_diff_prompt.rearrange("a b (t p) h c d -> p (a b t) (h c d)", p=P),
            "vd": v_diff_prompt.rearrange("a b (t p) h d -> p (a b t) (h d)", p=P),
            "kw": k_win_prompt.rearrange("a b (t p) h d -> p (a b t) (h d)", p=P),
            "vw": v_win_prompt.rearrange("a b (t p) h d -> p (a b t) (h d)", p=P),
            "mk": mem_k_prompt.rearrange("a b (t p) h d -> p (a b t) (h d)", p=P),
            "mv": mem_v_prompt.rearrange("a b (t p) h d -> p (a b t) (h d)", p=P),
        }
        out_rows = [
            [(k_diff_sample.rearrange("a b s h c d -> (a b s) (h c d)"), 8), (k_win_sample.rearrange("a b s h d -> (a b s) (h d)"), 4)],
            [(v_diff_sample.rearrange("a b s h d -> (a b s) (h d)"), 8), (v_win_sample.rearrange("a b s h d -> (a b s) (h d)"), 4)],
        ]
        x_s_nat = kT[0:DB, 0:D_MODEL]
        y_s_nat = gate[0:DB, 0:D_MODEL]
        g_fin = pages[:, 0:4, :].rearrange("p a b -> p (a b)")
        bd = b_small[:, 0:PAGES * H].rearrange("p (t h) -> p t h", h=H)
        bw = b_small[:, PAGES * H:PAGES * H + 4 * H].rearrange("p (t h) -> p t h", h=H)
        bn = b_small[:, PAGES * H + 4 * H:].rearrange("p (g n) -> p g n", g=2)
        SAMPLE = slice(SEQ, TOK)
        PROD, SNEW, MB, M1, L1, LR, DIAG, SQ = (dc[:, i, :] for i in range(8))

        def par(kind, h):
            return h % 2

        def key_slot(kind, h, c):
            return 2 * (h % 2) + c if kind == "kd" else h

        def gate_slot(kind, h, c):
            return {"gd": 2 * (h % 2) + c, "gw": 2 * (h % 2), "gm": 2 * (h % 2) + 1}[kind]

        def sample_slot(kind, h, c):
            return 2 * h + c if kind[1] == "d" else 8 + h

        def quarter_source(q):
            n, r = divmod(q, 4)
            kind, h, c = TILES[n]
            if n < FIRST_IN:
                col = (h + (H if kind == "mv" else 0)) * P
                return w_view["m"][r, :, :, col:col + P]
            if n < FIRST_OUT:
                col = COL[kind] + (2 * h + c if kind[1] == "d" else h) * P
                return w_view["i"][r, :, :, col:col + P]
            return w_view["o"][r, :, :, h * P:(h + 1) * P]

        def bias_index(kind, h):
            return h if kind == "diff" else H + h

        block = ctx.enter_context(nc.Block())

        @block.sync
        def _(sp):
            def weights(q):
                if q >= WIN_RING:
                    sp.wait_ge(s_lo, q - WIN_RING + 1)
                dst = w_raw[:, q % WIN_RING, :].rearrange("p (k f) -> p k f", k=4)
                sp.dma_start(dst, quarter_source(q)).then_inc(s_raw[q % WIN_RING], 16)

            def bias_table(i):
                if i >= 2:
                    prev = ("diff", i - 2) if i - 2 < H else ("dil", i - 2 - H)
                    sp.wait_ge(s_sfree, SCORES_READ[LAST_STEP[prev]])
                sp.dma_start(bias[:, i % 2, :], bias_tables[i]).then_inc(s_bias[i % 2], 16)

            def q_broadcast(i):
                if i >= 2:
                    sp.wait_ge(s_unit, 8 * (i - 1) if i - 2 < 16 else 256 + 2 * (i - 17))
                sp.wait_ge(s_qdram, 16 if i < 16 else 32)
                c, b = divmod(i, DB) if i < 16 else divmod(i - 16, DB)
                first = (0 if i < 16 else 8) + 4 * c
                src = q_rows_dram.rearrange("(t b) d -> b t d", b=DB)[b:b + 1, first:first + 4, :]
                dst = q_bc[:, i % 2, :].rearrange("p (t d) -> p t d", t=4)
                sp.dma_start(dst, src.broadcast_to((P, 4, P))).then_inc(s_qbc[i % 2], 16)

            page_ids = {}

            def cache_unit(seq, value, u):
                g, c, b, t = unit(u)
                slot = seq % PAGE_RING
                if seq >= PAGE_RING:
                    sp.wait_ge(s_unit, seq - PAGE_RING + 1)
                dst = pages[:, slot, :]
                if g == 0:
                    if t == 0:
                        for k in range(PAGES):
                            page_ids[k] = sp.value_load(ids[0:1, b * PAGES + k:b * PAGES + k + 1], min_val=0,
                                                        max_val=kpages.shape[0] - 1)
                    src = (vpages if value else kpages)[bass.ds(page_ids[t], 1), :, c * 512:(c + 1) * 512]
                    sp.dma_start(dst, src.rearrange("a p f -> (a p) f")).then_inc(s_page[slot], 16)
                elif c == 1:
                    src = (vmem if value else kmem)[b, t * P:(t + 1) * P, :]
                    sp.dma_start(dst, src).then_inc(s_page[slot], 16)
                elif t == 0:
                    src = (vwin if value else kwin)[b, PAST - P:PAST, :]
                    sp.dma_start(dst, src).then_inc(s_page[slot], 16)
                else:
                    cache = vwin if value else kwin
                    n4 = 96
                    near = cache[b, 512:896, :].rearrange("(k r) f -> k r f", r=4)[:, 0, :]
                    far = cache[b, 0:512, :].rearrange("(k r) f -> k r f", r=16)[:, 0, :]
                    sp.dma_start(dst[0:n4, :], near).then_inc(s_page[slot], 16)
                    sp.dma_start(dst[n4:P, :], far).then_inc(s_page[slot], 16)

            sp.dma_start(nat[:, 0, :], m_t[0]).then_inc(s_tok[0], 16)
            sp.dma_start(nat[:, 1, :], m_t[1]).then_inc(s_tok[1], 16)
            sp.dma_start(ident[:, :], identity).then_inc(s_const, 16)
            sp.dma_start(b_small[:, :], bias_small).then_inc(s_const, 16)
            for dst, src in ((gn, g_norm), (gmn, g_mem_norm)):
                sp.dma_start(dst[:, :], src.rearrange("a (k p) -> p (a k)", p=P),
                             allow_slow_non_contiguous=True).then_inc(s_const, 16)
            sp.dma_start(gsub[:, :], g_subln.rearrange("a (k p) -> p (a k)", p=P),
                         allow_slow_non_contiguous=True).then_inc(s_const, 16)
            for i, v in enumerate((lambda_q1, lambda_k1, lambda_q2, lambda_k2)):
                sp.dma_start(lam_in[:, i:i + 1], v.rearrange("a p -> p a"),
                             allow_slow_non_contiguous=True).then_inc(s_const, 16)
            sp.dma_start(ids[:, :], page_table.rearrange("(a b) n -> a (b n)", a=1)).then_inc(s_const, 16)
            for q in range(4):
                weights(q)
            for i in range(2, 4):
                sp.dma_start(nat[:, i, :], x_t[i]).then_inc(s_tok[i], 16)
            sp.dma_start(x_s_nat, xs).then_inc(s_tok[6], 16)
            for q in range(4, WIN_RING - 1):
                weights(q)
            sp.wait_ge(s_pfull, N_PREP)
            for i in range(2):
                sp.dma_start(nat[:, i, :], x_t[i]).then_inc(s_tok[4 + i], 16)
            sp.wait_ge(s_const, 16 * 10)
            bias_table(0)
            bias_table(1)

            order = UNITS
            sent = 0
            q_sent = 0
            for s, jobs in enumerate(PLAN):
                if WIN_RING - 1 + s < QUARTERS:
                    weights(WIN_RING - 1 + s)
                while sent < len(order) and order[sent][0] <= s + 3 and sent < PAGE_RING + sum(
                        1 for o in order[:sent + 1] if o[0] < s):
                    _, value, u = order[sent]
                    if not value:
                        need = (u // 8 if u < 128 else 16 + (u - 128) // 2) + 1
                        if SLOT["qrows", 0 if u < 128 else 1] >= s - 1:
                            break
                        while q_sent < need:
                            q_broadcast(q_sent)
                            q_sent += 1
                    cache_unit(sent, value, u)
                    sent += 1
                for i in range(2, 2 * H):
                    prev = ("diff", i - 2) if i - 2 < H else ("dil", i - 2 - H)
                    if SLOT["A", LAST_STEP[prev]] + 1 == s:
                        bias_table(i)
                for kind, what, use in (PLAN[s - 1] if s else []):
                    if kind == "nat":
                        tile_kind, h, c = TILES[what]
                        j = 2 * h + c if tile_kind[1] == "d" else h
                        dst = out_nat[tile_kind][:, :, j * P:(j + 1) * P]
                        if tile_kind in ("mk", "kd", "kw"):
                            sp.wait_ge(s_tfree, use["tb"] + 1)
                            nb = 2 if tile_kind == "mk" else NBLK
                            sp.dma_start(dst, k_nat[:, 0:nb, :]).then_inc(s_kout, 16)
                        elif tile_kind == "mv":
                            sp.wait_ge(s_tfree, use["tb"] + 1)
                            sp.dma_start(dst, mv_nat[:, :, j * P:(j + 1) * P]).then_inc(s_mvout, 16)
                        else:
                            sp.wait_ge(s_tfree, use["tb"] + 1)
                            sp.dma_start(dst, v_nat[:, h % 2, :, c * P:(c + 1) * P]).then_inc(s_vout[h % 2], 16)
                    if kind == "qrows":
                        sp.wait_ge(s_tfree, use["tb"] + 1)
                        sp.dma_start(q_rows_dram[what * 64:what * 64 + 64, :], rows[0:64, what, :]).then_inc(s_qdram, 16)
                    if kind == "kvrows":
                        sp.wait_ge(s_tfree, use["tb"] + 1)
                        row = 0
                        for dst, nt in out_rows[what]:
                            for t in range(nt):
                                sp.dma_start(dst[:, t * P:(t + 1) * P], rows[row:row + DB, what, :]).then_inc(s_kvout[what], 16)
                                row += DB
                if s == IN_END + 2:
                    sp.wait_ge(s_clo, KT)
                    for i in range(NBLK):
                        sp.dma_start(nat[:, i, :], x_t[i]).then_inc(s_res[i], 16)
                    sp.dma_start(y_s_nat, xs).then_inc(s_res[4], 16)
                    sp.wait_ge(s_unit, len(order))
                    sp.dma_start(g_fin, g_final.rearrange("(a f) -> a f", a=1).broadcast_to((P, D_MODEL))).then_inc(s_gf, 16)
            assert sent == len(order)
            for i in range(NBLK):
                sp.wait_ge(s_ydone[i], 1)
                sp.dma_start(y_prompt.rearrange("a (t p) f -> (a t) p f", p=P)[i], nat[:, i, :]).then_inc(s_yout, 16)
            sp.wait_ge(s_ydone[4], 1)
            sp.dma_start(y_sample.rearrange("b a f -> (b a) f"), y_s_nat).then_inc(s_yout, 16)
            sp.wait_ge(s_yout, 16 * 5)
            sp.wait_ge(s_kout, 16 * len(NAT_K))
            sp.wait_ge(s_mvout, 16 * H)
            for i in range(2):
                sp.wait_ge(s_vout[i], 16 * (4 + 2))
                sp.wait_ge(s_kvout[i], 16 * 12)
            sp.wait_ge(s_qdram, 32)

        def prep_base(pair):
            return {0: 0, 1: N_PREP, 2: 2 * N_PREP + 1}[pair]

        @block.tensor
        def _(pe):
            def prep(pair, u):
                use = prep_base(pair) + u
                pe.wait_ge(s_scaled, (2, 4, 7)[pair])
                if use >= 2:
                    pe.wait_ge(s_plo, use - 1)
                first = 2 if pair == 1 else 0
                for k in range(2):
                    for t in range(2):
                        kt = 2 * u + k
                        last = nc.tensor.transpose(s_ps[:, use % 2, (2 * k + t) * P:(2 * k + t + 1) * P],
                                                   nat[:, first + t, kt * P:(kt + 1) * P], ident[:, :])
                last.then_inc(s_pfull, 1)

            def prep_sample():
                use = 2 * N_PREP
                pe.wait_ge(s_scaled, 5)
                pe.wait_ge(s_plo, use - 1)
                for kt in range(KT):
                    last = nc.tensor.transpose(s_ps[:, use % 2, kt * DB:(kt + 1) * DB],
                                               x_s_nat[:, kt * P:(kt + 1) * P], ident[0:DB, 0:DB])
                last.then_inc(s_pfull, 1)

            def quarter(q):
                n, r = divmod(q, 4)
                zb = z[n % 2]
                if r == 0 and n >= 2:
                    pe.wait_ge(s_zfree[n % 2], n // 2)
                pe.wait_ge(s_lo, q + 1)
                if n == FIRST_IN:
                    pe.wait_ge(s_plo, prep_base(2) + 2 * r + 2)
                if n == 0:
                    pe.wait_ge(s_plo, 2 * r + 2)
                if n == FIRST_OUT:
                    pe.wait_ge(s_clo, 4 * r + 4)
                hi, lo = w_hi[:, q % SPLIT_RING, :], w_lo[:, q % SPLIT_RING, :]
                parts = [(0, 0, N_MEM)] if n < FIRST_IN else [(0, 0, HALF), (1, HALF, TOK)]
                for j in range(4):
                    kt = 4 * r + j
                    w = slice(j * P, (j + 1) * P)
                    for m, (lhs, rhs) in enumerate(((hi, act_hi), (hi, act_lo), (lo, act_hi))):
                        for bank, a, b in parts:
                            last = nc.tensor.matmul(zb[:, bank, 0:b - a], lhs[:, w], rhs[:, kt, a:b],
                                                    start=(kt == 0 and m == 0), stop=(kt == KT - 1 and m == 2))
                last.then_inc(s_quarter, 1)

            def turn_ready(use):
                if use["tb"] >= 1:
                    pe.wait_ge(s_tfree, use["tb"])

            def out_ready(use):
                if use["ob"] >= 1:
                    pe.wait_ge(s_ofree, use["ob"])

            def natural(n, use):
                kind, h, c = TILES[n]
                pe.wait_ge(s_zfree[n % 2], n // 2 + 1)
                turn_ready(use)
                src = {"mk": lambda: mk_T[:, h, :], "kd": lambda: kT_t[:, key_slot(kind, h, c), :],
                       "kw": lambda: kT_t[:, key_slot(kind, h, c), :]}.get(kind, lambda: tall[:, :])()
                for b in range(2 if kind[0] == "m" else NBLK):
                    last = nc.tensor.transpose(t_ps[:, b * P:(b + 1) * P], src[:, b * P:(b + 1) * P], ident[:, :])
                if kind == "y":
                    last.then_inc(s_tfull, 1)
                    out_ready(use)
                    last = nc.tensor.transpose(o_ps[0:DB, 0:P], src[:, SAMPLE], ident[:, :])
                    last.then_inc(s_ofull, 1)
                else:
                    last.then_inc(s_tfull, 1)

            def step_scores(t, use):
                kind, h, i, _ = STEPS[t]
                if t and STEPS[t - 1][0] == "mem":
                    pe.wait_ge(s_exp, t)
                elif t:
                    pe.wait_ge(s_sfree, SCORES_READ[t - 1])
                if kind == "diff":
                    n = AT["kd", h, 1]
                    pe.wait_ge(s_zfree[n % 2], n // 2 + 1)
                    for c in range(2):
                        last = nc.tensor.matmul(s_ps[:, c, 0:(i + 1) * P], cat_t[:, 2 * h + c, i * P:(i + 1) * P],
                                                kT_t[:, key_slot("kd", h, c), 0:(i + 1) * P], start=True, stop=True)
                elif kind == "dil":
                    n = AT["kw", h, 0]
                    pe.wait_ge(s_zfree[n % 2], n // 2 + 1)
                    last = nc.tensor.matmul(s_ps[:, 0, 0:(i + 1) * P], cat_t[:, 2 * H + h, i * P:(i + 1) * P],
                                            kT_t[:, key_slot("kw", h, 0), 0:(i + 1) * P], start=True, stop=True)
                else:
                    n = AT["qm", h, 0]
                    pe.wait_ge(s_zfree[n % 2], n // 2 + 1)
                    for c in range(2):
                        b = 2 * i + c
                        last = nc.tensor.matmul(s_ps[:, c, 0:N_MEM], cat_t[:, 3 * H + h, b * P:(b + 1) * P],
                                                mk_T[:, h, :], start=True, stop=True)
                last.then_inc(s_sfull, 1)

            def step_turn(t, use):
                kind, h, i, _ = STEPS[t]
                pe.wait_ge(s_probs, t + 1)
                turn_ready(use)
                if kind == "mem":
                    for kb in range(2):
                        for c in range(2):
                            k = 2 * kb + c
                            last = nc.tensor.transpose(t_ps[:, k * P:(k + 1) * P], probs[:, c, kb * P:(kb + 1) * P], ident[:, :])
                else:
                    for kb in range(i + 1):
                        last = nc.tensor.transpose(t_ps[:, kb * P:(kb + 1) * P], probs[:, 0, kb * P:(kb + 1) * P], ident[:, :])
                last.then_inc(s_tfull, 1)

            def step_values(t, use):
                kind, h, i, _ = STEPS[t]
                pe.wait_ge(s_tfree, USE["B", t]["tb"] + 1)
                out_ready(use)
                if kind == "diff":
                    pe.wait_ge(s_tfree, USE["nat", AT["vd", h, 1]]["tb"] + 1)
                    for kb in range(i + 1):
                        last = nc.tensor.matmul(o_ps[:, 0:2 * P], probs_T[:, kb * P:(kb + 1) * P],
                                                v_nat[:, h % 2, kb, :], start=(kb == 0), stop=(kb == i))
                elif kind == "dil":
                    pe.wait_ge(s_tfree, USE["nat", AT["vw", h, 0]]["tb"] + 1)
                    for kb in range(i + 1):
                        last = nc.tensor.matmul(o_ps[:, 0:P], v_nat[:, h % 2, kb, 0:P],
                                                probs_T[:, kb * P:(kb + 1) * P], start=(kb == 0), stop=(kb == i))
                else:
                    for kb in range(2):
                        last = nc.tensor.matmul(o_ps[:, 0:2 * P], mv_nat[:, kb, h * P:(h + 1) * P],
                                                probs_T[:, kb * 2 * P:(kb + 1) * 2 * P], start=(kb == 0), stop=(kb == 1))
                last.then_inc(s_ofull, 1)

            def step_turn_out(t, use):
                pe.wait_ge(s_ofree, USE["C", t]["ob"] + 1)
                turn_ready(use)
                for c in range(2):
                    last = nc.tensor.transpose(t_ps[:, c * P:(c + 1) * P], o_nat[:, c * P:(c + 1) * P], ident[:, :])
                last.then_inc(s_tfull, 1)

            def sample_rows(src, count, use):
                turn_ready(use)
                nc.tensor.transpose(t_ps[0:count, 0:P], src, ident[:, :]).then_inc(s_tfull, 1)

            def soft(g, k, use):
                if k == 0:
                    pe.wait_ge(s_dsm, 5 * g + 1)
                    turn_ready(use)
                    nc.tensor.transpose(t_ps[0:64, 0:P], M1, ident[:, :]).then_inc(s_tfull, 1)
                if k == 1:
                    pe.wait_ge(s_dsm, 5 * g + 2)
                    pe.wait_ge(s_dprod, g + 1)
                    out_ready(use)
                    nc.tensor.matmul(o_ps[:, 0:64], ones[0:64, :], DIAG[0:64, :], start=True, stop=True)
                    nc.tensor.matmul(o_ps[:, 64:128], ones[:, :], PROD, start=True, stop=True).then_inc(s_ofull, 1)
                if k == 2:
                    pe.wait_ge(s_dsm, 5 * g + 5)
                    out_ready(use)
                    nc.tensor.matmul(o_ps[:, 0:64], ones[:, :], L1, start=True, stop=True).then_inc(s_ofull, 1)

            def sum_values(i, use):
                last_unit = 8 * i + 7 if i < 16 else 128 + 2 * (i - 16) + 1
                pe.wait_ge(s_unit, UNIT_AT[True, last_unit] + 1)
                out_ready(use)
                for k in range(4):
                    last = nc.tensor.matmul(o_ps[:, k:k + 1], v_acc[:, i % 2, k * P:(k + 1) * P], ones[:, 0:1],
                                            start=True, stop=True)
                last.then_inc(s_ofull, 1)

            pe.wait_ge(s_const, 16 * 10)
            pe.wait_ge(s_init, 1)
            pe.wait_ge(s_lam, 1)
            nc.tensor.matmul(z[1][:, 0, 0:2], ones[:, :], lam_w[:, 0:2], start=True, stop=True).then_inc(s_lamp, 1)
            for u in range(N_PREP):
                prep(0, u)
            for s, jobs in enumerate(PLAN):
                if s < QUARTERS:
                    if s == 4:
                        pe.wait_ge(s_lame, 1)
                    quarter(s)
                for kind, what, use in jobs:
                    if kind == "prep":
                        prep(*what)
                    elif kind == "prep_sample":
                        prep_sample()
                    elif kind in ("nat", "ynat"):
                        natural(what, use)
                    elif kind == "A":
                        step_scores(what, use)
                    elif kind == "B":
                        step_turn(what, use)
                    elif kind == "C":
                        step_values(what, use)
                    elif kind == "D":
                        step_turn_out(what, use)
                    elif kind == "qrows":
                        pe.wait_ge(s_keep, 8 if what == 0 else KEPT["qm", 3, 0])
                        sample_rows(q_s[:, 8 * what:8 * what + 8, :].rearrange("p t b -> p (t b)"), 64, use)
                    elif kind == "kvrows":
                        pe.wait_ge(s_keep, KEPT["vw", 3, 0])
                        sample_rows((v_s if what else k_s)[:, :, :].rearrange("p t b -> p (t b)"), 96, use)
                    elif kind == "soft":
                        soft(*what, use)
                    elif kind == "do":
                        sum_values(what, use)
                    elif kind == "fin" and what == 1:
                        pe.wait_ge(s_fin, 1)
                        out_ready(use)
                        nc.tensor.matmul(o_ps[:, 0:64], ones[:, :], SQ, start=True, stop=True).then_inc(s_ofull, 1)

        @block.scalar
        def _(act):
            chain = [0]

            def link(ins):
                chain[0] += 1
                ins.then_inc(s_achain, 1)
                act.wait_ge(s_achain, chain[0])

            def squares(i, src, n):
                act.wait_ge(s_tok[i], 16)
                if i >= 1:
                    act.wait_ge(s_ss, ORDER_OF[i])
                nc.scalar.activation(gate[0:n, 0:D_MODEL], src, ACT.Square, accum_out=tok_ss[0:n, i:i + 1]).then_inc(s_ss, 1)

            def prep_hi(pair, u):
                use = prep_base(pair) + u
                g = gmn if pair == 0 else gn
                act.wait_ge(s_pfull, use + 1)
                if pair == 2:
                    act.wait_ge(s_quarter, 4 * FIRST_IN)
                first = N_MEM if pair == 1 else 0
                for k in range(2):
                    kt = 2 * u + k
                    last = nc.scalar.activation(act_hi[:, kt, first:first + 2 * P], s_ps[:, use % 2, k * 2 * P:(k + 1) * 2 * P],
                                                ACT.Identity, scale=g[:, kt:kt + 1])
                last.then_inc(s_phi, 1)

            def split_hi(q):
                act.wait_ge(s_raw[q % WIN_RING], 16 * (q // WIN_RING + 1))
                if q >= SPLIT_RING:
                    act.wait_ge(s_quarter, q - SPLIT_RING + 1)
                nc.scalar.activation(w_hi[:, q % SPLIT_RING, :], w_raw[:, q % WIN_RING, :], ACT.Copy).then_inc(s_hi, 1)

            def evac(n):
                kind, h, c = TILES[n]
                act.wait_ge(s_quarter, 4 * n + 4)
                free = s_zfree[n % 2]
                zz = z[n % 2][:, :, 0:HALF]
                two = lambda ap: ap.rearrange("p (a t) -> p a t", a=2)
                if kind == "mk":
                    nc.scalar.activation(mk_T[:, h, :], z[n % 2][:, 0, 0:N_MEM], ACT.Copy).then_inc(free, 1)
                elif kind == "mv":
                    if h >= 1:
                        act.wait_ge(s_tfull, USE["nat", n - 1]["tb"] + 1)
                    nc.scalar.activation(tall[:, 0:N_MEM], z[n % 2][:, 0, 0:N_MEM], ACT.Copy).then_inc(free, 1)
                elif kind[0] == "q":
                    if n == FIRST_IN:
                        act.wait_ge(s_pfull, 3 * N_PREP + 1)
                    nc.scalar.activation(two(cat_t[:, cat_slot(kind, h, c), :]), zz, ACT.Copy).then_inc(free, 1)
                elif kind[0] == "k":
                    if kind == "kd" and h >= 2:
                        act.wait_ge(s_sfull, USE["A", LAST_STEP["diff", h - 2]]["sb"] + 1)
                    if kind == "kw":
                        act.wait_ge(s_sfull, USE["A", LAST_STEP["diff", 2 + h // 2]]["sb"] + 1)
                    if kind != "kd" or h >= 2:
                        act.wait_ge(s_keep, KEPT["qm", 3, 0] if kind == "kw" else KEPT["gd", h - 1, 1])
                    nc.scalar.activation(two(kT_t[:, key_slot(kind, h, c), :]), zz, ACT.Copy).then_inc(free, 1)
                elif kind[0] == "v":
                    prev = NAT_V[NAT_V.index(n) - 1]
                    act.wait_ge(s_tfull, USE["nat", prev]["tb"] + 1)
                    if TILES[prev][0] != "mv":
                        act.wait_ge(s_keep, KEPT[TILES[prev]])
                    nc.scalar.activation(two(tall[:, :]), zz, ACT.Copy).then_inc(free, 1)
                elif kind[0] == "g":
                    if kind == "gd" and h >= 2:
                        act.wait_ge(s_tfree, USE["D", LAST_STEP["diff", h - 2]]["tb"] + 1)
                    if kind == "gw":
                        if h < 2:
                            act.wait_ge(s_tfree, USE["D", LAST_STEP["diff", 2 + h]]["tb"] + 1)
                        else:
                            act.wait_ge(s_ofree, USE["C", LAST_STEP["dil", h - 2]]["ob"] + 1)
                    if kind == "gm" and h >= 2:
                        act.wait_ge(s_gated, h - 1)
                    if kind in ("gd", "gw"):
                        act.wait_ge(s_keep, KEPT[kind, h, c] - 1)
                    nc.scalar.activation(two(gate_t[:, gate_slot(kind, h, c), :]), zz, ACT.Tanh, scale=0.5).then_inc(s_tanh, 1)
                else:
                    prev = n - 1
                    if h >= 1:
                        act.wait_ge(s_ofull, USE["ynat", prev]["ob"] + 1)
                    else:
                        act.wait_ge(s_tfull, USE["nat", NAT_V[-1]]["tb"] + 1)
                        act.wait_ge(s_keep, KEPT["vw", 3, 0])
                    nc.scalar.activation(two(tall[:, :]), zz, ACT.Copy).then_inc(free, 1)

            def natural(n, use):
                kind, h, c = TILES[n]
                act.wait_ge(s_tfull, use["tb"] + 1)
                if kind in ("mk", "kd", "kw"):
                    i = NAT_K.index(n)
                    if i >= 1:
                        act.wait_ge(s_kout, 16 * i)
                    w = N_MEM if kind == "mk" else SEQ
                    nc.scalar.activation(k_nat[:, :, :].rearrange("p t d -> p (t d)")[:, 0:w], t_ps[:, 0:w], ACT.Copy).then_inc(s_tfree, 1)
                elif kind == "mv":
                    nc.scalar.activation(mv_nat[:, :, h * P:(h + 1) * P], t_ps[:, 0:N_MEM].rearrange("p (t d) -> p t d", t=2),
                                         ACT.Copy).then_inc(s_tfree, 1)
                else:
                    if kind == "vd" and h >= 2:
                        act.wait_ge(s_ofull, USE["C", LAST_STEP["diff", h - 2]]["ob"] + 1)
                        act.wait_ge(s_vout[h % 2], 32)
                    if kind == "vw":
                        before = ("diff", 2 + h) if h < 2 else ("dil", h - 2)
                        act.wait_ge(s_ofull, USE["C", LAST_STEP[before]]["ob"] + 1)
                        act.wait_ge(s_vout[h % 2], 64 if h < 2 else 80)
                    nc.scalar.activation(v_nat[:, h % 2, :, c * P:(c + 1) * P], t_ps[:, :].rearrange("p (t d) -> p t d", t=NBLK),
                                         ACT.Copy).then_inc(s_tfree, 1)

            def step_exp(t):
                kind, h, i, _ = STEPS[t]
                act.wait_ge(s_max, t + 1)
                for c in range(1 if kind == "dil" else 2):
                    w = N_MEM if kind == "mem" else (i + 1) * P
                    src = s_ps[:, c, 0:w] if kind == "mem" else probs[:, c, 0:w]
                    last = nc.scalar.activation(probs[:, c, 0:w], src, ACT.Exp, bias=st_n[:, t % 2, c:c + 1], scale=SCALE,
                                                accum_out=st_l[:, t % 2, c:c + 1])
                last.then_inc(s_exp, 1)

            def step_probs(t):
                kind, h, i, _ = STEPS[t]
                if kind != "diff":
                    act.wait_ge(s_rec, RECS[t] + 1)
                    w = N_MEM if kind == "mem" else (i + 1) * P
                    for c in range(1 if kind == "dil" else 2):
                        last = nc.scalar.activation(probs[:, c, 0:w], probs[:, c, 0:w], ACT.Identity,
                                                    scale=st_r[:, t % 2, c:c + 1])
                    last.then_inc(s_probs, 1)

            def step_turn(t, use):
                kind, h, i, _ = STEPS[t]
                w = SEQ if kind == "mem" else (i + 1) * P
                act.wait_ge(s_tfull, use["tb"] + 1)
                nc.scalar.activation(probs_T[:, 0:w], t_ps[:, 0:w], ACT.Copy).then_inc(s_tfree, 1)

            act.wait_ge(s_lamp, 1)
            nc.scalar.activation(lam_w[:, 2:4], z[1][:, 0, 0:2], ACT.Exp).then_inc(s_lame, 1)
            squares(0, nat[:, 0, :], P)
            squares(1, nat[:, 1, :], P)
            for u in range(N_PREP):
                prep_hi(0, u)
                if u < AHEAD:
                    split_hi(u)
            squares(2, nat[:, 2, :], P)
            squares(3, nat[:, 3, :], P)
            squares(6, x_s_nat, DB)
            for s, jobs in enumerate(PLAN):
                if s + AHEAD < QUARTERS:
                    split_hi(s + AHEAD)
                for kind, what, use in jobs:
                    if kind == "evac":
                        evac(what)
                    elif kind == "prep":
                        prep_hi(*what)
                    elif kind == "prep_sample":
                        act.wait_ge(s_phi, 2 * N_PREP + 1)
                        nc.scalar.activation(act_hi[:, :, SAMPLE], tok_s[:, :, :], ACT.Copy).then_inc(s_phi, 1)
                    elif kind == "nat":
                        natural(what, use)
                    elif kind == "A":
                        step_exp(what)
                    elif kind == "P":
                        step_probs(what)
                    elif kind == "B":
                        step_turn(what, use)
                    elif kind == "C" and STEPS[what][0] == "diff":
                        act.wait_ge(s_ofull, use["ob"] + 1)
                        if what >= 1:
                            act.wait_ge(s_tfull, USE["D", what - 1]["tb"] + 1)
                        nc.scalar.activation(o_nat[:, :], o_ps[:, 0:2 * P], ACT.Square,
                                             accum_out=st_q[:, 0, 0:1]).then_inc(s_osq, 1)
                    elif kind in ("qrows", "kvrows"):
                        act.wait_ge(s_tfull, use["tb"] + 1)
                        n = 64 if kind == "qrows" else 96
                        if kind == "kvrows":
                            act.wait_ge(s_qdram, 32)
                        nc.scalar.activation(rows[0:n, what, :], t_ps[0:n, 0:P], ACT.Copy).then_inc(s_tfree, 1)
                    elif kind == "soft" and what[1] == 1:
                        g = what[0]
                        act.wait_ge(s_dsm, 5 * g + 4)
                        w = 512 if g == 0 else 128
                        nc.scalar.activation(dec_s[:, 0:w], dec_s[:, 0:w], ACT.Exp, scale=SCALE)
                        nc.scalar.activation(SNEW, SNEW, ACT.Exp, scale=SCALE).then_inc(s_dexp, 1)
                    elif kind == "ynat":
                        e = TILES[what][1]
                        for i in range(NBLK + 1):
                            n = P if i < NBLK else DB
                            src = nat[:, i, e * P:(e + 1) * P] if i < NBLK else y_s_nat[:, e * P:(e + 1) * P]
                            if i < NBLK:
                                act.wait_ge(s_tfree, use["tb"] + 1)
                            else:
                                act.wait_ge(s_ofree, use["ob"] + 1)
                            if i or e:
                                act.wait_ge(s_ysq, 5 * e + i)
                            nc.scalar.activation(o_nat[0:n, 0:P], src, ACT.Square,
                                                 accum_out=y_ss[0:n, i, e:e + 1]).then_inc(s_ysq, 1)
                if s in (16, 17):
                    squares(s - 12, nat[:, s - 16, :], P)
                if s == IN_END:
                    for kt in range(KT):
                        if kt == 0:
                            act.wait_ge(s_tfree, USE["D", LAST_STEP["diff", 3]]["tb"] + 1)
                            act.wait_ge(s_ofree, USE["C", LAST_STEP["dil", 3]]["ob"] + 1)
                            act.wait_ge(s_fin, 3)
                        if kt >= 3 * H:
                            act.wait_ge(s_gated, kt - 3 * H + 1)
                        act.wait_ge(s_quarter, IN_END - 4 + kt // 4 + 1)
                        nc.scalar.activation(act_hi[:, kt, :], cat_t[:, kt, :], ACT.Copy).then_inc(s_chi, 1)

        @block.vector
        def _(dve):
            chain = [0]

            def link(ins):
                chain[0] += 1
                ins.then_inc(s_chain, 1)
                dve.wait_ge(s_chain, chain[0])

            def scale_tokens(i, view):
                n = DB if i == 6 else P
                dve.wait_ge(s_rr, ORDER_OF[i] + 1)
                nc.vector.tensor_scalar(view, view, tok_r[0:n, i:i + 1], None, ALU.mult).then_inc(s_scaled, 1)

            def prep_lo(pair, u):
                use = prep_base(pair) + u
                g = gmn if pair == 0 else gn
                dve.wait_ge(s_phi, use + 1 + (use > 2 * N_PREP))
                first = N_MEM if pair == 1 else 0
                for k in range(2):
                    kt = 2 * u + k
                    cols = slice(first, first + 2 * P)
                    last = nc.vector.scalar_tensor_tensor(act_lo[:, kt, cols], s_ps[:, use % 2, k * 2 * P:(k + 1) * 2 * P],
                                                          g[:, kt:kt + 1], act_hi[:, kt, cols].bitcast(F32), ALU.mult, ALU.subtract)
                last.then_inc(s_plo, 1)

            def prep_sample():
                use = 2 * N_PREP
                dve.wait_ge(s_pfull, use + 1)
                src = s_ps[:, use % 2, 0:KT * DB].rearrange("p (k b) -> p k b", b=DB)
                nc.vector.tensor_tensor(tok_s[:, :, :], src, gn[:, :].unsqueeze(2).broadcast_to((P, KT, DB)), ALU.mult).then_inc(s_phi, 1)
                dve.wait_ge(s_phi, 2 * N_PREP + 2)
                nc.vector.tensor_tensor(act_lo[:, :, SAMPLE], tok_s[:, :, :], act_hi[:, :, SAMPLE].bitcast(F32), ALU.subtract).then_inc(s_plo, 1)

            def split_lo(q):
                dve.wait_ge(s_hi, q + 1)
                nc.vector.tensor_tensor(w_lo[:, q % SPLIT_RING, :], w_raw[:, q % WIN_RING, :],
                                        w_hi[:, q % SPLIT_RING, :].bitcast(F32), ALU.subtract).then_inc(s_lo, 1)

            def evac(n):
                kind, h, c = TILES[n]
                if kind[0] != "g":
                    return
                slot = gate_t[:, gate_slot(kind, h, c), :]
                dve.wait_ge(s_tanh, TANHS[n] + 1)
                two = slot.rearrange("p (a t) -> p a t", a=2)
                nc.vector.scalar_tensor_tensor(two, two, 1.0, z[n % 2][:, :, 0:HALF], ALU.add, ALU.mult).then_inc(s_zfree[n % 2], 1)
                if kind == "gm":
                    dve.wait_ge(s_zfree[n % 2], n // 2 + 1)
                    dve.wait_ge(s_ofree, max(USE["do", 31]["ob"], USE["C", LAST_STEP["mem", 3]]["ob"]) + 1)
                    out = cat_t[:, cat_slot(kind, h, c), :]
                    nc.vector.scalar_tensor_tensor(out, out, 0.5, slot, ALU.mult, ALU.mult).then_inc(s_gated, 1)

            def step_max(t, use):
                kind, h, i, _ = STEPS[t]
                tp = t % 2
                w = N_MEM if kind == "mem" else (i + 1) * P
                nc_ = 1 if kind == "dil" else 2
                dve.wait_ge(s_sfull, use["sb"] + 1)
                if kind != "mem":
                    bi = bias_index(kind, h)
                    dve.wait_ge(s_bias[bi % 2], 16 * (bi // 2 + 1))
                for c in range(nc_):
                    if kind == "mem":
                        last = nc.vector.reduce_max(st_m[:, tp, c:c + 1], s_ps[:, c, 0:w], AX_X)
                    else:
                        last = nc.vector.tensor_tensor_reduce(probs[:, c, 0:w], s_ps[:, c, 0:w], bias[:, bi % 2, SEQ - w:SEQ],
                                                              1.0, LOWEST, ALU.add, ALU.max, st_m[:, tp, c:c + 1])
                if kind == "mem":
                    link(last)
                else:
                    last.then_inc(s_sfree, 1)
                    dve.wait_ge(s_sfree, SCORES_READ[t])
                nc.vector.tensor_scalar(st_n[:, tp, 0:nc_], st_m[:, tp, 0:nc_], -SCALE, None, ALU.mult).then_inc(s_max, 1)

            def step_probs(t, use):
                kind, h, i, _ = STEPS[t]
                tp = t % 2
                w = N_MEM if kind == "mem" else (i + 1) * P
                nc_ = 1 if kind == "dil" else 2
                dve.wait_ge(s_exp, t + 1)
                if kind == "mem":
                    nc.vector.reciprocal(st_r[:, tp, 0:2], st_l[:, tp, 0:2]).then_inc(s_rec, 1)
                elif kind == "dil":
                    nc.vector.reciprocal(st_r[:, tp, 0:1], st_l[:, tp, 0:1]).then_inc(s_rec, 1)
                else:
                    link(nc.vector.reciprocal(st_r[:, tp, 0:2], st_l[:, tp, 0:2]))
                    if t == 0:
                        dve.wait_ge(s_neglam, 1)
                    nc.vector.tensor_scalar(st_r[:, tp, 2:3], st_r[:, tp, 1:2], lam_w[:, 5:6], None, ALU.mult)
                    link(nc.vector.tensor_scalar(probs[:, 0, 0:w], probs[:, 0, 0:w], st_r[:, tp, 0:1], None, ALU.mult))
                    nc.vector.scalar_tensor_tensor(probs[:, 0, 0:w], probs[:, 1, 0:w], st_r[:, tp, 2:3], probs[:, 0, 0:w],
                                                   ALU.mult, ALU.add).then_inc(s_probs, 1)

            def step_out(t, use):
                kind, h, i, _ = STEPS[t]
                if kind == "diff":
                    dve.wait_ge(s_orstd, t + 1)
                    nc.vector.tensor_scalar(o_nat[:, :], o_ps[:, 0:2 * P], st_q[:, 1, 0:1], None, ALU.mult).then_inc(s_ofree, 1)
                elif kind == "dil":
                    n = AT["gw", h, 0]
                    dve.wait_ge(s_zfree[n % 2], n // 2 + 1)
                    dve.wait_ge(s_ofull, use["ob"] + 1)
                    cols = slice(i * P, (i + 1) * P)
                    nc.vector.scalar_tensor_tensor(cat_t[:, 2 * H + h, cols], o_ps[:, 0:P], 0.5, gate_t[:, gate_slot("gw", h, 0), cols],
                                                   ALU.mult, ALU.mult).then_inc(s_ofree, 1)
                else:
                    dve.wait_ge(s_ofull, use["ob"] + 1)
                    nc.vector.tensor_copy(cat_t[:, 3 * H + h, 2 * i * P:2 * (i + 1) * P], o_ps[:, 0:2 * P]).then_inc(s_ofree, 1)

            def step_gate(t, use):
                kind, h, i, _ = STEPS[t]
                n = AT["gd", h, 1]
                dve.wait_ge(s_zfree[n % 2], n // 2 + 1)
                dve.wait_ge(s_zfree[(n - 1) % 2], (n - 1) // 2 + 1)
                dve.wait_ge(s_tfull, use["tb"] + 1)
                cols = slice(i * P, (i + 1) * P)
                for c in range(2):
                    last = nc.vector.scalar_tensor_tensor(cat_t[:, 2 * h + c, cols], t_ps[:, c * P:(c + 1) * P], gsub_c[:, c:c + 1],
                                                          gate_t[:, gate_slot("gd", h, c), cols], ALU.mult, ALU.mult)
                last.then_inc(s_tfree, 1)

            done = [0]

            def key_unit(u):
                g, c, b, t = unit(u)
                i = u // 8 if u < 128 else 16 + (u - 128) // 2
                slot = done[0] % PAGE_RING
                dve.wait_ge(s_qbc[i % 2], 16 * (i // 2 + 1))
                dve.wait_ge(s_page[slot], LANDED[done[0]])
                for k in range(4):
                    if g == 0:
                        h, part = 2 * c + k // 2, k % 2
                    else:
                        h, part = k, c
                    col = t * 64 + part * 32 + b * H + h
                    seg = pages[:, slot, k * P:(k + 1) * P]
                    last = nc.vector.tensor_tensor_reduce(seg, seg, q_bc[:, i % 2, k * P:(k + 1) * P], 1.0, 0.0,
                                                          ALU.mult, ALU.add, dec_s[:, col:col + 1])
                last.then_inc(s_unit, 1)
                done[0] += 1

            def value_unit(u):
                g, c, b, t = unit(u)
                i = u // 8 if u < 128 else 16 + (u - 128) // 2
                slot = done[0] % PAGE_RING
                acc = v_acc[:, i % 2, :]
                if t == 0 and i >= 2:
                    dve.wait_ge(s_ofree, USE["do", i - 2]["ob"] + 1)
                dve.wait_ge(s_page[slot], LANDED[done[0]])
                if t:
                    dve.wait_ge(s_unit, done[0])
                for k in range(2 if g == 0 else 4):
                    w = 256 if g == 0 else 128
                    seg = slice(k * w, (k + 1) * w)
                    if g == 0:
                        a = dec_a[:, t, b * H + 2 * c + k:b * H + 2 * c + k + 1]
                    else:
                        col = t * 64 + c * 32 + b * H + k
                        a = dec_s[:, col:col + 1]
                    if t == 0:
                        last = nc.vector.tensor_scalar(acc[:, seg], pages[:, slot, seg], a, None, ALU.mult)
                    else:
                        last = nc.vector.scalar_tensor_tensor(acc[:, seg], pages[:, slot, seg], a, acc[:, seg], ALU.mult, ALU.add)
                last.then_inc(s_unit, 1)
                done[0] += 1

            def values_out(i, use):
                first, b = (4 * (i // 8), i % 8) if i < 16 else (8 + 4 * ((i - 16) // 8), (i - 16) % 8)
                dve.wait_ge(s_ofull, use["ob"] + 1)
                dst = o_s[:, first:first + 4, b] if i < 24 else cat_t[:, 3 * H:4 * H, SEQ + b]
                nc.vector.tensor_copy(dst, o_ps[:, 0:4]).then_inc(s_ofree, 1)

            def soft(g, k, use):
                T = PAGES if g == 0 else 2
                s3 = dec_s[:, 0:T * 64].rearrange("p (t n) -> p t n", t=T)
                over = lambda ap: ap.unsqueeze(1).broadcast_to((P, T, 64))
                if k == 0:
                    dve.wait_ge(s_unit, 128 if g == 0 else 288)
                    if g == 0:
                        v = dec_s[:, :].rearrange("p (t b h) -> p t b h", t=T, h=H)
                        link(nc.vector.tensor_tensor(v, v, bd.unsqueeze(2).broadcast_to((P, T, 16, H)), ALU.add))
                    else:
                        v = dec_s[:, 0:128].rearrange("p (t b h) -> p t b h", t=4, h=H)
                        link(nc.vector.tensor_tensor(v, v, bw.unsqueeze(2).broadcast_to((P, 4, DB, H)), ALU.add))
                    nc.vector.tensor_reduce(M1, s3.rearrange("p t n -> p n t"), AX_X, ALU.max).then_inc(s_dsm, 1)
                    dve.wait_ge(s_keep, KEPT["kd", 3, 1] if g == 0 else KEPT["kw", 3, 0])
                    if g == 0:
                        for c in range(2):
                            prod = PROD[:, c * 32:(c + 1) * 32].rearrange("p (b h) -> p h b", h=H)
                            qv = q_s[:, 0:8, :].rearrange("p (h c) b -> p c h b", c=2)[:, c]
                            kv = k_s[:, 0:8, :].rearrange("p (h c) b -> p c h b", c=2)[:, c]
                            last = nc.vector.tensor_tensor(prod, qv, kv, ALU.mult)
                        last.then_inc(s_dprod, 1)
                    else:
                        nc.vector.memset(PROD[:, 32:64], 0.0)
                        prod = PROD[:, 0:32].rearrange("p (b h) -> p h b", h=H)
                        nc.vector.tensor_tensor(prod, q_s[:, 8:12, :], k_s[:, 8:12, :], ALU.mult).then_inc(s_dprod, 1)
                    dve.wait_ge(s_tfull, use["tb"] + 1)
                    nc.vector.reduce_max(MB[0:64, 0:1], t_ps[0:64, 0:P], AX_X).then_inc(s_tfree, 1)
                    dve.wait_ge(s_tfree, use["tb"] + 1)
                    nc.vector.tensor_scalar(DIAG[0:64, :], ident[0:64, 0:64], MB[0:64, 0:1], None, ALU.mult).then_inc(s_dsm, 1)
                if k == 1:
                    dve.wait_ge(s_ofull, use["ob"] + 1)
                    link(nc.vector.tensor_tensor(SNEW, o_ps[:, 64:128], bn[:, g, :], ALU.add))
                    nc.vector.tensor_tensor(MB, o_ps[:, 0:64], SNEW, ALU.max).then_inc(s_ofree, 1)
                    dve.wait_ge(s_ofree, use["ob"] + 1)
                    nc.vector.tensor_tensor(s3, s3, over(MB), ALU.subtract).then_inc(s_dsm, 1)
                    nc.vector.tensor_tensor(SNEW, SNEW, MB, ALU.subtract).then_inc(s_dsm, 1)
                    dve.wait_ge(s_dexp, g + 1)
                    nc.vector.tensor_reduce(L1, s3.rearrange("p t n -> p n t"), AX_X, ALU.add).then_inc(s_dsm, 1)
                if k == 2:
                    dve.wait_ge(s_ofull, use["ob"] + 1)
                    nc.vector.tensor_tensor(LR, o_ps[:, 0:64], SNEW, ALU.add).then_inc(s_ofree, 1)
                    dve.wait_ge(s_ofree, use["ob"] + 1)
                    link(nc.vector.reciprocal(LR, LR))
                    nc.vector.tensor_tensor(SNEW, SNEW, LR, ALU.mult)
                    link(nc.vector.tensor_tensor(s3, s3, over(LR), ALU.mult))
                if k == 3:
                    if g == 0:
                        nc.vector.scalar_tensor_tensor(dec_a[:, :, :], s3[:, :, 32:64], lam_w[:, 5:6], s3[:, :, 0:32], ALU.mult, ALU.add)
                        link(nc.vector.scalar_tensor_tensor(SNEW[:, 0:32], SNEW[:, 32:64], lam_w[:, 5:6], SNEW[:, 0:32], ALU.mult, ALU.add))
                        link(nc.vector.tensor_copy(a_new[:, 0, :], SNEW[:, 0:32]))
                    else:
                        link(nc.vector.tensor_copy(a_new[:, 1, :], SNEW[:, 0:32]))

            def finish(k, use):
                if k == 0:
                    dve.wait_ge(s_ofree, USE["do", 31]["ob"] + 1)
                    dve.wait_ge(s_keep, KEPT["vw", 3, 0])
                    od, vd = o_s[:, 0:8, :], v_s[:, 0:8, :]
                    an = a_new[:, 0, :].rearrange("p (b h) -> p h b", h=H)
                    for c in range(2):
                        link(nc.vector.tensor_tensor(tmp[:, 0:4, :], vd.rearrange("p (h c) b -> p c h b", c=2)[:, c], an, ALU.mult))
                        o1 = od.rearrange("p (h c) b -> p c h b", c=2)[:, c]
                        link(nc.vector.tensor_tensor(o1, o1, tmp[:, 0:4, :], ALU.add))
                    aw = a_new[:, 1, :].rearrange("p (b h) -> p h b", h=H)
                    link(nc.vector.tensor_tensor(tmp[:, 0:4, :], v_s[:, 8:12, :], aw, ALU.mult))
                    link(nc.vector.tensor_tensor(o_s[:, 8:12, :], o_s[:, 8:12, :], tmp[:, 0:4, :], ALU.add))
                    nc.vector.tensor_tensor(SQ.rearrange("p (t b) -> p t b", b=DB), od, od, ALU.mult).then_inc(s_fin, 1)
                if k == 1:
                    dve.wait_ge(s_ofull, use["ob"] + 1)
                    link(nc.vector.tensor_copy(L1, o_ps[:, 0:64]))
                    l3 = L1.rearrange("p (h c b) -> p h c b", c=2, b=DB)
                    nc.vector.tensor_tensor(M1[:, 0:32].rearrange("p (h b) -> p h b", b=DB), l3[:, :, 0, :], l3[:, :, 1, :],
                                            ALU.add).then_inc(s_ofree, 1)
                if k == 2:
                    dve.wait_ge(s_finp, 1)
                    r3 = M1[:, 32:64].rearrange("p (h b) -> p h b", b=DB)
                    for c in range(2):
                        o1 = o_s[:, 0:8, :].rearrange("p (h c) b -> p c h b", c=2)[:, c]
                        link(nc.vector.tensor_tensor(o1, o1, r3, ALU.mult))
                        link(nc.vector.tensor_scalar(o1, o1, gsub_c[:, c:c + 1], None, ALU.mult))
                    dve.wait_ge(s_keep, KEPT["gw", 3, 0])
                    nc.vector.tensor_tensor(cat_t[:, 0:8, SAMPLE], o_s[:, 0:8, :], g_s[:, 0:8, :], ALU.mult).then_inc(s_fin, 1)
                    nc.vector.scalar_tensor_tensor(cat_t[:, 8:12, SAMPLE], o_s[:, 8:12, :], 0.5, g_s[:, 8:12, :],
                                                   ALU.mult, ALU.mult).then_inc(s_fin, 1)

            nc.vector.memset(ones[:, :], 1.0).then_inc(s_init, 1)
            nc.vector.memset(power[:, :], -0.5).then_inc(s_init, 1)
            dve.wait_ge(s_const, 16 * 10)
            nc.vector.tensor_scalar(gsub_c[:, :], gsub[:, :], 0.5 * (1.0 - LAM_INIT), None, ALU.mult)
            nc.vector.tensor_tensor(lam_w[:, 0:1], lam_in[:, 0:1], lam_in[:, 1:2], ALU.mult)
            nc.vector.tensor_tensor(lam_w[:, 1:2], lam_in[:, 2:3], lam_in[:, 3:4], ALU.mult).then_inc(s_lam, 1)
            dve.wait_ge(s_lame, 1)
            link(nc.vector.tensor_tensor(lam_w[:, 4:5], lam_w[:, 3:4], lam_w[:, 2:3], ALU.subtract))
            nc.vector.tensor_scalar(lam_w[:, 5:6], lam_w[:, 4:5], -LAM_INIT, None, ALU.add).then_inc(s_neglam, 1)
            scale_tokens(0, nat[:, 0, :])
            scale_tokens(1, nat[:, 1, :])
            for u in range(N_PREP):
                prep_lo(0, u)
                if u < AHEAD:
                    split_lo(u)
            scale_tokens(2, nat[:, 2, :])
            scale_tokens(3, nat[:, 3, :])
            scale_tokens(6, x_s_nat)
            for s, jobs in enumerate(PLAN):
                if s + AHEAD < QUARTERS:
                    split_lo(s + AHEAD)
                for kind, what, use in jobs:
                    if kind == "evac":
                        evac(what)
                    elif kind == "prep":
                        prep_lo(*what)
                    elif kind == "prep_sample":
                        prep_sample()
                    elif kind == "A":
                        step_max(what, use)
                    elif kind == "P":
                        step_probs(what, use)
                    elif kind == "C":
                        step_out(what, use)
                    elif kind == "D":
                        step_gate(what, use)
                    elif kind == "dk":
                        key_unit(what)
                    elif kind == "dv":
                        value_unit(what)
                    elif kind == "do":
                        values_out(what, use)
                    elif kind == "soft":
                        soft(*what, use)
                    elif kind == "fin":
                        finish(what, use)
                    elif kind == "ynat":
                        e = TILES[what][1]
                        cols = slice(e * P, (e + 1) * P)
                        if e == 0:
                            for i in range(5):
                                dve.wait_ge(s_res[i], 16)
                        dve.wait_ge(s_tfull, use["tb"] + 1)
                        nc.vector.tensor_tensor(nat[:, :, cols], nat[:, :, cols], t_ps[:, :].rearrange("p (t f) -> p t f", t=NBLK),
                                                ALU.add).then_inc(s_tfree, 1)
                        dve.wait_ge(s_ofull, use["ob"] + 1)
                        nc.vector.tensor_tensor(y_s_nat[:, cols], y_s_nat[:, cols], o_ps[0:DB, 0:P], ALU.add).then_inc(s_ofree, 1)
                if s in (17, 18):
                    scale_tokens(s - 13, nat[:, s - 17, :])
                if s == IN_END:
                    for kt in range(KT):
                        dve.wait_ge(s_chi, kt + 1)
                        nc.vector.tensor_tensor(act_lo[:, kt, :], cat_t[:, kt, :], act_hi[:, kt, :].bitcast(F32),
                                                ALU.subtract).then_inc(s_clo, 1)
            dve.wait_ge(s_ysq, 5 * KT)
            link(nc.vector.tensor_reduce(y_r[:, 0:NBLK], y_ss[:, 0:NBLK, :], AX_X, ALU.add))
            nc.vector.tensor_reduce(y_r[0:DB, 4:5], y_ss[0:DB, 4, :], AX_X, ALU.add).then_inc(s_yr, 1)
            dve.wait_ge(s_yrp, 2)
            dve.wait_ge(s_gf, 16)
            for i in range(NBLK):
                nc.vector.scalar_tensor_tensor(nat[:, i, :], nat[:, i, :], y_r[:, i:i + 1], g_fin, ALU.mult, ALU.mult).then_inc(s_ydone[i], 1)
            nc.vector.scalar_tensor_tensor(y_s_nat, y_s_nat, y_r[0:DB, 4:5], g_fin[0:DB, :], ALU.mult, ALU.mult).then_inc(s_ydone[4], 1)

        @block.gpsimd
        def _(pool):
            chain = [0]

            def link(ins):
                chain[0] += 1
                ins.then_inc(s_pchain, 1)
                pool.wait_ge(s_pchain, chain[0])

            def token_rstd(i):
                n = DB if i == 6 else P
                pool.wait_ge(s_ss, ORDER_OF[i] + 1)
                link(nc.gpsimd.tensor_scalar(tok_r[0:n, i:i + 1], tok_ss[0:n, i:i + 1], 1.0 / D_MODEL, EPS, ALU.mult, ALU.add))
                nc.gpsimd.tensor_tensor(tok_r[0:n, i:i + 1], tok_r[0:n, i:i + 1], power[0:n, 0:1], ALU.pow).then_inc(s_rr, 1)

            def keep(n):
                kind, h, c = TILES[n]
                pool.wait_ge(s_zfree[n % 2], n // 2 + 1)
                if kind[0] == "q":
                    t = cat_slot(kind, h, c)
                    dst, src = q_s[:, t, :], cat_t[:, t, SAMPLE]
                elif kind[0] == "k":
                    dst, src = k_s[:, sample_slot(kind, h, c), :], kT_t[:, key_slot(kind, h, c), SAMPLE]
                elif kind[0] == "v":
                    dst, src = v_s[:, sample_slot(kind, h, c), :], tall[:, SAMPLE]
                else:
                    dst, src = g_s[:, sample_slot(kind, h, c), :], gate_t[:, gate_slot(kind, h, c), SAMPLE]
                nc.gpsimd.tensor_copy(dst, src).then_inc(s_keep, 1)

            pool.wait_ge(s_init, 2)
            token_rstd(0)
            token_rstd(1)
            token_rstd(2)
            token_rstd(3)
            token_rstd(6)
            for s, jobs in enumerate(PLAN):
                for kind, what, use in jobs:
                    if kind == "evac" and TILES[what] in KEPT:
                        keep(what)
                    elif kind == "C" and STEPS[what][0] == "diff":
                        t = what
                        pool.wait_ge(s_osq, t + 1)
                        link(nc.gpsimd.tensor_scalar(st_q[:, 1, 1:2], st_q[:, 0, 0:1], 1.0 / (2 * P), EPS, ALU.mult, ALU.add))
                        if t >= 1:
                            pool.wait_ge(s_ofree, USE["C", t - 1]["ob"] + 1)
                        nc.gpsimd.tensor_tensor(st_q[:, 1, 0:1], st_q[:, 1, 1:2], power[:, 0:1], ALU.pow).then_inc(s_orstd, 1)
                    elif kind == "fin" and what == 1:
                        pool.wait_ge(s_ofree, use["ob"] + 1)
                        link(nc.gpsimd.tensor_scalar(M1[:, 0:32], M1[:, 0:32], 1.0 / (2 * P), EPS, ALU.mult, ALU.add))
                        nc.gpsimd.tensor_tensor(M1[:, 32:64], M1[:, 0:32], power[:, 0:32], ALU.pow).then_inc(s_finp, 1)
                if s in (16, 17):
                    token_rstd(s - 12)
            pool.wait_ge(s_yr, 1)
            link(nc.gpsimd.tensor_scalar(y_sum[:, 0:4], y_r[:, 0:4], 1.0 / D_MODEL, EPS, ALU.mult, ALU.add))
            link(nc.gpsimd.tensor_scalar(y_sum[0:DB, 4:5], y_r[0:DB, 4:5], 1.0 / D_MODEL, EPS, ALU.mult, ALU.add))
            nc.gpsimd.tensor_tensor(y_r[:, 0:4], y_sum[:, 0:4], power[:, 0:4], ALU.pow).then_inc(s_yrp, 1)
            nc.gpsimd.tensor_tensor(y_r[0:DB, 4:5], y_sum[0:DB, 4:5], power[0:DB, 4:5], ALU.pow).then_inc(s_yrp, 1)


_INS = ["x_prompt", "x_sample", "mem_prompt", "cache_k_diff", "cache_v_diff", "page_table", "cache_k_win", "cache_v_win",
        "cache_mem_k", "cache_mem_v", "g_norm", "w_in", "lambda_q1", "lambda_k1", "lambda_q2", "lambda_k2", "g_subln",
        "g_mem_norm", "w_mem_kv", "w_out", "g_final"]
_OUTS = [(1, SEQ, D_MODEL), (DB, 1, D_MODEL), (1, 1, SEQ, H, 2, P), (1, 1, SEQ, H, 2 * P), (1, 1, SEQ, H, P), (1, 1, SEQ, H, P),
         (1, 1, N_MEM, H, P), (1, 1, N_MEM, H, P), (1, DB, 1, H, 2, P), (1, DB, 1, H, 2 * P), (1, DB, 1, H, P), (1, DB, 1, H, P)]


def kernel(**inputs):
    import concourse.bacc as bacc
    from concourse.bass_utils import run_bass_kernel_spmd

    nc = bacc.Bacc("TRN2", target_bir_lowering=False, num_devices=1, dynamic_dma_scratch_size=1024)
    arrays, args = {}, []
    given = {name: np.ascontiguousarray(inputs[name]) for name in _INS}
    given["bias_tables"], given["bias_small"], given["identity"] = constants()
    for name, a in given.items():
        arrays[f"in_{name}_dram"] = a
        args.append(nc.dram_tensor(f"in_{name}_dram", a.shape, mybir.dt.from_np(a.dtype), kind="ExternalInput").ap())
    for i, shape in enumerate(_OUTS):
        args.append(nc.dram_tensor(f"out_{i}_dram", shape, F32, kind="ExternalOutput").ap())
    args.append(nc.dram_tensor("q_rows_dram", (KT * DB, P), F32, kind="Internal").ap())
    hybrid_decoder(nc, *args)
    r = run_bass_kernel_spmd(nc, [arrays], core_ids=[0])
    return tuple(r.results[0][f"out_{i}_dram"] for i in range(len(_OUTS)))
```

```python
import math
from contextlib import ExitStack

import numpy as np

import concourse.bass as bass
from concourse import mybir

F32 = mybir.dt.float32
F32R = mybir.dt.float32r
I32 = mybir.dt.int32
ALU = mybir.AluOpType
ACT = mybir.ActivationFunctionType
AX_X = mybir.AxisListType.X

P = 128
D_MODEL = 2048
KT = D_MODEL // P
SEQ = 512
NBLK = SEQ // P
DB = 8
TOK = SEQ + DB
HALF = TOK // 2
N_MEM = 256
H = 4
PAGES = 8
PAST = PAGES * P
SCALE = P ** -0.5
EPS = 1e-6
LAM_INIT = 0.8 - 0.6 * math.exp(-0.3 * 0)
MASKED = -1e30
LOWEST = -3e38

WIN_RING = 6
SPLIT_RING = 4
AHEAD = 3
FIRST_SPLITS = (0, 1, 2, 4, 6)
SLOT_US = 3.6
PAGE_RING = 6

COL = dict(qd=0, kd=1024, vd=2048, gd=3072, qw=4096, kw=4608, vw=5120, gw=5632, qm=6144, gm=6656)


def slopes():
    s = 2.0 ** (-8.0 * np.arange(1, 2 * H + 1) / (2 * H))
    return s[0::2], s[1::2]


def branch_count(dist):
    n = np.zeros(dist.shape)
    for window, r in ((128, 1), (512, 4), (2048, 16)):
        n += (dist >= 0) & (dist <= window) & (dist % r == 0)
    return n


def log_count(n):
    return np.where(n > 0, np.log(np.maximum(n, 1)), MASKED)


def constants():
    sd, sw = slopes()
    dist = 3 * P + np.arange(P)[:, None] - np.arange(SEQ)[None, :]
    out = np.zeros((2 * H, P, SEQ))
    for h in range(H):
        out[h] = np.where(dist >= 0, -sd[h] * dist, MASKED)
        out[H + h] = np.where(branch_count(dist) > 0, -sw[h] * dist + log_count(branch_count(dist)), MASKED)
    key = np.arange(P)
    bd = -(PAST - (np.arange(PAGES)[None, :, None] * P + key[:, None, None])) * sd[None, None, :]
    far = np.concatenate([PAST - np.arange(512, 896, 4), PAST - np.arange(0, 512, 16)])
    bw = np.zeros((P, 2, 2, H))
    for t, d in enumerate((PAST - (896 + key), far)):
        bw[:, t, 0] = -d[:, None] * sw[None, :] + log_count(branch_count(d))[:, None]
    bn = np.zeros((2, 2, DB, H))
    bn[1, 0] = math.log(3.0)
    bn[1, 1] = MASKED
    small = np.concatenate([bd.reshape(P, -1), bw.reshape(P, -1), np.broadcast_to(bn.reshape(1, -1), (P, 128))], axis=1)
    return ((out / SCALE).astype(np.float32), (small / SCALE).astype(np.float32), np.eye(P, dtype=np.float32))


def tiles():
    out = [("mk", j, 0) for j in range(H)] + [("mv", j, 0) for j in range(H)]
    out += [("qd", h, c) for h in range(H) for c in range(2)]
    for h in range(H):
        out += [(kind, h, c) for kind in ("kd", "vd", "gd") for c in range(2)]
    out += [("qw", j, 0) for j in range(H)] + [("qm", j, 0) for j in range(H)] + [("kw", j, 0) for j in range(H)]
    out += [(kind, j, 0) for j in range(H) for kind in ("vw", "gw")]
    out += [("gm", j, 0) for j in range(H)]
    out += [("y", e, 0) for e in range(KT)]
    return out


TILES = tiles()
AT = {t: n for n, t in enumerate(TILES)}
N_TILES = len(TILES)
QUARTERS = 4 * N_TILES
FIRST_IN = AT["qd", 0, 0]
FIRST_OUT = AT["y", 0, 0]
IN_END = 4 * FIRST_OUT
KEEP = KT
N_PREP = KT // 2


SQUARES = ((2, 3), (3, 5), (6, 7), (4, 16), (5, 20))


def cat_slot(kind, h, c):
    return {"qd": 2 * h + c, "qw": 2 * H + h, "qm": 3 * H + h, "gm": 3 * H + h}[kind]


def att_steps():
    out = []
    for h in range(H):
        s0 = 4 * (AT["gd", h, 1] + 1) + 2
        period = 6 if h < H - 1 else 4
        out += [("diff", h, i, s0 + period * i) for i in range(NBLK)]
    s = out[-1][3] + 5
    for j in range(H):
        s = max(s, 4 * (AT["qm", j, 0] + 1) + 1)
        for pair in range(2):
            out.append(("mem", j, pair, s))
            s += 2
    s += 1
    for j in range(H):
        s = max(s, 4 * (AT["gw", j, 0] + 1) + 2)
        for i in range(NBLK):
            out.append(("dil", j, i, s))
            s += 2
    return out


STEPS = att_steps()


def unit(u, value):
    tiles = PAGES if u < 128 else 2
    g, u = (0, u) if u < 128 else (1, u - 128)
    b, rest = divmod(u, 2 * tiles)
    return (g, rest % 2, b, rest // 2) if value else (g, rest // tiles, b, rest % tiles)


def sequence(u):
    return u // 16 if u < 128 else DB + (u - 128) // 4


def last_of(b8):
    return 16 * b8 + 15 if b8 < DB else 128 + 4 * (b8 - DB) + 3


def q_row(u):
    return u // 8 if u < 128 else 16 + (u - 128) // 2


def last_of_row(i):
    return 8 * i + 7 if i < 16 else 128 + 2 * (i - 16) + 1


def plan():
    n_slots = QUARTERS + 8
    slots = [[] for _ in range(n_slots)]
    load = [0.65] * n_slots

    def put(s, kind, what=None, cost=0.0):
        slots[s].append((kind, what))
        load[s] += cost

    for i, s in SQUARES:
        put(s, "squares", i)
        put(s + 1, "scale", i)
    for u in range(N_PREP):
        put(9 + 2 * u, "prep", (1, u), 0.7)
    put(25, "prep_sample", None, 0.7)
    for u in range(N_PREP):
        put(29 + u // 2, "prep", (2, u), 0.7)
    for n, (kind, h, c) in enumerate(TILES):
        s = 4 * n + 4
        put(s, "evac", n, 0.65 if kind in ("gd", "gw") else 1.3 if kind == "gm" else 0.0)
        if kind in ("mk", "mv", "kd", "kw", "vd", "vw"):
            put(s + 1, "nat", n)
        if kind == "y":
            put(s + 1, "ynat", n, 0.8)
    put(4 * (AT["qd", 3, 1] + 1) + 1, "qrows", 0)
    put(4 * (AT["qm", 3, 0] + 1) + 1, "qrows", 1)
    put(4 * (AT["vw", 3, 0] + 1) + 3, "kvrows", 0)
    put(4 * (AT["vw", 3, 0] + 1) + 4, "kvrows", 1)
    for t, (kind, h, i, s) in enumerate(STEPS):
        w = (i + 1) * P
        put(s, "A", t, {"diff": 3.5 * w * 1.04e-3 + 0.4, "mem": 1.0, "dil": w * 1.04e-3 + 0.3}[kind])
        put(s + 1, "P", t, 0.0)
        put(s + 2, "B", t)
        put(s + 3, "C", t, {"diff": 0.35, "mem": 0.35, "dil": 0.2}[kind])
        if kind == "diff":
            put(s + 4, "D", t, 0.45)
    summed = {}

    def spread(units, first, end):
        room = [max(0.4, SLOT_US - load[s]) for s in range(first, end)]
        s, passed = first, 0.0
        for i, (value, u) in enumerate(units):
            while s < end - 1 and passed + room[s - first] < i * sum(room) / len(units):
                passed += room[s - first]
                s += 1
            b8 = sequence(u)
            if value:
                s = max(s, summed.get(b8 - 2, 0))
            assert s < end, (value, u, s, end)
            slots[s].append(("dv" if value else "dk", u))
            if value and u == last_of(b8):
                summed[b8] = s + (2 if u < 128 else 1)
                slots[summed[b8]].append(("do", b8))

    K0 = 4 * (AT["qd", 3, 1] + 1) + 4
    S0 = 4 * (AT["kd", 3, 1] + 1) + 3
    W0 = 4 * (AT["qm", 3, 0] + 1) + 5
    S1 = 4 * (AT["kw", 3, 0] + 1) + 3
    END = 4 * AT["gm", 0, 0] + 2
    SPACE = 2
    spread([(False, u) for u in range(128)], K0, S0)
    for g, s in ((0, S0), (1, S1)):
        for k in range(4):
            put(s + SPACE * k, "soft", (g, k), 0.8)
    V0, V1 = S0 + 3 * SPACE + 1, S1 + 3 * SPACE + 1
    rate = (128 + 64) / (END - V0)
    early = 16 * int(rate * (W0 - V0) / 16)
    late = 16 * int((END - V1 - 32 / rate) * rate / 16)
    late = max(0, min(128 - early, late))
    spread([(True, u) for u in range(early)], V0, W0)
    spread([(False, u) for u in range(128, 160)] + [(True, u) for u in range(early, 128 - late)], W0, V1)
    spread([(True, u) for u in range(128 - late, 160)], V1, END)
    fin0 = max(summed[15], 4 * (AT["gw", 3, 0] + 1) + 1)
    for k in range(3):
        put(fin0 + 2 * k, "fin", k, 0.8)
    assert summed[15] < 4 * AT["gm", 0, 0] + 4 and fin0 + 4 < IN_END - 4
    rank = {"evac": 0, "P": 1, "B": 2, "D": 3, "C": 4, "A": 5}
    used = {"tb": 0, "ob": 0, "sb": 0}
    bank = {"nat": "tb", "ynat": "tb ob", "qrows": "tb", "kvrows": "tb", "A": "sb", "B": "tb", "C": "ob", "D": "tb", "do": "ob"}
    out = []
    for jobs in slots:
        row = []
        for kind, what in sorted(jobs, key=lambda j: rank.get(j[0], 6)):
            banks = bank.get(kind, "")
            if kind == "soft":
                banks = ("tb", "ob", "ob", "")[what[1]]
            if kind == "fin":
                banks = "ob" if what == 1 else ""
            use = {}
            for b in banks.split():
                use[b] = used[b]
                used[b] += 1
            row.append((kind, what, use))
        out.append(row)
    return out, used


PLAN, USED = plan()
USE = {(kind, what): use for jobs in PLAN for kind, what, use in jobs}
SLOT = {(kind, what): s for s, jobs in enumerate(PLAN) for kind, what, _ in jobs}
LAST_STEP = {}
for _t, (_kind, _h, _i, _s) in enumerate(STEPS):
    LAST_STEP[_kind, _h] = _t
NAT_K = [n for n, t in enumerate(TILES) if t[0] in ("mk", "kd", "kw")]
NAT_V = [n for n, t in enumerate(TILES) if t[0] in ("mv", "vd", "vw")]
PAIRS = 3


ORDER_OF = {0: 0, 1: 1, 2: 2, 3: 3, 6: 4, 4: 5, 5: 6}
KEPT_KINDS = ("qd", "qw", "qm", "kd", "kw", "vd", "vw", "gd", "gw")
KEPT = {}
for _tile in TILES:
    if _tile[0] in KEPT_KINDS:
        KEPT[_tile] = len(KEPT) + 1
TANHS = {n: i for i, n in enumerate(n for n, t in enumerate(TILES) if t[0][0] == "g")}
RECS, SCORES_READ = {}, {}
for _t, _step in enumerate(STEPS):
    if _step[0] != "diff":
        RECS[_t] = len(RECS)
    SCORES_READ[_t] = sum(x[0] != "mem" for x in STEPS[:_t + 1])


UNITS = [(s, kind == "dv", what) for s, jobs in enumerate(PLAN) for kind, what, _ in jobs if kind in ("dk", "dv")]
UNIT_AT = {(value, u): i for i, (_, value, u) in enumerate(UNITS)}
LANDED = []
for _i, (_, _value, _u) in enumerate(UNITS):
    _g, _c, _b, _tile = unit(_u, _value)
    _before = LANDED[_i - PAGE_RING] if _i >= PAGE_RING else 0
    LANDED.append(_before + (32 if (_g, _c, _tile) == (1, 0, 1) else 16))


def hybrid_decoder(nc, x_prompt, x_sample, mem_prompt, cache_k_diff, cache_v_diff, page_table, cache_k_win,
                   cache_v_win, cache_mem_k, cache_mem_v, g_norm, w_in, lambda_q1, lambda_k1, lambda_q2, lambda_k2,
                   g_subln, g_mem_norm, w_mem_kv, w_out, g_final, bias_tables, bias_small, identity,
                   y_prompt, y_sample, k_diff_prompt, v_diff_prompt, k_win_prompt, v_win_prompt, mem_k_prompt,
                   mem_v_prompt, k_diff_sample, v_diff_sample, k_win_sample, v_win_sample, q_rows_dram):
    with ExitStack() as ctx:
        def sb(name, shape, dt=F32):
            return ctx.enter_context(nc.sbuf_tensor(name, shape, dt))

        def sem(name):
            return ctx.enter_context(nc.semaphore(name))

        act_hi = sb("act_hi", [P, KT, TOK], F32R)
        act_lo = sb("act_lo", [P, KT, TOK], F32R)
        w_raw = sb("w_raw", [P, WIN_RING, 4 * P])
        w_hi = sb("w_hi", [P, SPLIT_RING, 4 * P], F32R)
        w_lo = sb("w_lo", [P, SPLIT_RING, 4 * P], F32R)
        cat = sb("cat", [P, KT * TOK])
        cat_t = cat[:, :].rearrange("p (k t) -> p k t", k=KT)
        nat = cat[:, 0:NBLK * D_MODEL].rearrange("p (t f) -> p t f", t=NBLK)
        kT = sb("kT", [P, 4 * TOK])
        kT_t = kT[:, :].rearrange("p (k t) -> p k t", k=4)
        gate = sb("gate", [P, 4 * TOK])
        gate_t = gate[:, :].rearrange("p (k t) -> p k t", k=4)
        v_nat = sb("v_nat", [P, 2, NBLK, 2 * P])
        k_nat = sb("k_nat", [P, NBLK, P])
        tall = sb("tall", [P, TOK])
        mk_T = sb("mk_T", [P, H, N_MEM])
        mv_nat = sb("mv_nat", [P, 2, H * P])
        bias = sb("bias", [P, 2, SEQ])
        probs = sb("probs", [P, 2, SEQ])
        probs_T = sb("probs_T", [P, SEQ])
        o_nat = sb("o_nat", [P, 2 * P])
        pages = sb("pages", [P, PAGE_RING, 512])
        q_bc = sb("q_bc", [P, 2, 512])
        v_acc = sb("v_acc", [P, 4, 512])
        dec_s = sb("dec_s", [P, 512])
        dec_a = sb("dec_a", [P, PAGES, DB * H])
        ident = sb("ident", [P, P])
        ones = sb("ones", [P, P])
        b_small = sb("b_small", [P, PAGES * H + 4 * H + P])
        rows = sb("rows", [P, 2, P])
        q_s = sb("q_s", [P, KT, DB])
        k_s = sb("k_s", [P, 12, DB])
        v_s = sb("v_s", [P, 12, DB])
        g_s = sb("g_s", [P, 12, DB])
        o_s = sb("o_s", [P, 16, DB])
        gn = sb("gn", [P, KT])
        gmn = sb("gmn", [P, KT])
        gsub = sb("gsub", [P, 2])
        gsub_c = sb("gsub_c", [P, 2])
        lam_in = sb("lam_in", [P, 4])
        lam_w = sb("lam_w", [P, 8])
        power = sb("power", [P, 32])
        ids = sb("ids", [1, DB * PAGES], I32)
        tok_ss = sb("tok_ss", [P, 8])
        tok_r = sb("tok_r", [P, 8])
        tok_s = sb("tok_s", [P, KT, DB])
        a_new = sb("a_new", [P, 2, DB * H])
        tmp = sb("tmp", [P, H, DB])
        y_ss = sb("y_ss", [P, 5, KT])
        y_sum = sb("y_sum", [P, 5])
        y_r = sb("y_r", [P, 5])
        st_m = sb("st_m", [P, 2, 2])
        st_n = sb("st_n", [P, 2, 2])
        st_l = sb("st_l", [P, 2, 2])
        st_r = sb("st_r", [P, 2, 3])
        st_q = sb("st_q", [P, 2, 2])
        dc = sb("dc", [P, 8, 64])
        z = [ctx.enter_context(nc.psum_tensor(f"z{i}", [P, 2, 512], F32)) for i in range(2)]
        s_ps = ctx.enter_context(nc.psum_tensor("s_ps", [P, 2, 512], F32))
        t_ps = ctx.enter_context(nc.psum_tensor("t_ps", [P, 512], F32))
        o_ps = ctx.enter_context(nc.psum_tensor("o_ps", [P, 512], F32))

        SMALL = ["ident", "bsmall", "gn", "gmn", "gsub", "lam", "ids"]
        s_const = sem("const_loaded")
        s_ident = sem("identity_loaded")
        s_gm = sem("g_mem_loaded")
        s_tok = [sem(f"tokens_loaded{i}") for i in range(7)]
        s_ss = sem("token_squares")
        s_r1 = sem("token_mean")
        s_rr = sem("token_rstd")
        s_scaled = sem("tokens_scaled")
        s_pfull = sem("prep_full")
        s_phi = sem("prep_hi")
        s_plo = sem("prep_lo")
        s_raw = [sem(f"weights_loaded{i}") for i in range(WIN_RING)]
        s_hi = sem("weights_hi")
        s_lo = sem("weights_lo")
        s_quarter = sem("quarter_multiplied")
        s_zfree = [sem("z0_free"), sem("z1_free")]
        s_tanh = sem("gate_tanh")
        s_bias = [sem("bias_loaded0"), sem("bias_loaded1")]
        s_sfull, s_sfree = sem("scores_full"), sem("scores_free")
        s_tfull, s_tfree = sem("turned_full"), sem("turned_free")
        s_ofull, s_ofree = sem("out_full"), sem("out_free")
        s_max, s_exp, s_rec, s_probs = sem("row_max"), sem("probs_exp"), sem("probs_rec"), sem("probs_ready")
        s_osq, s_opow1, s_orstd = sem("o_squares"), sem("o_mean"), sem("o_rstd")
        s_kout, s_vout = sem("k_stored"), [sem("v_stored0"), sem("v_stored1")]
        s_mvout = sem("mv_stored")
        s_keep = sem("sample_columns_kept")
        s_lam, s_lamp, s_lame = sem("lambda_products"), sem("lambda_sums"), sem("lambda_exp")
        s_neglam = sem("lambda_ready")
        s_init = sem("constants_set")
        s_qrow, s_qdram = sem("q_rows_ready"), sem("q_rows_stored")
        s_kvrow, s_kvout = sem("kv_rows_ready"), [sem("k_rows_stored"), sem("v_rows_stored")]
        s_qbc = [sem("q_bc_loaded0"), sem("q_bc_loaded1")]
        s_page = [sem(f"page_loaded{i}") for i in range(PAGE_RING)]
        s_unit = sem("unit_done")
        s_dsm, s_dexp = sem("decode_softmax_dve"), sem("decode_exp")
        s_dprod = sem("new_key_products")
        s_fin, s_finp = sem("decode_out_dve"), sem("decode_out_rstd")
        s_gated = sem("memory_gated")
        s_chi, s_clo = sem("cat_hi"), sem("cat_lo")
        s_res = [sem(f"residual_loaded{i}") for i in range(5)]
        s_gf = sem("g_final_loaded")
        s_ysq = sem("y_squares")
        s_yg = sem("y_times_g")
        s_yr, s_yrp = sem("y_mean"), sem("y_rstd")
        s_ydone = [sem(f"y_done{i}") for i in range(5)]
        s_yout = sem("y_stored")
        s_chain = sem("vector_chain")
        s_pchain = sem("pool_chain")
        s_achain = sem("scalar_chain")

        x_t = x_prompt.rearrange("a (t p) f -> (a t) p f", p=P)
        m_t = mem_prompt.rearrange("a (t p) f -> (a t) p f", p=P)
        xs = x_sample.rearrange("b a f -> (b a) f")
        w_dram = {"m": w_mem_kv, "i": w_in, "o": w_out}
        w_view = {k: v.rearrange("a (r k p) f -> (a r) p k f", r=4, p=P) for k, v in w_dram.items()}
        kpages = cache_k_diff.rearrange("a n p h c d -> (a n) p (h c d)")
        vpages = cache_v_diff.rearrange("a n p h d -> (a n) p (h d)")
        kwin = cache_k_win.rearrange("a b w h d -> (a b) w (h d)")
        vwin = cache_v_win.rearrange("a b w h d -> (a b) w (h d)")
        kmem = cache_mem_k.rearrange("a b w h d -> (a b) w (h d)")
        vmem = cache_mem_v.rearrange("a b w h d -> (a b) w (h d)")
        out_nat = {
            "kd": k_diff_prompt.rearrange("a b (t p) h c d -> p (a b t) (h c d)", p=P),
            "vd": v_diff_prompt.rearrange("a b (t p) h d -> p (a b t) (h d)", p=P),
            "kw": k_win_prompt.rearrange("a b (t p) h d -> p (a b t) (h d)", p=P),
            "vw": v_win_prompt.rearrange("a b (t p) h d -> p (a b t) (h d)", p=P),
            "mk": mem_k_prompt.rearrange("a b (t p) h d -> p (a b t) (h d)", p=P),
            "mv": mem_v_prompt.rearrange("a b (t p) h d -> p (a b t) (h d)", p=P),
        }
        out_rows = [
            [(k_diff_sample.rearrange("a b s h c d -> (a b s) (h c d)"), 8), (k_win_sample.rearrange("a b s h d -> (a b s) (h d)"), 4)],
            [(v_diff_sample.rearrange("a b s h d -> (a b s) (h d)"), 8), (v_win_sample.rearrange("a b s h d -> (a b s) (h d)"), 4)],
        ]
        x_s_nat = kT[0:DB, 0:D_MODEL]
        y_s_nat = gate[0:DB, 0:D_MODEL]
        g_fin = pages[:, 0:4, :].rearrange("p a b -> p (a b)")
        bd = b_small[:, 0:PAGES * H].rearrange("p (t h) -> p t h", h=H)
        bw = b_small[:, PAGES * H:PAGES * H + 4 * H].rearrange("p (t h) -> p t h", h=H)
        bn = b_small[:, PAGES * H + 4 * H:].rearrange("p (g n) -> p g n", g=2)
        SAMPLE = slice(SEQ, TOK)
        PROD, SNEW, MB, M1, L1, LR, DIAG, SQ = (dc[:, i, :] for i in range(8))

        def par(kind, h):
            return h % 2

        def key_slot(kind, h, c):
            return 2 * (h % 2) + c if kind == "kd" else h

        def gate_slot(kind, h, c):
            return {"gd": 2 * (h % 2) + c, "gw": 2 * (h % 2), "gm": 2 * (h % 2) + 1}[kind]

        def sample_slot(kind, h, c):
            return 2 * h + c if kind[1] == "d" else 8 + h

        def quarter_source(q):
            n, r = divmod(q, 4)
            kind, h, c = TILES[n]
            if n < FIRST_IN:
                col = (h + (H if kind == "mv" else 0)) * P
                return w_view["m"][r, :, :, col:col + P]
            if n < FIRST_OUT:
                col = COL[kind] + (2 * h + c if kind[1] == "d" else h) * P
                return w_view["i"][r, :, :, col:col + P]
            return w_view["o"][r, :, :, h * P:(h + 1) * P]

        def bias_index(kind, h):
            return h if kind == "diff" else H + h

        block = ctx.enter_context(nc.Block())

        @block.sync
        def _(sp):
            def weights(q):
                if q >= WIN_RING:
                    sp.wait_ge(s_lo, q - WIN_RING + 1)
                dst = w_raw[:, q % WIN_RING, :].rearrange("p (k f) -> p k f", k=4)
                sp.dma_start(dst, quarter_source(q)).then_inc(s_raw[q % WIN_RING], 16)

            def bias_table(i):
                if i >= 2:
                    prev = ("diff", i - 2) if i - 2 < H else ("dil", i - 2 - H)
                    sp.wait_ge(s_sfree, SCORES_READ[LAST_STEP[prev]])
                sp.dma_start(bias[:, i % 2, :], bias_tables[i]).then_inc(s_bias[i % 2], 16)

            def q_broadcast(i):
                if i >= 2:
                    sp.wait_ge(s_unit, UNIT_AT[False, last_of_row(i - 2)] + 1)
                sp.wait_ge(s_qdram, 16 if i < 16 else 32)
                b, c = divmod(i % 16, 2)
                first = (0 if i < 16 else 8) + 4 * c
                src = q_rows_dram.rearrange("(t b) d -> b t d", b=DB)[b:b + 1, first:first + 4, :]
                dst = q_bc[:, i % 2, :].rearrange("p (t d) -> p t d", t=4)
                sp.dma_start(dst, src.broadcast_to((P, 4, P))).then_inc(s_qbc[i % 2], 16)

            page_ids = {}

            def cache_unit(seq, value, u):
                g, c, b, t = unit(u, value)
                slot = seq % PAGE_RING
                if seq >= PAGE_RING:
                    sp.wait_ge(s_unit, seq - PAGE_RING + 1)
                dst = pages[:, slot, :]
                if g == 0:
                    if c == 0:
                        page_ids[t] = sp.value_load(ids[0:1, b * PAGES + t:b * PAGES + t + 1], min_val=0,
                                                    max_val=kpages.shape[0] - 1)
                    src = (vpages if value else kpages)[bass.ds(page_ids[t], 1), :, c * 512:(c + 1) * 512]
                    sp.dma_start(dst, src.rearrange("a p f -> (a p) f")).then_inc(s_page[slot], 16)
                elif c == 1:
                    src = (vmem if value else kmem)[b, t * P:(t + 1) * P, :]
                    sp.dma_start(dst, src).then_inc(s_page[slot], 16)
                elif t == 0:
                    src = (vwin if value else kwin)[b, PAST - P:PAST, :]
                    sp.dma_start(dst, src).then_inc(s_page[slot], 16)
                else:
                    cache = vwin if value else kwin
                    n4 = 96
                    near = cache[b, 512:896, :].rearrange("(k r) f -> k r f", r=4)[:, 0, :]
                    far = cache[b, 0:512, :].rearrange("(k r) f -> k r f", r=16)[:, 0, :]
                    sp.dma_start(dst[0:n4, :], near).then_inc(s_page[slot], 16)
                    sp.dma_start(dst[n4:P, :], far).then_inc(s_page[slot], 16)

            sp.dma_start(nat[:, 0, :], m_t[0]).then_inc(s_tok[0], 16)
            sp.dma_start(nat[:, 1, :], m_t[1]).then_inc(s_tok[1], 16)
            sp.dma_start(ident[:, :], identity).then_inc(s_ident, 16)
            sp.dma_start(gmn[:, :], g_mem_norm.rearrange("a (k p) -> p (a k)", p=P),
                         allow_slow_non_contiguous=True).then_inc(s_gm, 16)
            for q in range(2):
                weights(q)
            sp.dma_start(b_small[:, :], bias_small).then_inc(s_const, 16)
            sp.dma_start(gn[:, :], g_norm.rearrange("a (k p) -> p (a k)", p=P),
                         allow_slow_non_contiguous=True).then_inc(s_const, 16)
            sp.dma_start(gsub[:, :], g_subln.rearrange("a (k p) -> p (a k)", p=P),
                         allow_slow_non_contiguous=True).then_inc(s_const, 16)
            for i, v in enumerate((lambda_q1, lambda_k1, lambda_q2, lambda_k2)):
                sp.dma_start(lam_in[:, i:i + 1], v.rearrange("a p -> p a"),
                             allow_slow_non_contiguous=True).then_inc(s_const, 16)
            sp.dma_start(ids[:, :], page_table.rearrange("(a b) n -> a (b n)", a=1)).then_inc(s_const, 16)
            for q in range(2, 4):
                weights(q)
            for q in range(4, WIN_RING - 1):
                weights(q)
            for i in range(2, 4):
                sp.dma_start(nat[:, i, :], x_t[i]).then_inc(s_tok[i], 16)
            sp.dma_start(x_s_nat, xs).then_inc(s_tok[6], 16)
            sp.wait_ge(s_const, 16 * 8)

            order = UNITS
            sent = 0
            q_sent = 0
            for s, jobs in enumerate(PLAN):
                if WIN_RING - 1 + s < QUARTERS:
                    weights(WIN_RING - 1 + s)
                if s in (5, 8):
                    i = (5, 8).index(s)
                    sp.wait_ge(s_pfull, N_PREP)
                    sp.dma_start(nat[:, i, :], x_t[i]).then_inc(s_tok[4 + i], 16)
                if s in (30, 31):
                    bias_table(s - 30)
                while sent < len(order) and order[sent][0] <= s + 3 and sent < PAGE_RING + sum(
                        1 for o in order[:sent + 1] if o[0] < s):
                    _, value, u = order[sent]
                    if not value:
                        need = q_row(u) + 1
                        if SLOT["qrows", 0 if u < 128 else 1] >= s - 1:
                            break
                        while q_sent < need:
                            q_broadcast(q_sent)
                            q_sent += 1
                    cache_unit(sent, value, u)
                    sent += 1
                for i in range(2, 2 * H):
                    prev = ("diff", i - 2) if i - 2 < H else ("dil", i - 2 - H)
                    if SLOT["A", LAST_STEP[prev]] + 1 == s:
                        bias_table(i)
                for kind, what, use in (PLAN[s - 1] if s else []):
                    if kind == "nat":
                        tile_kind, h, c = TILES[what]
                        j = 2 * h + c if tile_kind[1] == "d" else h
                        dst = out_nat[tile_kind][:, :, j * P:(j + 1) * P]
                        if tile_kind in ("mk", "kd", "kw"):
                            sp.wait_ge(s_tfree, use["tb"] + 1)
                            nb = 2 if tile_kind == "mk" else NBLK
                            sp.dma_start(dst, k_nat[:, 0:nb, :]).then_inc(s_kout, 16)
                        elif tile_kind == "mv":
                            sp.wait_ge(s_tfree, use["tb"] + 1)
                            sp.dma_start(dst, mv_nat[:, :, j * P:(j + 1) * P]).then_inc(s_mvout, 16)
                        else:
                            sp.wait_ge(s_tfree, use["tb"] + 1)
                            sp.dma_start(dst, v_nat[:, h % 2, :, c * P:(c + 1) * P]).then_inc(s_vout[h % 2], 16)
                    if kind == "qrows":
                        sp.wait_ge(s_tfree, use["tb"] + 1)
                        sp.dma_start(q_rows_dram[what * 64:what * 64 + 64, :], rows[0:64, what, :]).then_inc(s_qdram, 16)
                    if kind == "kvrows":
                        sp.wait_ge(s_tfree, use["tb"] + 1)
                        row = 0
                        for dst, nt in out_rows[what]:
                            for t in range(nt):
                                sp.dma_start(dst[:, t * P:(t + 1) * P], rows[row:row + DB, what, :]).then_inc(s_kvout[what], 16)
                                row += DB
                if s == IN_END + 2:
                    sp.wait_ge(s_clo, KT)
                    for i in range(NBLK):
                        sp.dma_start(nat[:, i, :], x_t[i]).then_inc(s_res[i], 16)
                    sp.dma_start(y_s_nat, xs).then_inc(s_res[4], 16)
                    sp.wait_ge(s_unit, len(order))
                    sp.dma_start(g_fin, g_final.rearrange("(a f) -> a f", a=1).broadcast_to((P, D_MODEL))).then_inc(s_gf, 16)
            assert sent == len(order)
            for i in range(NBLK):
                sp.wait_ge(s_ydone[i], 1)
                sp.dma_start(y_prompt.rearrange("a (t p) f -> (a t) p f", p=P)[i], nat[:, i, :]).then_inc(s_yout, 16)
            sp.wait_ge(s_ydone[4], 1)
            sp.dma_start(y_sample.rearrange("b a f -> (b a) f"), y_s_nat).then_inc(s_yout, 16)
            sp.wait_ge(s_yout, 16 * 5)
            sp.wait_ge(s_kout, 16 * len(NAT_K))
            sp.wait_ge(s_mvout, 16 * H)
            for i in range(2):
                sp.wait_ge(s_vout[i], 16 * (4 + 2))
                sp.wait_ge(s_kvout[i], 16 * 12)
            sp.wait_ge(s_qdram, 32)

        def prep_base(pair):
            return {0: 0, 1: N_PREP, 2: 2 * N_PREP + 1}[pair]

        @block.tensor
        def _(pe):
            def prep(pair, u):
                use = prep_base(pair) + u
                pe.wait_ge(s_scaled, (2, 4, 7)[pair])
                if use >= 2:
                    pe.wait_ge(s_plo, use - 1)
                first = 2 if pair == 1 else 0
                for k in range(2):
                    for t in range(2):
                        kt = 2 * u + k
                        last = nc.tensor.transpose(s_ps[:, use % 2, (2 * k + t) * P:(2 * k + t + 1) * P],
                                                   nat[:, first + t, kt * P:(kt + 1) * P], ident[:, :])
                last.then_inc(s_pfull, 1)

            def prep_sample():
                use = 2 * N_PREP
                pe.wait_ge(s_scaled, 5)
                pe.wait_ge(s_plo, use - 1)
                for kt in range(KT):
                    last = nc.tensor.transpose(s_ps[:, use % 2, kt * DB:(kt + 1) * DB],
                                               x_s_nat[:, kt * P:(kt + 1) * P], ident[0:DB, 0:DB])
                last.then_inc(s_pfull, 1)

            def quarter(q):
                n, r = divmod(q, 4)
                zb = z[n % 2]
                if r == 0 and n >= 2:
                    pe.wait_ge(s_zfree[n % 2], n // 2)
                pe.wait_ge(s_lo, q + 1)
                if n == FIRST_IN:
                    pe.wait_ge(s_plo, prep_base(2) + 2 * r + 2)
                if n == 0:
                    pe.wait_ge(s_plo, 2 * r + 2)
                if n == FIRST_OUT:
                    pe.wait_ge(s_clo, 4 * r + 4)
                hi, lo = w_hi[:, q % SPLIT_RING, :], w_lo[:, q % SPLIT_RING, :]
                parts = [(0, 0, N_MEM)] if n < FIRST_IN else [(0, 0, HALF), (1, HALF, TOK)]
                for j in range(4):
                    kt = 4 * r + j
                    w = slice(j * P, (j + 1) * P)
                    for m, (lhs, rhs) in enumerate(((hi, act_hi), (hi, act_lo), (lo, act_hi))):
                        for bank, a, b in parts:
                            last = nc.tensor.matmul(zb[:, bank, 0:b - a], lhs[:, w], rhs[:, kt, a:b],
                                                    start=(kt == 0 and m == 0), stop=(kt == KT - 1 and m == 2))
                last.then_inc(s_quarter, 1)

            def turn_ready(use):
                if use["tb"] >= 1:
                    pe.wait_ge(s_tfree, use["tb"])

            def out_ready(use):
                if use["ob"] >= 1:
                    pe.wait_ge(s_ofree, use["ob"])

            def natural(n, use):
                kind, h, c = TILES[n]
                pe.wait_ge(s_zfree[n % 2], n // 2 + 1)
                turn_ready(use)
                src = {"mk": lambda: mk_T[:, h, :], "kd": lambda: kT_t[:, key_slot(kind, h, c), :],
                       "kw": lambda: kT_t[:, key_slot(kind, h, c), :]}.get(kind, lambda: tall[:, :])()
                for b in range(2 if kind[0] == "m" else NBLK):
                    last = nc.tensor.transpose(t_ps[:, b * P:(b + 1) * P], src[:, b * P:(b + 1) * P], ident[:, :])
                if kind == "y":
                    last.then_inc(s_tfull, 1)
                    out_ready(use)
                    last = nc.tensor.transpose(o_ps[0:DB, 0:P], src[:, SAMPLE], ident[:, :])
                    last.then_inc(s_ofull, 1)
                else:
                    last.then_inc(s_tfull, 1)

            def step_scores(t, use):
                kind, h, i, _ = STEPS[t]
                if t and STEPS[t - 1][0] == "mem":
                    pe.wait_ge(s_exp, t)
                elif t:
                    pe.wait_ge(s_sfree, SCORES_READ[t - 1])
                if kind == "diff":
                    n = AT["kd", h, 1]
                    pe.wait_ge(s_zfree[n % 2], n // 2 + 1)
                    for c in range(2):
                        last = nc.tensor.matmul(s_ps[:, c, 0:(i + 1) * P], cat_t[:, 2 * h + c, i * P:(i + 1) * P],
                                                kT_t[:, key_slot("kd", h, c), 0:(i + 1) * P], start=True, stop=True)
                elif kind == "dil":
                    n = AT["kw", h, 0]
                    pe.wait_ge(s_zfree[n % 2], n // 2 + 1)
                    last = nc.tensor.matmul(s_ps[:, 0, 0:(i + 1) * P], cat_t[:, 2 * H + h, i * P:(i + 1) * P],
                                            kT_t[:, key_slot("kw", h, 0), 0:(i + 1) * P], start=True, stop=True)
                else:
                    n = AT["qm", h, 0]
                    pe.wait_ge(s_zfree[n % 2], n // 2 + 1)
                    for c in range(2):
                        b = 2 * i + c
                        last = nc.tensor.matmul(s_ps[:, c, 0:N_MEM], cat_t[:, 3 * H + h, b * P:(b + 1) * P],
                                                mk_T[:, h, :], start=True, stop=True)
                last.then_inc(s_sfull, 1)

            def step_turn(t, use):
                kind, h, i, _ = STEPS[t]
                pe.wait_ge(s_probs, t + 1)
                turn_ready(use)
                if kind == "mem":
                    for kb in range(2):
                        for c in range(2):
                            k = 2 * kb + c
                            last = nc.tensor.transpose(t_ps[:, k * P:(k + 1) * P], probs[:, c, kb * P:(kb + 1) * P], ident[:, :])
                else:
                    for kb in range(i + 1):
                        last = nc.tensor.transpose(t_ps[:, kb * P:(kb + 1) * P], probs[:, 0, kb * P:(kb + 1) * P], ident[:, :])
                last.then_inc(s_tfull, 1)

            def step_values(t, use):
                kind, h, i, _ = STEPS[t]
                pe.wait_ge(s_tfree, USE["B", t]["tb"] + 1)
                out_ready(use)
                if kind == "diff":
                    pe.wait_ge(s_tfree, USE["nat", AT["vd", h, 1]]["tb"] + 1)
                    for kb in range(i + 1):
                        last = nc.tensor.matmul(o_ps[:, 0:2 * P], probs_T[:, kb * P:(kb + 1) * P],
                                                v_nat[:, h % 2, kb, :], start=(kb == 0), stop=(kb == i))
                elif kind == "dil":
                    pe.wait_ge(s_tfree, USE["nat", AT["vw", h, 0]]["tb"] + 1)
                    for kb in range(i + 1):
                        last = nc.tensor.matmul(o_ps[:, 0:P], v_nat[:, h % 2, kb, 0:P],
                                                probs_T[:, kb * P:(kb + 1) * P], start=(kb == 0), stop=(kb == i))
                else:
                    for kb in range(2):
                        last = nc.tensor.matmul(o_ps[:, 0:2 * P], mv_nat[:, kb, h * P:(h + 1) * P],
                                                probs_T[:, kb * 2 * P:(kb + 1) * 2 * P], start=(kb == 0), stop=(kb == 1))
                last.then_inc(s_ofull, 1)

            def step_turn_out(t, use):
                pe.wait_ge(s_ofree, USE["C", t]["ob"] + 1)
                turn_ready(use)
                for c in range(2):
                    last = nc.tensor.transpose(t_ps[:, c * P:(c + 1) * P], o_nat[:, c * P:(c + 1) * P], ident[:, :])
                last.then_inc(s_tfull, 1)

            def sample_rows(src, count, use):
                turn_ready(use)
                nc.tensor.transpose(t_ps[0:count, 0:P], src, ident[:, :]).then_inc(s_tfull, 1)

            def soft(g, k, use):
                if k == 0:
                    pe.wait_ge(s_dsm, 5 * g + 1)
                    turn_ready(use)
                    nc.tensor.transpose(t_ps[0:64, 0:P], M1, ident[:, :]).then_inc(s_tfull, 1)
                if k == 1:
                    pe.wait_ge(s_dsm, 5 * g + 2)
                    pe.wait_ge(s_dprod, g + 1)
                    out_ready(use)
                    nc.tensor.matmul(o_ps[:, 0:64], ones[0:64, :], DIAG[0:64, :], start=True, stop=True)
                    nc.tensor.matmul(o_ps[:, 64:128], ones[:, :], PROD, start=True, stop=True).then_inc(s_ofull, 1)
                if k == 2:
                    pe.wait_ge(s_dsm, 5 * g + 5)
                    out_ready(use)
                    nc.tensor.matmul(o_ps[:, 0:64], ones[:, :], L1, start=True, stop=True).then_inc(s_ofull, 1)

            def sum_values(i, use):
                pe.wait_ge(s_unit, UNIT_AT[True, last_of(i)] + 1)
                out_ready(use)
                for k in range(8):
                    last = nc.tensor.matmul(o_ps[:, k:k + 1], v_acc[:, 2 * (i % 2) + k // 4, k % 4 * P:(k % 4 + 1) * P],
                                            ones[:, 0:1], start=True, stop=True)
                last.then_inc(s_ofull, 1)

            pe.wait_ge(s_ident, 16)
            for u in range(4):
                prep(0, u)
            quarter(0)
            prep(0, 4)
            prep(0, 5)
            quarter(1)
            prep(0, 6)
            prep(0, 7)
            pe.wait_ge(s_lam, 1)
            nc.tensor.matmul(z[1][:, 0, 0:2], ones[:, :], lam_w[:, 0:2], start=True, stop=True).then_inc(s_lamp, 1)
            for s, jobs in enumerate(PLAN):
                if 2 <= s < QUARTERS:
                    if s == 4:
                        pe.wait_ge(s_lame, 1)
                    quarter(s)
                for kind, what, use in jobs:
                    if kind == "prep":
                        prep(*what)
                    elif kind == "prep_sample":
                        prep_sample()
                    elif kind in ("nat", "ynat"):
                        natural(what, use)
                    elif kind == "A":
                        step_scores(what, use)
                    elif kind == "B":
                        step_turn(what, use)
                    elif kind == "C":
                        step_values(what, use)
                    elif kind == "D":
                        step_turn_out(what, use)
                    elif kind == "qrows":
                        pe.wait_ge(s_keep, 8 if what == 0 else KEPT["qm", 3, 0])
                        sample_rows(q_s[:, 8 * what:8 * what + 8, :].rearrange("p t b -> p (t b)"), 64, use)
                    elif kind == "kvrows":
                        pe.wait_ge(s_keep, KEPT["vw", 3, 0])
                        sample_rows((v_s if what else k_s)[:, :, :].rearrange("p t b -> p (t b)"), 96, use)
                    elif kind == "soft":
                        soft(*what, use)
                    elif kind == "do":
                        sum_values(what, use)
                    elif kind == "fin" and what == 1:
                        pe.wait_ge(s_fin, 1)
                        out_ready(use)
                        nc.tensor.matmul(o_ps[:, 0:64], ones[:, :], SQ, start=True, stop=True).then_inc(s_ofull, 1)

        @block.scalar
        def _(act):
            chain = [0]

            def link(ins):
                chain[0] += 1
                ins.then_inc(s_achain, 1)
                act.wait_ge(s_achain, chain[0])

            def squares(i):
                n = DB if i == 6 else P
                src = x_s_nat if i == 6 else nat[:, i % 4, :]
                act.wait_ge(s_tok[i], 16)
                if i >= 1:
                    act.wait_ge(s_ss, ORDER_OF[i])
                nc.scalar.activation(gate[0:n, 0:D_MODEL], src, ACT.Square, accum_out=tok_ss[0:n, i:i + 1]).then_inc(s_ss, 1)

            def prep_hi(pair, u):
                use = prep_base(pair) + u
                g = gmn if pair == 0 else gn
                act.wait_ge(s_pfull, use + 1)
                if pair == 2:
                    act.wait_ge(s_quarter, 4 * FIRST_IN - 3 + u // 2)
                first = N_MEM if pair == 1 else 0
                for k in range(2):
                    kt = 2 * u + k
                    last = nc.scalar.activation(act_hi[:, kt, first:first + 2 * P], s_ps[:, use % 2, k * 2 * P:(k + 1) * 2 * P],
                                                ACT.Identity, scale=g[:, kt:kt + 1])
                last.then_inc(s_phi, 1)

            def split_hi(q):
                act.wait_ge(s_raw[q % WIN_RING], 16 * (q // WIN_RING + 1))
                if q >= SPLIT_RING:
                    act.wait_ge(s_quarter, q - SPLIT_RING + 1)
                nc.scalar.activation(w_hi[:, q % SPLIT_RING, :], w_raw[:, q % WIN_RING, :], ACT.Copy).then_inc(s_hi, 1)

            def evac(n):
                kind, h, c = TILES[n]
                act.wait_ge(s_quarter, 4 * n + 4)
                free = s_zfree[n % 2]
                zz = z[n % 2][:, :, 0:HALF]
                two = lambda ap: ap.rearrange("p (a t) -> p a t", a=2)
                if kind == "mk":
                    nc.scalar.activation(mk_T[:, h, :], z[n % 2][:, 0, 0:N_MEM], ACT.Copy).then_inc(free, 1)
                elif kind == "mv":
                    if h >= 1:
                        act.wait_ge(s_tfull, USE["nat", n - 1]["tb"] + 1)
                    nc.scalar.activation(tall[:, 0:N_MEM], z[n % 2][:, 0, 0:N_MEM], ACT.Copy).then_inc(free, 1)
                elif kind[0] == "q":
                    if n == FIRST_IN:
                        act.wait_ge(s_pfull, 3 * N_PREP + 1)
                    nc.scalar.activation(two(cat_t[:, cat_slot(kind, h, c), :]), zz, ACT.Copy).then_inc(free, 1)
                elif kind[0] == "k":
                    if kind == "kd" and h >= 2:
                        act.wait_ge(s_sfull, USE["A", LAST_STEP["diff", h - 2]]["sb"] + 1)
                    if kind == "kw":
                        act.wait_ge(s_sfull, USE["A", LAST_STEP["diff", 2 + h // 2]]["sb"] + 1)
                    if kind != "kd" or h >= 2:
                        act.wait_ge(s_keep, KEPT["qm", 3, 0] if kind == "kw" else KEPT["gd", h - 1, 1])
                    nc.scalar.activation(two(kT_t[:, key_slot(kind, h, c), :]), zz, ACT.Copy).then_inc(free, 1)
                elif kind[0] == "v":
                    prev = NAT_V[NAT_V.index(n) - 1]
                    act.wait_ge(s_tfull, USE["nat", prev]["tb"] + 1)
                    if TILES[prev][0] != "mv":
                        act.wait_ge(s_keep, KEPT[TILES[prev]])
                    nc.scalar.activation(two(tall[:, :]), zz, ACT.Copy).then_inc(free, 1)
                elif kind[0] == "g":
                    if kind == "gd" and h >= 2:
                        act.wait_ge(s_tfree, USE["D", LAST_STEP["diff", h - 2]]["tb"] + 1)
                    if kind == "gw":
                        if h < 2:
                            act.wait_ge(s_tfree, USE["D", LAST_STEP["diff", 2 + h]]["tb"] + 1)
                        else:
                            act.wait_ge(s_ofree, USE["C", LAST_STEP["dil", h - 2]]["ob"] + 1)
                    if kind == "gm" and h >= 2:
                        act.wait_ge(s_gated, h - 1)
                    if kind in ("gd", "gw"):
                        act.wait_ge(s_keep, KEPT[kind, h, c] - 1)
                    nc.scalar.activation(two(gate_t[:, gate_slot(kind, h, c), :]), zz, ACT.Tanh, scale=0.5).then_inc(s_tanh, 1)
                else:
                    prev = n - 1
                    if h >= 1:
                        act.wait_ge(s_ofull, USE["ynat", prev]["ob"] + 1)
                    else:
                        act.wait_ge(s_tfull, USE["nat", NAT_V[-1]]["tb"] + 1)
                        act.wait_ge(s_keep, KEPT["vw", 3, 0])
                    nc.scalar.activation(two(tall[:, :]), zz, ACT.Copy).then_inc(free, 1)

            def natural(n, use):
                kind, h, c = TILES[n]
                act.wait_ge(s_tfull, use["tb"] + 1)
                if kind in ("mk", "kd", "kw"):
                    i = NAT_K.index(n)
                    if i >= 1:
                        act.wait_ge(s_kout, 16 * i)
                    w = N_MEM if kind == "mk" else SEQ
                    nc.scalar.activation(k_nat[:, :, :].rearrange("p t d -> p (t d)")[:, 0:w], t_ps[:, 0:w], ACT.Copy).then_inc(s_tfree, 1)
                elif kind == "mv":
                    nc.scalar.activation(mv_nat[:, :, h * P:(h + 1) * P], t_ps[:, 0:N_MEM].rearrange("p (t d) -> p t d", t=2),
                                         ACT.Copy).then_inc(s_tfree, 1)
                else:
                    if kind == "vd" and h >= 2:
                        act.wait_ge(s_ofull, USE["C", LAST_STEP["diff", h - 2]]["ob"] + 1)
                        act.wait_ge(s_vout[h % 2], 32)
                    if kind == "vw":
                        before = ("diff", 2 + h) if h < 2 else ("dil", h - 2)
                        act.wait_ge(s_ofull, USE["C", LAST_STEP[before]]["ob"] + 1)
                        act.wait_ge(s_vout[h % 2], 64 if h < 2 else 80)
                    nc.scalar.activation(v_nat[:, h % 2, :, c * P:(c + 1) * P], t_ps[:, :].rearrange("p (t d) -> p t d", t=NBLK),
                                         ACT.Copy).then_inc(s_tfree, 1)

            def step_exp(t):
                kind, h, i, _ = STEPS[t]
                act.wait_ge(s_max, t + 1)
                for c in range(1 if kind == "dil" else 2):
                    w = N_MEM if kind == "mem" else (i + 1) * P
                    src = s_ps[:, c, 0:w] if kind == "mem" else probs[:, c, 0:w]
                    last = nc.scalar.activation(probs[:, c, 0:w], src, ACT.Exp, bias=st_n[:, t % 2, c:c + 1], scale=SCALE,
                                                accum_out=st_l[:, t % 2, c:c + 1])
                last.then_inc(s_exp, 1)

            def step_probs(t):
                kind, h, i, _ = STEPS[t]
                if kind != "diff":
                    act.wait_ge(s_rec, RECS[t] + 1)
                    w = N_MEM if kind == "mem" else (i + 1) * P
                    for c in range(1 if kind == "dil" else 2):
                        last = nc.scalar.activation(probs[:, c, 0:w], probs[:, c, 0:w], ACT.Identity,
                                                    scale=st_r[:, t % 2, c:c + 1])
                    last.then_inc(s_probs, 1)

            def step_turn(t, use):
                kind, h, i, _ = STEPS[t]
                w = SEQ if kind == "mem" else (i + 1) * P
                act.wait_ge(s_tfull, use["tb"] + 1)
                nc.scalar.activation(probs_T[:, 0:w], t_ps[:, 0:w], ACT.Copy).then_inc(s_tfree, 1)

            squares(0)
            squares(1)
            act.wait_ge(s_gm, 16)
            for u in range(N_PREP):
                prep_hi(0, u)
                if u in FIRST_SPLITS:
                    split_hi(FIRST_SPLITS.index(u))
            act.wait_ge(s_lamp, 1)
            nc.scalar.activation(lam_w[:, 2:4], z[1][:, 0, 0:2], ACT.Exp).then_inc(s_lame, 1)
            for s, jobs in enumerate(PLAN):
                if 2 <= s < QUARTERS - AHEAD:
                    split_hi(s + AHEAD)
                for kind, what, use in jobs:
                    if kind == "evac":
                        evac(what)
                    elif kind == "squares":
                        squares(what)
                    elif kind == "prep":
                        if what == (1, 0):
                            act.wait_ge(s_const, 16 * 8)
                        prep_hi(*what)
                    elif kind == "prep_sample":
                        act.wait_ge(s_phi, 2 * N_PREP + 1)
                        nc.scalar.activation(act_hi[:, :, SAMPLE], tok_s[:, :, :], ACT.Copy).then_inc(s_phi, 1)
                    elif kind == "nat":
                        natural(what, use)
                    elif kind == "A":
                        step_exp(what)
                    elif kind == "P":
                        step_probs(what)
                    elif kind == "B":
                        step_turn(what, use)
                    elif kind == "C" and STEPS[what][0] == "diff":
                        act.wait_ge(s_ofull, use["ob"] + 1)
                        if what >= 1:
                            act.wait_ge(s_tfull, USE["D", what - 1]["tb"] + 1)
                        nc.scalar.activation(o_nat[:, :], o_ps[:, 0:2 * P], ACT.Square,
                                             accum_out=st_q[:, 0, 0:1]).then_inc(s_osq, 1)
                    elif kind in ("qrows", "kvrows"):
                        act.wait_ge(s_tfull, use["tb"] + 1)
                        n = 64 if kind == "qrows" else 96
                        if kind == "kvrows":
                            act.wait_ge(s_qdram, 32)
                        nc.scalar.activation(rows[0:n, what, :], t_ps[0:n, 0:P], ACT.Copy).then_inc(s_tfree, 1)
                    elif kind == "soft" and what[1] == 1:
                        g = what[0]
                        act.wait_ge(s_dsm, 5 * g + 4)
                        w = 512 if g == 0 else 128
                        nc.scalar.activation(dec_s[:, 0:w], dec_s[:, 0:w], ACT.Exp, scale=SCALE)
                        nc.scalar.activation(SNEW, SNEW, ACT.Exp, scale=SCALE).then_inc(s_dexp, 1)
                    elif kind == "ynat":
                        e = TILES[what][1]
                        for i in range(NBLK + 1):
                            n = P if i < NBLK else DB
                            src = nat[:, i, e * P:(e + 1) * P] if i < NBLK else y_s_nat[:, e * P:(e + 1) * P]
                            if i < NBLK:
                                act.wait_ge(s_tfree, use["tb"] + 1)
                            else:
                                act.wait_ge(s_ofree, use["ob"] + 1)
                            if i or e:
                                act.wait_ge(s_ysq, 5 * e + i)
                            nc.scalar.activation(o_nat[0:n, 0:P], src, ACT.Square,
                                                 accum_out=y_ss[0:n, i, e:e + 1]).then_inc(s_ysq, 1)
                if IN_END - 3 <= s <= IN_END:
                    if s == IN_END - 3:
                        act.wait_ge(s_tfree, USE["D", LAST_STEP["diff", 3]]["tb"] + 1)
                        act.wait_ge(s_ofree, USE["C", LAST_STEP["dil", 3]]["ob"] + 1)
                        act.wait_ge(s_fin, 3)
                    r = s - (IN_END - 3)
                    act.wait_ge(s_quarter, IN_END - 3 + r)
                    for kt in range(4 * r, 4 * r + 4):
                        if kt >= 3 * H:
                            act.wait_ge(s_gated, kt - 3 * H + 1)
                        nc.scalar.activation(act_hi[:, kt, :], cat_t[:, kt, :], ACT.Copy).then_inc(s_chi, 1)

            act.wait_ge(s_yrp, 1)
            act.wait_ge(s_yg, KT)
            nc.scalar.activation(nat[:, 1, :], nat[:, 1, :], ACT.Copy, scale=y_r[:, 1:2]).then_inc(s_ydone[1], 1)

        @block.vector
        def _(dve):
            chain = [0]

            def link(ins):
                chain[0] += 1
                ins.then_inc(s_chain, 1)
                dve.wait_ge(s_chain, chain[0])

            def scale_tokens(i):
                n = DB if i == 6 else P
                view = x_s_nat if i == 6 else nat[:, i % 4, :]
                dve.wait_ge(s_rr, ORDER_OF[i] + 1)
                nc.vector.tensor_scalar(view, view, tok_r[0:n, i:i + 1], None, ALU.mult).then_inc(s_scaled, 1)

            def prep_lo(pair, u):
                use = prep_base(pair) + u
                g = gmn if pair == 0 else gn
                dve.wait_ge(s_phi, use + 1 + (use > 2 * N_PREP))
                first = N_MEM if pair == 1 else 0
                for k in range(2):
                    kt = 2 * u + k
                    cols = slice(first, first + 2 * P)
                    last = nc.vector.scalar_tensor_tensor(act_lo[:, kt, cols], s_ps[:, use % 2, k * 2 * P:(k + 1) * 2 * P],
                                                          g[:, kt:kt + 1], act_hi[:, kt, cols].bitcast(F32), ALU.mult, ALU.subtract)
                last.then_inc(s_plo, 1)

            def prep_sample():
                use = 2 * N_PREP
                dve.wait_ge(s_pfull, use + 1)
                src = s_ps[:, use % 2, 0:KT * DB].rearrange("p (k b) -> p k b", b=DB)
                nc.vector.tensor_tensor(tok_s[:, :, :], src, gn[:, :].unsqueeze(2).broadcast_to((P, KT, DB)), ALU.mult).then_inc(s_phi, 1)
                dve.wait_ge(s_phi, 2 * N_PREP + 2)
                nc.vector.tensor_tensor(act_lo[:, :, SAMPLE], tok_s[:, :, :], act_hi[:, :, SAMPLE].bitcast(F32), ALU.subtract).then_inc(s_plo, 1)

            def split_lo(q):
                dve.wait_ge(s_hi, q + 1)
                nc.vector.tensor_tensor(w_lo[:, q % SPLIT_RING, :], w_raw[:, q % WIN_RING, :],
                                        w_hi[:, q % SPLIT_RING, :].bitcast(F32), ALU.subtract).then_inc(s_lo, 1)

            def evac(n):
                kind, h, c = TILES[n]
                if kind[0] != "g":
                    return
                slot = gate_t[:, gate_slot(kind, h, c), :]
                dve.wait_ge(s_tanh, TANHS[n] + 1)
                two = slot.rearrange("p (a t) -> p a t", a=2)
                nc.vector.scalar_tensor_tensor(two, two, 1.0, z[n % 2][:, :, 0:HALF], ALU.add, ALU.mult).then_inc(s_zfree[n % 2], 1)
                if kind == "gm":
                    dve.wait_ge(s_zfree[n % 2], n // 2 + 1)
                    dve.wait_ge(s_ofree, max(USE["do", 15]["ob"], USE["C", LAST_STEP["mem", 3]]["ob"]) + 1)
                    out = cat_t[:, cat_slot(kind, h, c), :]
                    nc.vector.scalar_tensor_tensor(out, out, 0.5, slot, ALU.mult, ALU.mult).then_inc(s_gated, 1)

            def step_max(t, use):
                kind, h, i, _ = STEPS[t]
                tp = t % 2
                w = N_MEM if kind == "mem" else (i + 1) * P
                nc_ = 1 if kind == "dil" else 2
                dve.wait_ge(s_sfull, use["sb"] + 1)
                if kind != "mem":
                    bi = bias_index(kind, h)
                    dve.wait_ge(s_bias[bi % 2], 16 * (bi // 2 + 1))
                for c in range(nc_):
                    if kind == "mem":
                        last = nc.vector.reduce_max(st_m[:, tp, c:c + 1], s_ps[:, c, 0:w], AX_X)
                    else:
                        last = nc.vector.tensor_tensor_reduce(probs[:, c, 0:w], s_ps[:, c, 0:w], bias[:, bi % 2, SEQ - w:SEQ],
                                                              1.0, LOWEST, ALU.add, ALU.max, st_m[:, tp, c:c + 1])
                if kind == "mem":
                    link(last)
                else:
                    last.then_inc(s_sfree, 1)
                    dve.wait_ge(s_sfree, SCORES_READ[t])
                nc.vector.tensor_scalar(st_n[:, tp, 0:nc_], st_m[:, tp, 0:nc_], -SCALE, None, ALU.mult).then_inc(s_max, 1)

            def step_probs(t, use):
                kind, h, i, _ = STEPS[t]
                tp = t % 2
                w = N_MEM if kind == "mem" else (i + 1) * P
                nc_ = 1 if kind == "dil" else 2
                dve.wait_ge(s_exp, t + 1)
                if kind == "mem":
                    nc.vector.reciprocal(st_r[:, tp, 0:2], st_l[:, tp, 0:2]).then_inc(s_rec, 1)
                elif kind == "dil":
                    nc.vector.reciprocal(st_r[:, tp, 0:1], st_l[:, tp, 0:1]).then_inc(s_rec, 1)
                else:
                    link(nc.vector.reciprocal(st_r[:, tp, 0:2], st_l[:, tp, 0:2]))
                    if t == 0:
                        dve.wait_ge(s_neglam, 1)
                    nc.vector.tensor_scalar(st_r[:, tp, 2:3], st_r[:, tp, 1:2], lam_w[:, 5:6], None, ALU.mult)
                    link(nc.vector.tensor_scalar(probs[:, 0, 0:w], probs[:, 0, 0:w], st_r[:, tp, 0:1], None, ALU.mult))
                    nc.vector.scalar_tensor_tensor(probs[:, 0, 0:w], probs[:, 1, 0:w], st_r[:, tp, 2:3], probs[:, 0, 0:w],
                                                   ALU.mult, ALU.add).then_inc(s_probs, 1)

            def step_out(t, use):
                kind, h, i, _ = STEPS[t]
                if kind == "diff":
                    dve.wait_ge(s_orstd, t + 1)
                    nc.vector.tensor_scalar(o_nat[:, :], o_ps[:, 0:2 * P], st_q[:, 1, 0:1], None, ALU.mult).then_inc(s_ofree, 1)
                elif kind == "dil":
                    n = AT["gw", h, 0]
                    dve.wait_ge(s_zfree[n % 2], n // 2 + 1)
                    dve.wait_ge(s_ofull, use["ob"] + 1)
                    cols = slice(i * P, (i + 1) * P)
                    nc.vector.scalar_tensor_tensor(cat_t[:, 2 * H + h, cols], o_ps[:, 0:P], 0.5, gate_t[:, gate_slot("gw", h, 0), cols],
                                                   ALU.mult, ALU.mult).then_inc(s_ofree, 1)
                else:
                    dve.wait_ge(s_ofull, use["ob"] + 1)
                    nc.vector.tensor_copy(cat_t[:, 3 * H + h, 2 * i * P:2 * (i + 1) * P], o_ps[:, 0:2 * P]).then_inc(s_ofree, 1)

            def step_gate(t, use):
                kind, h, i, _ = STEPS[t]
                n = AT["gd", h, 1]
                dve.wait_ge(s_zfree[n % 2], n // 2 + 1)
                dve.wait_ge(s_zfree[(n - 1) % 2], (n - 1) // 2 + 1)
                dve.wait_ge(s_tfull, use["tb"] + 1)
                cols = slice(i * P, (i + 1) * P)
                for c in range(2):
                    last = nc.vector.scalar_tensor_tensor(cat_t[:, 2 * h + c, cols], t_ps[:, c * P:(c + 1) * P], gsub_c[:, c:c + 1],
                                                          gate_t[:, gate_slot("gd", h, c), cols], ALU.mult, ALU.mult)
                last.then_inc(s_tfree, 1)

            done = [0]

            def key_unit(u):
                g, c, b, t = unit(u, False)
                i = q_row(u)
                slot = done[0] % PAGE_RING
                dve.wait_ge(s_qbc[i % 2], 16 * (i // 2 + 1))
                dve.wait_ge(s_page[slot], LANDED[done[0]])
                for k in range(4):
                    if g == 0:
                        h, part = 2 * c + k // 2, k % 2
                    else:
                        h, part = k, c
                    col = t * 64 + part * 32 + b * H + h
                    seg = pages[:, slot, k * P:(k + 1) * P]
                    last = nc.vector.tensor_tensor_reduce(seg, seg, q_bc[:, i % 2, k * P:(k + 1) * P], 1.0, 0.0,
                                                          ALU.mult, ALU.add, dec_s[:, col:col + 1])
                last.then_inc(s_unit, 1)
                done[0] += 1

            def value_unit(u):
                g, c, b, t = unit(u, True)
                i = sequence(u)
                slot = done[0] % PAGE_RING
                acc = v_acc[:, 2 * (i % 2) + c, :]
                if t == 0 and c == 0 and i >= 2:
                    dve.wait_ge(s_ofree, USE["do", i - 2]["ob"] + 1)
                dve.wait_ge(s_page[slot], LANDED[done[0]])
                if t:
                    dve.wait_ge(s_unit, UNIT_AT[True, u - 2] + 1)
                for k in range(2 if g == 0 else 4):
                    w = 256 if g == 0 else 128
                    seg = slice(k * w, (k + 1) * w)
                    if g == 0:
                        a = dec_a[:, t, b * H + 2 * c + k:b * H + 2 * c + k + 1]
                    else:
                        col = t * 64 + c * 32 + b * H + k
                        a = dec_s[:, col:col + 1]
                    if t == 0:
                        last = nc.vector.tensor_scalar(acc[:, seg], pages[:, slot, seg], a, None, ALU.mult)
                    else:
                        last = nc.vector.scalar_tensor_tensor(acc[:, seg], pages[:, slot, seg], a, acc[:, seg], ALU.mult, ALU.add)
                last.then_inc(s_unit, 1)
                done[0] += 1

            def values_out(i, use):
                dve.wait_ge(s_ofull, use["ob"] + 1)
                if i < DB:
                    nc.vector.tensor_copy(o_s[:, 0:8, i], o_ps[:, 0:8]).then_inc(s_ofree, 1)
                else:
                    nc.vector.tensor_copy(o_s[:, 8:12, i - DB], o_ps[:, 0:4])
                    nc.vector.tensor_copy(cat_t[:, 3 * H:4 * H, SEQ + i - DB], o_ps[:, 4:8]).then_inc(s_ofree, 1)

            def soft(g, k, use):
                T = PAGES if g == 0 else 2
                s3 = dec_s[:, 0:T * 64].rearrange("p (t n) -> p t n", t=T)
                over = lambda ap: ap.unsqueeze(1).broadcast_to((P, T, 64))
                if k == 0:
                    dve.wait_ge(s_unit, UNIT_AT[False, 127 if g == 0 else 159] + 1)
                    if g == 0:
                        v = dec_s[:, :].rearrange("p (t b h) -> p t b h", t=T, h=H)
                        link(nc.vector.tensor_tensor(v, v, bd.unsqueeze(2).broadcast_to((P, T, 16, H)), ALU.add))
                    else:
                        v = dec_s[:, 0:128].rearrange("p (t b h) -> p t b h", t=4, h=H)
                        link(nc.vector.tensor_tensor(v, v, bw.unsqueeze(2).broadcast_to((P, 4, DB, H)), ALU.add))
                    nc.vector.tensor_reduce(M1, s3.rearrange("p t n -> p n t"), AX_X, ALU.max).then_inc(s_dsm, 1)
                    dve.wait_ge(s_keep, KEPT["kd", 3, 1] if g == 0 else KEPT["kw", 3, 0])
                    if g == 0:
                        for c in range(2):
                            prod = PROD[:, c * 32:(c + 1) * 32].rearrange("p (b h) -> p h b", h=H)
                            qv = q_s[:, 0:8, :].rearrange("p (h c) b -> p c h b", c=2)[:, c]
                            kv = k_s[:, 0:8, :].rearrange("p (h c) b -> p c h b", c=2)[:, c]
                            last = nc.vector.tensor_tensor(prod, qv, kv, ALU.mult)
                        last.then_inc(s_dprod, 1)
                    else:
                        nc.vector.memset(PROD[:, 32:64], 0.0)
                        prod = PROD[:, 0:32].rearrange("p (b h) -> p h b", h=H)
                        nc.vector.tensor_tensor(prod, q_s[:, 8:12, :], k_s[:, 8:12, :], ALU.mult).then_inc(s_dprod, 1)
                    dve.wait_ge(s_tfull, use["tb"] + 1)
                    nc.vector.reduce_max(MB[0:64, 0:1], t_ps[0:64, 0:P], AX_X).then_inc(s_tfree, 1)
                    dve.wait_ge(s_tfree, use["tb"] + 1)
                    nc.vector.tensor_scalar(DIAG[0:64, :], ident[0:64, 0:64], MB[0:64, 0:1], None, ALU.mult).then_inc(s_dsm, 1)
                if k == 1:
                    dve.wait_ge(s_ofull, use["ob"] + 1)
                    link(nc.vector.tensor_tensor(SNEW, o_ps[:, 64:128], bn[:, g, :], ALU.add))
                    nc.vector.tensor_tensor(MB, o_ps[:, 0:64], SNEW, ALU.max).then_inc(s_ofree, 1)
                    dve.wait_ge(s_ofree, use["ob"] + 1)
                    nc.vector.tensor_tensor(s3, s3, over(MB), ALU.subtract).then_inc(s_dsm, 1)
                    nc.vector.tensor_tensor(SNEW, SNEW, MB, ALU.subtract).then_inc(s_dsm, 1)
                    dve.wait_ge(s_dexp, g + 1)
                    nc.vector.tensor_reduce(L1, s3.rearrange("p t n -> p n t"), AX_X, ALU.add).then_inc(s_dsm, 1)
                if k == 2:
                    dve.wait_ge(s_ofull, use["ob"] + 1)
                    nc.vector.tensor_tensor(LR, o_ps[:, 0:64], SNEW, ALU.add).then_inc(s_ofree, 1)
                    dve.wait_ge(s_ofree, use["ob"] + 1)
                    link(nc.vector.reciprocal(LR, LR))
                    nc.vector.tensor_tensor(SNEW, SNEW, LR, ALU.mult)
                    link(nc.vector.tensor_tensor(s3, s3, over(LR), ALU.mult))
                if k == 3:
                    if g == 0:
                        nc.vector.scalar_tensor_tensor(dec_a[:, :, :], s3[:, :, 32:64], lam_w[:, 5:6], s3[:, :, 0:32], ALU.mult, ALU.add)
                        link(nc.vector.scalar_tensor_tensor(SNEW[:, 0:32], SNEW[:, 32:64], lam_w[:, 5:6], SNEW[:, 0:32], ALU.mult, ALU.add))
                        link(nc.vector.tensor_copy(a_new[:, 0, :], SNEW[:, 0:32]))
                    else:
                        link(nc.vector.tensor_copy(a_new[:, 1, :], SNEW[:, 0:32]))

            def finish(k, use):
                if k == 0:
                    dve.wait_ge(s_ofree, USE["do", 15]["ob"] + 1)
                    dve.wait_ge(s_keep, KEPT["vw", 3, 0])
                    od, vd = o_s[:, 0:8, :], v_s[:, 0:8, :]
                    an = a_new[:, 0, :].rearrange("p (b h) -> p h b", h=H)
                    for c in range(2):
                        link(nc.vector.tensor_tensor(tmp[:, 0:4, :], vd.rearrange("p (h c) b -> p c h b", c=2)[:, c], an, ALU.mult))
                        o1 = od.rearrange("p (h c) b -> p c h b", c=2)[:, c]
                        link(nc.vector.tensor_tensor(o1, o1, tmp[:, 0:4, :], ALU.add))
                    aw = a_new[:, 1, :].rearrange("p (b h) -> p h b", h=H)
                    link(nc.vector.tensor_tensor(tmp[:, 0:4, :], v_s[:, 8:12, :], aw, ALU.mult))
                    link(nc.vector.tensor_tensor(o_s[:, 8:12, :], o_s[:, 8:12, :], tmp[:, 0:4, :], ALU.add))
                    nc.vector.tensor_tensor(SQ.rearrange("p (t b) -> p t b", b=DB), od, od, ALU.mult).then_inc(s_fin, 1)
                if k == 1:
                    dve.wait_ge(s_ofull, use["ob"] + 1)
                    link(nc.vector.tensor_copy(L1, o_ps[:, 0:64]))
                    l3 = L1.rearrange("p (h c b) -> p h c b", c=2, b=DB)
                    nc.vector.tensor_tensor(M1[:, 0:32].rearrange("p (h b) -> p h b", b=DB), l3[:, :, 0, :], l3[:, :, 1, :],
                                            ALU.add).then_inc(s_ofree, 1)
                if k == 2:
                    dve.wait_ge(s_finp, 1)
                    r3 = M1[:, 32:64].rearrange("p (h b) -> p h b", b=DB)
                    for c in range(2):
                        o1 = o_s[:, 0:8, :].rearrange("p (h c) b -> p c h b", c=2)[:, c]
                        link(nc.vector.tensor_tensor(o1, o1, r3, ALU.mult))
                        link(nc.vector.tensor_scalar(o1, o1, gsub_c[:, c:c + 1], None, ALU.mult))
                    dve.wait_ge(s_keep, KEPT["gw", 3, 0])
                    nc.vector.tensor_tensor(cat_t[:, 0:8, SAMPLE], o_s[:, 0:8, :], g_s[:, 0:8, :], ALU.mult).then_inc(s_fin, 1)
                    nc.vector.scalar_tensor_tensor(cat_t[:, 8:12, SAMPLE], o_s[:, 8:12, :], 0.5, g_s[:, 8:12, :],
                                                   ALU.mult, ALU.mult).then_inc(s_fin, 1)

            def times_g(e):
                cols = slice(e * P, (e + 1) * P)
                if e == 0:
                    dve.wait_ge(s_gf, 16)
                dve.wait_ge(s_ysq, 5 * e + 5)
                g = g_fin[:, cols].unsqueeze(1).broadcast_to((P, NBLK, P))
                nc.vector.tensor_tensor(nat[:, :, cols], nat[:, :, cols], g, ALU.mult)
                nc.vector.tensor_tensor(y_s_nat[:, cols], y_s_nat[:, cols], g_fin[0:DB, cols], ALU.mult).then_inc(s_yg, 1)

            nc.vector.memset(ones[:, :], 1.0).then_inc(s_init, 1)
            nc.vector.memset(power[:, :], -0.5).then_inc(s_init, 1)
            nc.vector.memset(y_ss[:, :, :], 0.0)
            scale_tokens(0)
            scale_tokens(1)
            dve.wait_ge(s_gm, 16)
            for u in range(N_PREP):
                prep_lo(0, u)
                if u in FIRST_SPLITS:
                    split_lo(FIRST_SPLITS.index(u))
                if u == 5:
                    dve.wait_ge(s_const, 16 * 8)
                    nc.vector.tensor_tensor(lam_w[:, 0:1], lam_in[:, 0:1], lam_in[:, 1:2], ALU.mult)
                    nc.vector.tensor_tensor(lam_w[:, 1:2], lam_in[:, 2:3], lam_in[:, 3:4], ALU.mult).then_inc(s_lam, 1)
                    nc.vector.tensor_scalar(gsub_c[:, :], gsub[:, :], 0.5 * (1.0 - LAM_INIT), None, ALU.mult)
            dve.wait_ge(s_lame, 1)
            link(nc.vector.tensor_tensor(lam_w[:, 4:5], lam_w[:, 3:4], lam_w[:, 2:3], ALU.subtract))
            nc.vector.tensor_scalar(lam_w[:, 5:6], lam_w[:, 4:5], -LAM_INIT, None, ALU.add).then_inc(s_neglam, 1)
            for s, jobs in enumerate(PLAN):
                if 2 <= s < QUARTERS - AHEAD:
                    split_lo(s + AHEAD)
                for kind, what, use in jobs:
                    if kind == "evac":
                        evac(what)
                    elif kind == "scale":
                        scale_tokens(what)
                    elif kind == "prep":
                        prep_lo(*what)
                    elif kind == "prep_sample":
                        prep_sample()
                    elif kind == "A":
                        step_max(what, use)
                    elif kind == "P":
                        step_probs(what, use)
                    elif kind == "C":
                        step_out(what, use)
                    elif kind == "D":
                        step_gate(what, use)
                    elif kind == "dk":
                        key_unit(what)
                    elif kind == "dv":
                        value_unit(what)
                    elif kind == "do":
                        values_out(what, use)
                    elif kind == "soft":
                        soft(*what, use)
                    elif kind == "fin":
                        finish(what, use)
                    elif kind == "ynat":
                        e = TILES[what][1]
                        cols = slice(e * P, (e + 1) * P)
                        if e == 0:
                            for i in range(5):
                                dve.wait_ge(s_res[i], 16)
                        dve.wait_ge(s_tfull, use["tb"] + 1)
                        nc.vector.tensor_tensor(nat[:, :, cols], nat[:, :, cols], t_ps[:, :].rearrange("p (t f) -> p t f", t=NBLK),
                                                ALU.add).then_inc(s_tfree, 1)
                        dve.wait_ge(s_ofull, use["ob"] + 1)
                        nc.vector.tensor_tensor(y_s_nat[:, cols], y_s_nat[:, cols], o_ps[0:DB, 0:P], ALU.add).then_inc(s_ofree, 1)
                        if e >= 1:
                            times_g(e - 1)
                if IN_END - 3 <= s <= IN_END:
                    for kt in range(4 * (s - IN_END + 3), 4 * (s - IN_END + 3) + 4):
                        dve.wait_ge(s_chi, kt + 1)
                        nc.vector.tensor_tensor(act_lo[:, kt, :], cat_t[:, kt, :], act_hi[:, kt, :].bitcast(F32),
                                                ALU.subtract).then_inc(s_clo, 1)
            dve.wait_ge(s_ysq, 5 * KT)
            nc.vector.tensor_reduce(y_r[:, :], y_ss[:, :, :], AX_X, ALU.add).then_inc(s_yr, 1)
            times_g(KT - 1)
            dve.wait_ge(s_yrp, 1)
            dve.wait_ge(s_yg, KT)
            for i in (0, 2, 3):
                nc.vector.tensor_scalar(nat[:, i, :], nat[:, i, :], y_r[:, i:i + 1], None, ALU.mult).then_inc(s_ydone[i], 1)
            nc.vector.tensor_scalar(y_s_nat, y_s_nat, y_r[0:DB, 4:5], None, ALU.mult).then_inc(s_ydone[4], 1)

        @block.gpsimd
        def _(pool):
            chain = [0]

            def link(ins):
                chain[0] += 1
                ins.then_inc(s_pchain, 1)
                pool.wait_ge(s_pchain, chain[0])

            def token_rstd(i):
                n = DB if i == 6 else P
                pool.wait_ge(s_ss, ORDER_OF[i] + 1)
                link(nc.gpsimd.tensor_scalar(tok_r[0:n, i:i + 1], tok_ss[0:n, i:i + 1], 1.0 / D_MODEL, EPS, ALU.mult, ALU.add))
                nc.gpsimd.tensor_tensor(tok_r[0:n, i:i + 1], tok_r[0:n, i:i + 1], power[0:n, 0:1], ALU.pow).then_inc(s_rr, 1)

            def keep(n):
                kind, h, c = TILES[n]
                pool.wait_ge(s_zfree[n % 2], n // 2 + 1)
                if kind[0] == "q":
                    t = cat_slot(kind, h, c)
                    dst, src = q_s[:, t, :], cat_t[:, t, SAMPLE]
                elif kind[0] == "k":
                    dst, src = k_s[:, sample_slot(kind, h, c), :], kT_t[:, key_slot(kind, h, c), SAMPLE]
                elif kind[0] == "v":
                    dst, src = v_s[:, sample_slot(kind, h, c), :], tall[:, SAMPLE]
                else:
                    dst, src = g_s[:, sample_slot(kind, h, c), :], gate_t[:, gate_slot(kind, h, c), SAMPLE]
                nc.gpsimd.tensor_copy(dst, src).then_inc(s_keep, 1)

            pool.wait_ge(s_init, 2)
            token_rstd(0)
            token_rstd(1)
            for s, jobs in enumerate(PLAN):
                for kind, what, use in jobs:
                    if kind == "squares":
                        token_rstd(what)
                    elif kind == "evac" and TILES[what] in KEPT:
                        keep(what)
                    elif kind == "C" and STEPS[what][0] == "diff":
                        t = what
                        pool.wait_ge(s_osq, t + 1)
                        link(nc.gpsimd.tensor_scalar(st_q[:, 1, 1:2], st_q[:, 0, 0:1], 1.0 / (2 * P), EPS, ALU.mult, ALU.add))
                        if t >= 1:
                            pool.wait_ge(s_ofree, USE["C", t - 1]["ob"] + 1)
                        nc.gpsimd.tensor_tensor(st_q[:, 1, 0:1], st_q[:, 1, 1:2], power[:, 0:1], ALU.pow).then_inc(s_orstd, 1)
                    elif kind == "fin" and what == 1:
                        pool.wait_ge(s_ofree, use["ob"] + 1)
                        link(nc.gpsimd.tensor_scalar(M1[:, 0:32], M1[:, 0:32], 1.0 / (2 * P), EPS, ALU.mult, ALU.add))
                        nc.gpsimd.tensor_tensor(M1[:, 32:64], M1[:, 0:32], power[:, 0:32], ALU.pow).then_inc(s_finp, 1)
            pool.wait_ge(s_yr, 1)
            link(nc.gpsimd.tensor_scalar(y_sum[:, :], y_r[:, :], 1.0 / D_MODEL, EPS, ALU.mult, ALU.add))
            nc.gpsimd.tensor_tensor(y_r[:, :], y_sum[:, :], power[:, 0:5], ALU.pow).then_inc(s_yrp, 1)


_INS = ["x_prompt", "x_sample", "mem_prompt", "cache_k_diff", "cache_v_diff", "page_table", "cache_k_win", "cache_v_win",
        "cache_mem_k", "cache_mem_v", "g_norm", "w_in", "lambda_q1", "lambda_k1", "lambda_q2", "lambda_k2", "g_subln",
        "g_mem_norm", "w_mem_kv", "w_out", "g_final"]
_OUTS = [(1, SEQ, D_MODEL), (DB, 1, D_MODEL), (1, 1, SEQ, H, 2, P), (1, 1, SEQ, H, 2 * P), (1, 1, SEQ, H, P), (1, 1, SEQ, H, P),
         (1, 1, N_MEM, H, P), (1, 1, N_MEM, H, P), (1, DB, 1, H, 2, P), (1, DB, 1, H, 2 * P), (1, DB, 1, H, P), (1, DB, 1, H, P)]


def kernel(**inputs):
    import concourse.bacc as bacc
    from concourse.bass_utils import run_bass_kernel_spmd

    nc = bacc.Bacc("TRN2", target_bir_lowering=False, num_devices=1, dynamic_dma_scratch_size=1024)
    arrays, args = {}, []
    given = {name: np.ascontiguousarray(inputs[name]) for name in _INS}
    given["bias_tables"], given["bias_small"], given["identity"] = constants()
    for name, a in given.items():
        arrays[f"in_{name}_dram"] = a
        args.append(nc.dram_tensor(f"in_{name}_dram", a.shape, mybir.dt.from_np(a.dtype), kind="ExternalInput").ap())
    for i, shape in enumerate(_OUTS):
        args.append(nc.dram_tensor(f"out_{i}_dram", shape, F32, kind="ExternalOutput").ap())
    args.append(nc.dram_tensor("q_rows_dram", (KT * DB, P), F32, kind="Internal").ap())
    hybrid_decoder(nc, *args)
    r = run_bass_kernel_spmd(nc, [arrays], core_ids=[0])
    return tuple(r.results[0][f"out_{i}_dram"] for i in range(len(_OUTS)))
```

```python
import math
from contextlib import ExitStack

import numpy as np

import concourse.bass as bass
from concourse import mybir

F32 = mybir.dt.float32
F32R = mybir.dt.float32r
I32 = mybir.dt.int32
ALU = mybir.AluOpType
ACT = mybir.ActivationFunctionType
AX_X = mybir.AxisListType.X

P = 128
D_MODEL = 2048
KT = D_MODEL // P
SEQ = 512
NBLK = SEQ // P
DB = 8
TOK = SEQ + DB
HALF = TOK // 2
N_MEM = 256
H = 4
PAGES = 8
PAST = PAGES * P
SCALE = P ** -0.5
EPS = 1e-6
LAM_INIT = 0.8 - 0.6 * math.exp(-0.3 * 0)
MASKED = -1e30
LOWEST = -3e38

WIN_RING = 8
SPLIT_RING = 4
AHEAD = 3
FIRST_SPLITS = (0, 1, 2, 4, 6)
SOFT_AT = (0, 3, 5, 7, 8)
LATE_KEYS = (1, 2)
PAGE_RING = 6

COL = dict(qd=0, kd=1024, vd=2048, gd=3072, qw=4096, kw=4608, vw=5120, gw=5632, qm=6144, gm=6656)


def slopes():
    s = 2.0 ** (-8.0 * np.arange(1, 2 * H + 1) / (2 * H))
    return s[0::2], s[1::2]


def branch_count(dist):
    n = np.zeros(dist.shape)
    for window, r in ((128, 1), (512, 4), (2048, 16)):
        n += (dist >= 0) & (dist <= window) & (dist % r == 0)
    return n


def log_count(n):
    return np.where(n > 0, np.log(np.maximum(n, 1)), MASKED)


def constants():
    sd, sw = slopes()
    dist = 3 * P + np.arange(P)[:, None] - np.arange(SEQ)[None, :]
    out = np.zeros((2 * H, P, SEQ))
    for h in range(H):
        out[h] = np.where(dist >= 0, -sd[h] * dist, MASKED)
        out[H + h] = np.where(branch_count(dist) > 0, -sw[h] * dist + log_count(branch_count(dist)), MASKED)
    key = np.arange(P)
    bd = -(PAST - (np.arange(PAGES)[None, :, None] * P + key[:, None, None])) * sd[None, None, :]
    far = np.concatenate([PAST - np.arange(512, 896, 4), PAST - np.arange(0, 512, 16)])
    bw = np.zeros((P, 2, 2, H))
    for t, d in enumerate((PAST - (896 + key), far)):
        bw[:, t, 0] = -d[:, None] * sw[None, :] + log_count(branch_count(d))[:, None]
    small = np.concatenate([bd.reshape(P, -1), bw.reshape(P, -1)], axis=1)
    return ((out / SCALE).astype(np.float32), (small / SCALE).astype(np.float32), np.eye(P, dtype=np.float32))


TWICE = 3
Y_BLOCKS = ((0, 1, 2, 3, 4), (0, 1), (2, 3, 4))


def tiles():
    out = [("mk", j, 0) for j in range(H)] + [("mv", j, 0) for j in range(H)]
    out += [("qd", h, c) for h in range(H) for c in range(2)]
    for h in range(H):
        out += [(kind, h, c) for kind in ("kd", "vd", "gd") for c in range(2)]
    out += [("qm", j, 0) for j in range(H)] + [("qw", j, 0) for j in range(H)] + [("kw", j, 0) for j in range(H)]
    out += [(kind, j, 0) for j in range(H) for kind in ("vw", "gw")]
    out += [("gm", j, 0) for j in range(H)]
    out += [("y", e, 0) for e in range(KT - TWICE)]
    out += [("y", e, part) for part in (1, 2) for e in range(KT - TWICE, KT)]
    return out


TILES = tiles()
AT = {t: n for n, t in enumerate(TILES)}
N_TILES = len(TILES)
QUARTERS = 4 * N_TILES
FIRST_IN = AT["qd", 0, 0]
FIRST_OUT = AT["y", 0, 0]
IN_END = 4 * FIRST_OUT
N_PREP = KT // 2


SQUARES = ((2, 3), (3, 5), (6, 7), (4, 16), (5, 20))


def cat_slot(kind, h, c):
    return {"qd": 2 * h + c, "qw": 2 * H + h, "qm": 3 * H + h, "gm": 3 * H + h}[kind]


def att_steps():
    out = []
    for h in range(H):
        s0 = 4 * (AT["gd", h, 1] + 1) + 2
        period = 6 if h < H - 1 else 4
        out += [("diff", h, i, s0 + period * i) for i in range(NBLK)]
    s = out[-1][3] + 6
    for j in range(H):
        s = max(s, 4 * (AT["qm", j, 0] + 1) + 1)
        for pair in range(2):
            out.append(("mem", j, pair, s))
            s += 2
    s += 1
    for j in range(H):
        s = max(s, 4 * (AT["gw", j, 0] + 1) + 2)
        for i in range(NBLK):
            out.append(("dil", j, i, s))
            s += 2
    return out


STEPS = att_steps()


GROUPS = (0, 1, 3, 2)
G_TILES = (PAGES, PAGES, 2, 2)
WINDOW, MEMORY = 2, 3
ROWS = [(g, b) for g in GROUPS for b in range(DB)]
PAIRS = [(g, p) for g in GROUPS for p in range(DB // 2)]
NEW_BIAS = (0.0, 0.0, math.log(3.0) / SCALE, MASKED / SCALE)


def key_units(g):
    return [("dk", (g, b, t)) for b in range(DB) for t in range(G_TILES[g])]


def value_units(g, p):
    return [("dv", (g, 2 * p + j, t)) for t in range(G_TILES[g]) for j in range(2)]


def plan():
    n_slots = QUARTERS + 8
    slots = [[] for _ in range(n_slots)]
    load = [0.65] * n_slots
    span = [1.4 if s < 4 * FIRST_IN else 2.75 for s in range(n_slots)]

    def put(s, kind, what=None, cost=0.0, pe=0.0):
        slots[s].append((kind, what))
        load[s] += cost
        span[s] += pe

    for i, s in SQUARES:
        put(s, "squares", i)
        put(s + 1, "scale", i)
    for u in range(N_PREP):
        put(9 + 2 * u, "prep", (1, u), 0.7)
    put(25, "prep_sample", None, 0.7)
    for u in range(N_PREP):
        put(29 + u // 2, "prep", (2, u), 0.7)
    for n, (kind, h, c) in enumerate(TILES):
        s = 4 * n + 4
        put(s, "evac", n, 0.65 if kind in ("gd", "gw") else 1.3 if kind == "gm" else 0.0)
        if kind in ("mk", "mv", "kd", "kw", "vd", "vw"):
            put(s + 1, "nat", n)
        if kind == "y":
            put(s + 1, "ynat", n, 0.8)
            if (h, c) == (KT - 1, 1):
                put(s + 3, "mean", 0)
                put(s + 6, "norm", 0)
    put(4 * (AT["qd", 3, 1] + 1) + 1, "qrows", 0)
    put(4 * (AT["qm", 3, 0] + 1) + 1, "qrows", 1)
    put(4 * (AT["qw", 3, 0] + 1) + 1, "qrows", 2)
    put(4 * (AT["vw", 3, 0] + 1) + 3, "kvrows", 0)
    put(4 * (AT["vw", 3, 0] + 1) + 4, "kvrows", 1)
    for t, (kind, h, i, s) in enumerate(STEPS):
        w = (i + 1) * P
        put(s, "A", t, {"diff": 2.1e-3 * w + 0.3, "mem": 0.7, "dil": 1.04e-3 * w + 0.3}[kind],
            {"diff": 3.3e-3 * w, "mem": 0.86, "dil": 1.7e-3 * w}[kind])
        put(s + 1, "P", t, {"diff": 1.6e-3 * w + 0.3, "mem": 0.1, "dil": 0.1}[kind])
        s += (kind, i) == ("diff", NBLK - 1)
        put(s + 2, "B", t, 0.0, 0.11 * (i + 1))
        put(s + 3, "C", t, {"diff": 0.4, "mem": 0.35, "dil": 0.2}[kind], {"diff": 0.43 * (i + 1), "mem": 0.86, "dil": 0.22 * (i + 1)}[kind])
        if kind == "diff":
            put(s + 4, "D", t, 0.55, 0.22)
    new_key = {0: AT["kd", 1, 1], 1: AT["kd", 3, 1], WINDOW: AT["kw", 3, 0], MEMORY: 0}
    queries = {0: AT["qd", 3, 1], 1: AT["qd", 3, 1], WINDOW: AT["qw", 3, 0], MEMORY: AT["qm", 3, 0]}
    order = key_units(0) + [("soft", 0)] + key_units(1)
    values = [(0, p) for p in range(4)] + ["soft1"] + [(1, p) for p in range(4)]
    for item in values:
        order += [("soft", 1)] if item == "soft1" else value_units(*item) + [("do", item)]
    order_late = (key_units(MEMORY) + [("soft", MEMORY)], key_units(WINDOW) + [("soft", WINDOW)])
    tail = []
    for g in (MEMORY, WINDOW):
        for p in range(4):
            tail += value_units(g, p) + [("do", (g, p))]
    at = order.index(("do", (1, LATE_KEYS[0]))) + 1
    order[at:at] = order_late[0]
    at = order.index(("do", (1, LATE_KEYS[1]))) + 1
    order[at:at] = order_late[1]
    order += tail
    n_units = sum(kind in ("dk", "dv") for kind, _ in order)
    first, end = 4 * (AT["qd", 3, 1] + 1) + 4, 4 * AT["gm", 0, 0] + 2
    room = [max(0.3, 1.5 * span[s] - load[s]) for s in range(n_slots)]
    total = sum(room[first:end])
    s, passed, done = first, 0.0, 0
    summed, soft_end, keys_end = {}, {}, {}
    for kind, what in order:
        if kind == "soft":
            s0 = max(keys_end[what] + 3, 4 * (new_key[what] + 1) + 3, max(soft_end.values(), default=0) + 1)
            for k in range(5):
                put(s0 + SOFT_AT[k], "soft", (what, k), 0.6)
            soft_end[what] = s0 + SOFT_AT[4]
        elif kind == "do":
            g, p = what
            for j in range(2):
                summed[g, 2 * p + j] = s + j + (2 if g < WINDOW else 1)
                put(summed[g, 2 * p + j], "do", (g, 2 * p + j), 0.0, 0.45)
        else:
            g, b, t = what
            while s < end - 1 and passed + room[s] < done * total / n_units:
                passed += room[s]
                s += 1
            least = 4 * (queries[g] + 1) + 4 if kind == "dk" else soft_end[g] + 1
            if kind == "dv":
                i = PAIRS.index((g, b // 2))
                if i >= 2:
                    before_g, before_p = PAIRS[i - 2]
                    least = max(least, summed[before_g, 2 * before_p + b % 2])
            while s < least:
                passed += room[s]
                s += 1
            assert s < end, (kind, what, s)
            slots[s].append((kind, what))
            keys_end[g] = s
            done += 1
    fin0 = max(summed[WINDOW, DB - 1], 4 * (AT["gw", 3, 0] + 1) + 1)
    for k in range(3):
        put(fin0 + (0, 3, 5)[k], "fin", k, 0.8)
    assert summed[WINDOW, DB - 1] < 4 * AT["gm", 0, 0] + 4 and fin0 + 5 < IN_END - 4
    rank = {"evac": 0, "P": 1, "B": 2, "D": 3, "C": 4, "A": 5, "do": 7, "dk": 8, "dv": 8}
    used = {"tb": 0, "ob": 0, "sb": 0}
    bank = {"nat": "tb", "ynat": "tb", "qrows": "tb", "kvrows": "tb", "A": "sb", "B": "tb", "C": "ob", "D": "tb"}
    out = []
    for jobs in slots:
        row = []
        turns = any(kind in ("B", "D", "nat", "qrows", "kvrows") or (kind, what) == ("soft", 1) for kind, what in jobs)
        free = ["tb", "ob"] if turns else ["ob", "tb"]
        for kind, what in sorted(jobs, key=lambda j: rank.get(j[0], 6)):
            banks = bank.get(kind, "")
            if kind == "ynat" and TILES[what][2] != 1:
                banks = "tb ob"
            if kind == "soft":
                banks = ("", "tb", "ob", "ob", "")[what[1]]
            if kind == "fin":
                banks = "ob" if what == 1 else ""
            if kind == "do":
                banks = free[-1]
                free.reverse()
            use = {}
            for b in banks.split():
                use[b] = used[b]
                used[b] += 1
            row.append((kind, what, use))
        out.append(row)
    return out


PLAN = plan()
USE = {(kind, what): use for jobs in PLAN for kind, what, use in jobs}
SLOT = {(kind, what): s for s, jobs in enumerate(PLAN) for kind, what, _ in jobs}
LAST_STEP = {}
for _t, (_kind, _h, _i, _s) in enumerate(STEPS):
    LAST_STEP[_kind, _h] = _t
NAT_K = [n for n, t in enumerate(TILES) if t[0] in ("mk", "kd", "kw")]
NAT_V = [n for n, t in enumerate(TILES) if t[0] in ("mv", "vd", "vw")]



ORDER_OF = {0: 0, 1: 1, 2: 2, 3: 3, 6: 4, 4: 5, 5: 6}
KEPT_KINDS = ("qd", "qw", "qm", "kd", "kw", "vd", "vw", "gd", "gw")
KEPT = {}
for _tile in TILES:
    if _tile[0] in KEPT_KINDS:
        KEPT[_tile] = len(KEPT) + 1
TANHS = {n: i for i, n in enumerate(n for n, t in enumerate(TILES) if t[0][0] == "g")}
RECS, SCORES_READ = {}, {}
for _t, _step in enumerate(STEPS):
    if _step[0] != "diff":
        RECS[_t] = len(RECS)
    SCORES_READ[_t] = sum(x[0] != "mem" for x in STEPS[:_t + 1])


PER_TURN = 8
LOOPS = {4 * FIRST_IN + 8: 3, IN_END + 8: (KT - TWICE - 2) // 2}


def in_loop(s):
    return any(first <= s < first + PER_TURN * turns for first, turns in LOOPS.items())


YSQ, _n = {}, 0
for _i in range(FIRST_OUT, N_TILES):
    YSQ[_i] = _n
    _n += len(Y_BLOCKS[TILES[_i][2]])
YSQ[N_TILES] = _n

Q_ROWS = ((0, 8, 0), (12, 4, 1), (8, 4, 0))
Q_STORE = {0: 0, 1: 0, MEMORY: 1, WINDOW: 2}
UNITS = [(s, kind == "dv", what) for s, jobs in enumerate(PLAN) for kind, what, _ in jobs if kind in ("dk", "dv")]
UNIT_AT = {(value, unit): i for i, (_, value, unit) in enumerate(UNITS)}
LANDED = []
for _i, (_, _value, (_g, _b, _tile)) in enumerate(UNITS):
    _before = LANDED[_i - PAGE_RING] if _i >= PAGE_RING else 0
    LANDED.append(_before + (32 if (_g, _tile) == (WINDOW, 1) else 16))


def hybrid_decoder(nc, x_prompt, x_sample, mem_prompt, cache_k_diff, cache_v_diff, page_table, cache_k_win,
                   cache_v_win, cache_mem_k, cache_mem_v, g_norm, w_in, lambda_q1, lambda_k1, lambda_q2, lambda_k2,
                   g_subln, g_mem_norm, w_mem_kv, w_out, g_final, bias_tables, bias_small, identity,
                   y_prompt, y_sample, k_diff_prompt, v_diff_prompt, k_win_prompt, v_win_prompt, mem_k_prompt,
                   mem_v_prompt, k_diff_sample, v_diff_sample, k_win_sample, v_win_sample, q_rows_dram):
    with ExitStack() as ctx:
        def sb(name, shape, dt=F32):
            return ctx.enter_context(nc.sbuf_tensor(name, shape, dt))

        def sem(name):
            return ctx.enter_context(nc.semaphore(name))

        act_hi = sb("act_hi", [P, KT, TOK], F32R)
        act_lo = sb("act_lo", [P, KT, TOK], F32R)
        w_raw = sb("w_raw", [P, WIN_RING, 4 * P])
        w_hi = sb("w_hi", [P, SPLIT_RING, 4 * P], F32R)
        w_lo = sb("w_lo", [P, SPLIT_RING, 4 * P], F32R)
        cat = sb("cat", [P, KT * TOK])
        cat_t = cat[:, :].rearrange("p (k t) -> p k t", k=KT)
        nat = cat[:, 0:NBLK * D_MODEL].rearrange("p (t f) -> p t f", t=NBLK)
        kT = sb("kT", [P, 4 * TOK])
        kT_t = kT[:, :].rearrange("p (k t) -> p k t", k=4)
        gate = sb("gate", [P, 4 * TOK])
        gate_t = gate[:, :].rearrange("p (k t) -> p k t", k=4)
        v_nat = sb("v_nat", [P, 2, NBLK, 2 * P])
        k_nat = sb("k_nat", [P, NBLK, P])
        tall = sb("tall", [P, TOK])
        mk_T = sb("mk_T", [P, H, N_MEM])
        mv_nat = sb("mv_nat", [P, 2, H * P])
        bias = sb("bias", [P, 2, SEQ])
        probs = sb("probs", [P, 2, SEQ])
        probs_T = sb("probs_T", [P, SEQ])
        o_nat = sb("o_nat", [P, 2 * P])
        pages = sb("pages", [P, PAGE_RING, 512])
        q_bc = sb("q_bc", [P, 2, 512])
        v_acc = sb("v_acc", [P, 4, 512])
        dec_s = sb("dec_s", [P, 512])
        dec_a = sb("dec_a", [P, PAGES, DB * H])
        ident = sb("ident", [P, P])
        ones = sb("ones", [P, P])
        b_small = sb("b_small", [P, PAGES * H + 4 * H])
        rows = sb("rows", [P, 2, P])
        q_s = sb("q_s", [P, KT, DB])
        k_s = sb("k_s", [P, 12, DB])
        v_s = sb("v_s", [P, 12, DB])
        g_s = sb("g_s", [P, 12, DB])
        o_s = sb("o_s", [P, 16, DB])
        gn = sb("gn", [P, KT])
        gmn = sb("gmn", [P, KT])
        gsub = sb("gsub", [P, 2])
        gsub_c = sb("gsub_c", [P, 2])
        lam_in = sb("lam_in", [P, 4])
        lam_w = sb("lam_w", [P, 8])
        power = sb("power", [P, 32])
        ids = sb("ids", [1, DB * PAGES], I32)
        tok_ss = sb("tok_ss", [P, 8])
        tok_r = sb("tok_r", [P, 8])
        tok_s = sb("tok_s", [P, KT, DB])
        a_new = sb("a_new", [P, 2, DB * H])
        tmp = sb("tmp", [P, H, DB])
        y_ss = sb("y_ss", [P, 5, KT])
        y_sum = sb("y_sum", [P, 5])
        y_r = sb("y_r", [P, 5])
        st_m = sb("st_m", [P, 2, 2])
        st_n = sb("st_n", [P, 2, 2])
        st_l = sb("st_l", [P, 2, 2])
        st_r = sb("st_r", [P, 2, 3])
        st_q = sb("st_q", [P, 2, 2])
        dc = sb("dc", [P, 8, 64])
        z = [ctx.enter_context(nc.psum_tensor(f"z{i}", [P, 2, 512], F32)) for i in range(2)]
        s_ps = ctx.enter_context(nc.psum_tensor("s_ps", [P, 2, 512], F32))
        t_ps = ctx.enter_context(nc.psum_tensor("t_ps", [P, 512], F32))
        o_ps = ctx.enter_context(nc.psum_tensor("o_ps", [P, 512], F32))

        s_const = sem("const_loaded")
        s_ident = sem("identity_loaded")
        s_gm = sem("g_mem_loaded")
        s_tok = [sem(f"tokens_loaded{i}") for i in range(7)]
        s_ss = sem("token_squares")
        s_rr = sem("token_rstd")
        s_scaled = sem("tokens_scaled")
        s_pfull = sem("prep_full")
        s_phi = sem("prep_hi")
        s_plo = sem("prep_lo")
        s_raw = [sem(f"weights_loaded{i}") for i in range(WIN_RING)]
        s_hi = sem("weights_hi")
        s_lo = sem("weights_lo")
        s_quarter = sem("quarter_multiplied")
        s_zfree = [sem("z0_free"), sem("z1_free")]
        s_tanh = sem("gate_tanh")
        s_bias = [sem("bias_loaded0"), sem("bias_loaded1")]
        s_sfull, s_sfree = sem("scores_full"), sem("scores_free")
        s_tfull, s_tfree = sem("turned_full"), sem("turned_free")
        s_ofull, s_ofree = sem("out_full"), sem("out_free")
        s_max, s_exp, s_rec, s_probs = sem("row_max"), sem("probs_exp"), sem("probs_rec"), sem("probs_ready")
        s_osq, s_orstd = sem("o_squares"), sem("o_rstd")
        s_kout, s_vout = sem("k_stored"), [sem("v_stored0"), sem("v_stored1")]
        s_mvout = sem("mv_stored")
        s_keep = sem("sample_columns_kept")
        s_lam, s_lamp, s_lame = sem("lambda_products"), sem("lambda_sums"), sem("lambda_exp")
        s_neglam = sem("lambda_ready")
        s_init = sem("constants_set")
        s_qdram = [sem(f"q_rows_stored{i}") for i in range(3)]
        s_kvout = [sem("k_rows_stored"), sem("v_rows_stored")]
        s_qbc = [sem("q_bc_loaded0"), sem("q_bc_loaded1")]
        s_page = [sem(f"page_loaded{i}") for i in range(PAGE_RING)]
        s_unit = sem("unit_done")
        s_dsm, s_dexp = sem("decode_softmax_dve"), sem("decode_exp")
        s_dprod = sem("new_key_products")
        s_fin, s_finp = sem("decode_out_dve"), sem("decode_out_rstd")
        s_gated = sem("memory_gated")
        s_chi, s_clo = sem("cat_hi"), sem("cat_lo")
        s_res = [sem(f"residual_loaded{i}") for i in range(5)]
        s_gf = sem("g_final_loaded")
        s_ysq = sem("y_squares")
        s_yg = sem("y_times_g")
        s_yr, s_yrp = sem("y_mean"), sem("y_rstd")
        s_ydone = [sem(f"y_done{i}") for i in range(5)]
        s_yout = sem("y_stored")
        s_chain = sem("vector_chain")
        s_pchain = sem("pool_chain")
        s_achain = sem("scalar_chain")

        x_t = x_prompt.rearrange("a (t p) f -> (a t) p f", p=P)
        m_t = mem_prompt.rearrange("a (t p) f -> (a t) p f", p=P)
        xs = x_sample.rearrange("b a f -> (b a) f")
        w_dram = {"m": w_mem_kv, "i": w_in, "o": w_out}
        w_view = {k: v.rearrange("a (r k p) f -> (a r) p k f", r=4, p=P) for k, v in w_dram.items()}
        kpages = cache_k_diff.rearrange("a n p h c d -> (a n) p (h c d)")
        vpages = cache_v_diff.rearrange("a n p h d -> (a n) p (h d)")
        kwin = cache_k_win.rearrange("a b w h d -> (a b) w (h d)")
        vwin = cache_v_win.rearrange("a b w h d -> (a b) w (h d)")
        kmem = cache_mem_k.rearrange("a b w h d -> (a b) w (h d)")
        vmem = cache_mem_v.rearrange("a b w h d -> (a b) w (h d)")
        out_nat = {
            "kd": k_diff_prompt.rearrange("a b (t p) h c d -> p (a b t) (h c d)", p=P),
            "vd": v_diff_prompt.rearrange("a b (t p) h d -> p (a b t) (h d)", p=P),
            "kw": k_win_prompt.rearrange("a b (t p) h d -> p (a b t) (h d)", p=P),
            "vw": v_win_prompt.rearrange("a b (t p) h d -> p (a b t) (h d)", p=P),
            "mk": mem_k_prompt.rearrange("a b (t p) h d -> p (a b t) (h d)", p=P),
            "mv": mem_v_prompt.rearrange("a b (t p) h d -> p (a b t) (h d)", p=P),
        }
        out_rows = [
            [(k_diff_sample.rearrange("a b s h c d -> (a b s) (h c d)"), 8), (k_win_sample.rearrange("a b s h d -> (a b s) (h d)"), 4)],
            [(v_diff_sample.rearrange("a b s h d -> (a b s) (h d)"), 8), (v_win_sample.rearrange("a b s h d -> (a b s) (h d)"), 4)],
        ]
        x_s_nat = kT[0:DB, 0:D_MODEL]
        y_s_nat = gate[0:DB, 0:D_MODEL]
        g_fin = pages[:, 0:4, :].rearrange("p a b -> p (a b)")
        bd = b_small[:, 0:PAGES * H].rearrange("p (t h) -> p t h", h=H)
        bw = b_small[:, PAGES * H:].rearrange("p (t c h) -> p t c h", c=2, h=H)
        SAMPLE = slice(SEQ, TOK)
        PROD, SNEW, MB, M1, L1, LR, DIAG, SQ = (dc[:, i, :] for i in range(8))

        def scores_of(g):
            if g < WINDOW:
                return dec_s[:, :].rearrange("p (t n) -> p t n", n=64)[:, :, 32 * g:32 * g + 32]
            first = 2 * (g - WINDOW)
            return dec_s[:, :].rearrange("p (t n) -> p t n", n=64)[:, first:first + 2, 0:32]

        def key_slot(kind, h, c):
            return 2 * (h % 2) + c if kind == "kd" else h

        def gate_slot(kind, h, c):
            return {"gd": 2 * (h % 2) + c, "gw": 2 * (h % 2), "gm": 2 * (h % 2) + 1}[kind]

        def sample_slot(kind, h, c):
            return 2 * h + c if kind[1] == "d" else 8 + h

        def quarter_source(q, turn):
            n, r = divmod(q, 4)
            kind, h, c = TILES[n]
            if n < FIRST_IN:
                matrix, col = "m", (h + (H if kind == "mv" else 0)) * P
            elif n < FIRST_OUT:
                matrix, col = "i", COL[kind] + (2 * h + c if kind[1] == "d" else h) * P
            else:
                matrix, col = "o", h * P
            return w_view[matrix][r, :, :, bass.ds(col + 2 * P * turn, P)]

        def turned_bank(what):
            use = USE["do", what]
            if "tb" in use:
                return t_ps, s_tfull, s_tfree, use["tb"]
            return o_ps, s_ofull, s_ofree, use["ob"]

        def bias_index(kind, h):
            return h if kind == "diff" else H + h

        block = ctx.enter_context(nc.Block())

        @block.sync
        def _(sp):
            def weights(q, turn=0):
                if q >= WIN_RING:
                    sp.wait_ge(s_lo, q - WIN_RING + 1 + PER_TURN * turn)
                dst = w_raw[:, q % WIN_RING, :].rearrange("p (k f) -> p k f", k=4)
                sp.dma_start(dst, quarter_source(q, turn)).then_inc(s_raw[q % WIN_RING], 16)

            def bias_table(i):
                if i >= 2:
                    prev = ("diff", i - 2) if i - 2 < H else ("dil", i - 2 - H)
                    sp.wait_ge(s_sfree, SCORES_READ[LAST_STEP[prev]])
                sp.dma_start(bias[:, i % 2, :], bias_tables[i]).then_inc(s_bias[i % 2], 16)

            def q_broadcast(i):
                if i >= 2:
                    before_g, before_b = ROWS[i - 2]
                    sp.wait_ge(s_unit, UNIT_AT[False, (before_g, before_b, G_TILES[before_g] - 1)] + 1)
                g, b = ROWS[i]
                sp.wait_ge(s_qdram[Q_STORE[g]], 16)
                src = q_rows_dram.rearrange("(t b) d -> b t d", b=DB)[b:b + 1, 4 * g:4 * g + 4, :]
                dst = q_bc[:, i % 2, :].rearrange("p (t d) -> p t d", t=4)
                sp.dma_start(dst, src.broadcast_to((P, 4, P))).then_inc(s_qbc[i % 2], 16)

            def cache_unit(seq, value, g, b, t):
                slot = seq % PAGE_RING
                if seq >= PAGE_RING:
                    sp.wait_ge(s_unit, seq - PAGE_RING + 1)
                dst = pages[:, slot, :]
                if g < WINDOW:
                    page = sp.value_load(ids[0:1, b * PAGES + t:b * PAGES + t + 1], min_val=0, max_val=kpages.shape[0] - 1)
                    src = (vpages if value else kpages)[bass.ds(page, 1), :, g * 512:(g + 1) * 512]
                    sp.dma_start(dst, src.rearrange("a p f -> (a p) f")).then_inc(s_page[slot], 16)
                elif g == MEMORY:
                    src = (vmem if value else kmem)[b, t * P:(t + 1) * P, :]
                    sp.dma_start(dst, src).then_inc(s_page[slot], 16)
                elif t == 0:
                    src = (vwin if value else kwin)[b, PAST - P:PAST, :]
                    sp.dma_start(dst, src).then_inc(s_page[slot], 16)
                else:
                    cache = vwin if value else kwin
                    n4 = 96
                    near = cache[b, 512:896, :].rearrange("(k r) f -> k r f", r=4)[:, 0, :]
                    far = cache[b, 0:512, :].rearrange("(k r) f -> k r f", r=16)[:, 0, :]
                    sp.dma_start(dst[0:n4, :], near).then_inc(s_page[slot], 16)
                    sp.dma_start(dst[n4:P, :], far).then_inc(s_page[slot], 16)

            def store_y(i):
                sp.wait_ge(s_ydone[i], 1)
                sp.dma_start(y_prompt.rearrange("a (t p) f -> (a t) p f", p=P)[i], nat[:, i, :]).then_inc(s_yout, 16)

            sp.dma_start(nat[:, 0, :], m_t[0]).then_inc(s_tok[0], 16)
            sp.dma_start(nat[:, 1, :], m_t[1]).then_inc(s_tok[1], 16)
            sp.dma_start(ident[:, :], identity).then_inc(s_ident, 16)
            sp.dma_start(gmn[:, :], g_mem_norm.rearrange("a (k p) -> p (a k)", p=P),
                         allow_slow_non_contiguous=True).then_inc(s_gm, 16)
            for q in range(2):
                weights(q)
            sp.dma_start(b_small[:, :], bias_small).then_inc(s_const, 16)
            sp.dma_start(gn[:, :], g_norm.rearrange("a (k p) -> p (a k)", p=P),
                         allow_slow_non_contiguous=True).then_inc(s_const, 16)
            sp.dma_start(gsub[:, :], g_subln.rearrange("a (k p) -> p (a k)", p=P),
                         allow_slow_non_contiguous=True).then_inc(s_const, 16)
            for i, v in enumerate((lambda_q1, lambda_k1, lambda_q2, lambda_k2)):
                sp.dma_start(lam_in[:, i:i + 1], v.rearrange("a p -> p a"),
                             allow_slow_non_contiguous=True).then_inc(s_const, 16)
            sp.dma_start(ids[:, :], page_table.rearrange("(a b) n -> a (b n)", a=1)).then_inc(s_const, 16)
            for q in range(2, 4):
                weights(q)
            for q in range(4, WIN_RING - 1):
                weights(q)
            for i in range(2, 4):
                sp.dma_start(nat[:, i, :], x_t[i]).then_inc(s_tok[i], 16)
            sp.dma_start(x_s_nat, xs).then_inc(s_tok[6], 16)
            sp.wait_ge(s_const, 16 * 8)

            order = UNITS
            sent = 0
            q_sent = 0
            def slot(s, jobs, turn=0):
                nonlocal sent, q_sent
                if WIN_RING - 1 + s < QUARTERS:
                    weights(WIN_RING - 1 + s, turn)
                if s in (5, 8):
                    i = (5, 8).index(s)
                    sp.wait_ge(s_pfull, N_PREP)
                    sp.dma_start(nat[:, i, :], x_t[i]).then_inc(s_tok[4 + i], 16)
                if s in (30, 31):
                    bias_table(s - 30)
                while sent < len(order) and order[sent][0] <= s + 3 and sent < PAGE_RING + sum(
                        1 for o in order[:sent + 1] if o[0] < s):
                    _, value, (g, b, t) = order[sent]
                    if not value:
                        if SLOT["qrows", Q_STORE[g]] >= s - 1:
                            break
                        while q_sent < ROWS.index((g, b)) + 1:
                            q_broadcast(q_sent)
                            q_sent += 1
                    cache_unit(sent, value, g, b, t)
                    sent += 1
                for i in range(2, 2 * H):
                    prev = ("diff", i - 2) if i - 2 < H else ("dil", i - 2 - H)
                    if SLOT["A", LAST_STEP[prev]] + 1 == s:
                        bias_table(i)
                for kind, what, use in (PLAN[s - 1] if s else []):
                    if kind == "nat":
                        tile_kind, h, c = TILES[what]
                        j = 2 * h + c if tile_kind[1] == "d" else h
                        dst = out_nat[tile_kind][:, :, j * P:(j + 1) * P]
                        if tile_kind in ("mk", "kd", "kw"):
                            sp.wait_ge(s_tfree, use["tb"] + 1)
                            nb = 2 if tile_kind == "mk" else NBLK
                            sp.dma_start(dst, k_nat[:, 0:nb, :]).then_inc(s_kout, 16)
                        elif tile_kind == "mv":
                            sp.wait_ge(s_tfree, use["tb"] + 1)
                            sp.dma_start(dst, mv_nat[:, :, j * P:(j + 1) * P]).then_inc(s_mvout, 16)
                        else:
                            sp.wait_ge(s_tfree, use["tb"] + 1)
                            sp.dma_start(dst, v_nat[:, h % 2, :, c * P:(c + 1) * P]).then_inc(s_vout[h % 2], 16)
                    if kind == "qrows":
                        sp.wait_ge(s_tfree, use["tb"] + 1)
                        first, count, place = Q_ROWS[what]
                        sp.dma_start(q_rows_dram[first * DB:(first + count) * DB, :],
                                     rows[0:count * DB, place, :]).then_inc(s_qdram[what], 16)
                    if kind == "norm":
                        store_y(0)
                        store_y(1)
                    if kind == "kvrows":
                        sp.wait_ge(s_tfree, use["tb"] + 1)
                        row = 0
                        for dst, nt in out_rows[what]:
                            for t in range(nt):
                                sp.dma_start(dst[:, t * P:(t + 1) * P], rows[row:row + DB, what, :]).then_inc(s_kvout[what], 16)
                                row += DB
                if IN_END - 2 <= s <= IN_END + 1:
                    i = s - (IN_END - 2)
                    sp.wait_ge(s_clo, 4 * i + 4)
                    sp.dma_start(nat[:, i, :], x_t[i]).then_inc(s_res[i], 16)
                if s == IN_END + 2:
                    sp.dma_start(y_s_nat, xs).then_inc(s_res[4], 16)
                    sp.wait_ge(s_unit, len(order))
                    sp.dma_start(g_fin, g_final.rearrange("(a f) -> a f", a=1).broadcast_to((P, D_MODEL))).then_inc(s_gf, 16)
            for s, jobs in enumerate(PLAN):
                if s in LOOPS:
                    with sp.Fori(0, LOOPS[s]) as turn:
                        for k in range(PER_TURN):
                            slot(s + k, PLAN[s + k], turn)
                elif not in_loop(s):
                    slot(s, jobs)
            assert sent == len(order)
            for i in (2, 3):
                store_y(i)
            sp.wait_ge(s_ydone[4], 1)
            sp.dma_start(y_sample.rearrange("b a f -> (b a) f"), y_s_nat).then_inc(s_yout, 16)
            sp.wait_ge(s_yout, 16 * 5)
            sp.wait_ge(s_kout, 16 * len(NAT_K))
            sp.wait_ge(s_mvout, 16 * H)
            for i in range(2):
                sp.wait_ge(s_vout[i], 16 * (4 + 2))
                sp.wait_ge(s_kvout[i], 16 * 12)
            for i in range(3):
                sp.wait_ge(s_qdram[i], 16)

        def prep_base(pair):
            return {0: 0, 1: N_PREP, 2: 2 * N_PREP + 1}[pair]

        @block.tensor
        def _(pe):
            def prep(pair, u):
                use = prep_base(pair) + u
                pe.wait_ge(s_scaled, (2, 4, 7)[pair])
                if use >= 2:
                    pe.wait_ge(s_plo, use - 1)
                first = 2 if pair == 1 else 0
                for k in range(2):
                    for t in range(2):
                        kt = 2 * u + k
                        last = nc.tensor.transpose(s_ps[:, use % 2, (2 * k + t) * P:(2 * k + t + 1) * P],
                                                   nat[:, first + t, kt * P:(kt + 1) * P], ident[:, :])
                last.then_inc(s_pfull, 1)

            def prep_sample():
                use = 2 * N_PREP
                pe.wait_ge(s_scaled, 5)
                pe.wait_ge(s_plo, use - 1)
                for kt in range(KT):
                    last = nc.tensor.transpose(s_ps[:, use % 2, kt * DB:(kt + 1) * DB],
                                               x_s_nat[:, kt * P:(kt + 1) * P], ident[0:DB, 0:DB])
                last.then_inc(s_pfull, 1)

            def quarter(q, turn=0):
                n, r = divmod(q, 4)
                zb = z[n % 2]
                if r == 0 and n >= 2:
                    pe.wait_ge(s_zfree[n % 2], n // 2 + turn)
                pe.wait_ge(s_lo, q + 1 + PER_TURN * turn)
                if n == FIRST_IN:
                    pe.wait_ge(s_plo, prep_base(2) + 2 * r + 2)
                if n == 0:
                    pe.wait_ge(s_plo, 2 * r + 2)
                if n == FIRST_OUT:
                    pe.wait_ge(s_clo, 4 * r + 4)
                hi, lo = w_hi[:, q % SPLIT_RING, :], w_lo[:, q % SPLIT_RING, :]
                parts = [(0, 0, N_MEM)] if n < FIRST_IN else [(0, 0, HALF), (1, HALF, TOK)]
                if n >= FIRST_OUT and TILES[n][2]:
                    parts = [(0, 0, 2 * P)] if TILES[n][2] == 1 else [(1, 2 * P, TOK)]
                for j in range(4):
                    kt = 4 * r + j
                    w = slice(j * P, (j + 1) * P)
                    for m, (lhs, rhs) in enumerate(((hi, act_hi), (hi, act_lo), (lo, act_hi))):
                        for bank, a, b in parts:
                            last = nc.tensor.matmul(zb[:, bank, 0:b - a], lhs[:, w], rhs[:, kt, a:b],
                                                    start=(kt == 0 and m == 0), stop=(kt == KT - 1 and m == 2))
                last.then_inc(s_quarter, 1)

            def turn_ready(use, turn=0):
                if use["tb"] >= 1:
                    pe.wait_ge(s_tfree, use["tb"] + 2 * turn)

            def out_ready(use, turn=0):
                if use["ob"] >= 1:
                    pe.wait_ge(s_ofree, use["ob"] + 2 * turn)

            def natural(n, use, turn):
                kind, h, c = TILES[n]
                pe.wait_ge(s_zfree[n % 2], n // 2 + 1 + turn)
                turn_ready(use, turn)
                src = {"mk": lambda: mk_T[:, h, :], "kd": lambda: kT_t[:, key_slot(kind, h, c), :],
                       "kw": lambda: kT_t[:, key_slot(kind, h, c), :]}.get(kind, lambda: tall[:, :])()
                blocks = range(2) if kind[0] == "m" else range(NBLK)
                if kind == "y":
                    blocks = [b for b in Y_BLOCKS[c] if b < NBLK]
                for b in blocks:
                    last = nc.tensor.transpose(t_ps[:, b * P:(b + 1) * P], src[:, b * P:(b + 1) * P], ident[:, :])
                if kind == "y" and c != 1:
                    last.then_inc(s_tfull, 1)
                    out_ready(use, turn)
                    last = nc.tensor.transpose(o_ps[0:DB, 0:P], src[:, SAMPLE], ident[:, :])
                    last.then_inc(s_ofull, 1)
                else:
                    last.then_inc(s_tfull, 1)

            def step_scores(t, use):
                kind, h, i, _ = STEPS[t]
                if t and STEPS[t - 1][0] == "mem":
                    pe.wait_ge(s_exp, t)
                elif t:
                    pe.wait_ge(s_sfree, SCORES_READ[t - 1])
                if kind == "diff":
                    n = AT["kd", h, 1]
                    pe.wait_ge(s_zfree[n % 2], n // 2 + 1)
                    for c in range(2):
                        last = nc.tensor.matmul(s_ps[:, c, 0:(i + 1) * P], cat_t[:, 2 * h + c, i * P:(i + 1) * P],
                                                kT_t[:, key_slot("kd", h, c), 0:(i + 1) * P], start=True, stop=True)
                elif kind == "dil":
                    n = AT["kw", h, 0]
                    pe.wait_ge(s_zfree[n % 2], n // 2 + 1)
                    last = nc.tensor.matmul(s_ps[:, 0, 0:(i + 1) * P], cat_t[:, 2 * H + h, i * P:(i + 1) * P],
                                            kT_t[:, key_slot("kw", h, 0), 0:(i + 1) * P], start=True, stop=True)
                else:
                    n = AT["qm", h, 0]
                    pe.wait_ge(s_zfree[n % 2], n // 2 + 1)
                    for c in range(2):
                        b = 2 * i + c
                        last = nc.tensor.matmul(s_ps[:, c, 0:N_MEM], cat_t[:, 3 * H + h, b * P:(b + 1) * P],
                                                mk_T[:, h, :], start=True, stop=True)
                last.then_inc(s_sfull, 1)

            def step_turn(t, use):
                kind, h, i, _ = STEPS[t]
                pe.wait_ge(s_probs, t + 1)
                turn_ready(use)
                if kind == "mem":
                    for kb in range(2):
                        for c in range(2):
                            k = 2 * kb + c
                            last = nc.tensor.transpose(t_ps[:, k * P:(k + 1) * P], probs[:, c, kb * P:(kb + 1) * P], ident[:, :])
                else:
                    for kb in range(i + 1):
                        last = nc.tensor.transpose(t_ps[:, kb * P:(kb + 1) * P], probs[:, 0, kb * P:(kb + 1) * P], ident[:, :])
                last.then_inc(s_tfull, 1)

            def step_values(t, use):
                kind, h, i, _ = STEPS[t]
                pe.wait_ge(s_tfree, USE["B", t]["tb"] + 1)
                out_ready(use)
                if kind == "diff":
                    pe.wait_ge(s_tfree, USE["nat", AT["vd", h, 1]]["tb"] + 1)
                    for kb in range(i + 1):
                        last = nc.tensor.matmul(o_ps[:, 0:2 * P], probs_T[:, kb * P:(kb + 1) * P],
                                                v_nat[:, h % 2, kb, :], start=(kb == 0), stop=(kb == i))
                elif kind == "dil":
                    pe.wait_ge(s_tfree, USE["nat", AT["vw", h, 0]]["tb"] + 1)
                    for kb in range(i + 1):
                        last = nc.tensor.matmul(o_ps[:, 0:P], v_nat[:, h % 2, kb, 0:P],
                                                probs_T[:, kb * P:(kb + 1) * P], start=(kb == 0), stop=(kb == i))
                else:
                    for kb in range(2):
                        last = nc.tensor.matmul(o_ps[:, 0:2 * P], mv_nat[:, kb, h * P:(h + 1) * P],
                                                probs_T[:, kb * 2 * P:(kb + 1) * 2 * P], start=(kb == 0), stop=(kb == 1))
                last.then_inc(s_ofull, 1)

            def step_turn_out(t, use):
                pe.wait_ge(s_ofree, USE["C", t]["ob"] + 1)
                turn_ready(use)
                for c in range(2):
                    last = nc.tensor.transpose(t_ps[:, c * P:(c + 1) * P], o_nat[:, c * P:(c + 1) * P], ident[:, :])
                last.then_inc(s_tfull, 1)

            def sample_rows(src, count, use):
                turn_ready(use)
                nc.tensor.transpose(t_ps[0:count, 0:P], src, ident[:, :]).then_inc(s_tfull, 1)

            def soft(g, k, use):
                n = GROUPS.index(g)
                if k == 1:
                    pe.wait_ge(s_dsm, 5 * n + 1)
                    turn_ready(use)
                    nc.tensor.transpose(t_ps[0:32, 0:P], M1[:, 0:32], ident[:, :]).then_inc(s_tfull, 1)
                if k == 2:
                    pe.wait_ge(s_dsm, 5 * n + 2)
                    pe.wait_ge(s_dprod, n + 1)
                    out_ready(use)
                    nc.tensor.matmul(o_ps[:, 0:32], ones[0:32, :], DIAG[0:32, 0:32], start=True, stop=True)
                    nc.tensor.matmul(o_ps[:, 32:64], ones[:, :], PROD[:, 0:32], start=True, stop=True).then_inc(s_ofull, 1)
                if k == 3:
                    pe.wait_ge(s_dsm, 5 * n + 5)
                    out_ready(use)
                    nc.tensor.matmul(o_ps[:, 0:32], ones[:, :], L1[:, 0:32], start=True, stop=True).then_inc(s_ofull, 1)

            def turn_values(g, b):
                i = PAIRS.index((g, b // 2))
                pe.wait_ge(s_unit, UNIT_AT[True, (g, b, G_TILES[g] - 1)] + 1)
                bank, full, free, n = turned_bank((g, b))
                if n:
                    pe.wait_ge(free, n)
                for k in range(4):
                    last = nc.tensor.transpose(bank[:, k * P:(k + 1) * P], v_acc[:, 2 * (i % 2) + b % 2, k * P:(k + 1) * P], ident[:, :])
                last.then_inc(full, 1)

            pe.wait_ge(s_ident, 16)
            for u in range(4):
                prep(0, u)
            quarter(0)
            prep(0, 4)
            prep(0, 5)
            quarter(1)
            prep(0, 6)
            prep(0, 7)
            pe.wait_ge(s_lam, 1)
            nc.tensor.matmul(z[1][:, 0, 0:2], ones[:, :], lam_w[:, 0:2], start=True, stop=True).then_inc(s_lamp, 1)
            def slot(s, jobs, turn=0):
                if 2 <= s < QUARTERS:
                    if s == 4:
                        pe.wait_ge(s_lame, 1)
                    quarter(s, turn)
                for kind, what, use in jobs:
                    if kind == "prep":
                        prep(*what)
                    elif kind == "prep_sample":
                        prep_sample()
                    elif kind in ("nat", "ynat"):
                        natural(what, use, turn)
                    elif kind == "A":
                        step_scores(what, use)
                    elif kind == "B":
                        step_turn(what, use)
                    elif kind == "C":
                        step_values(what, use)
                    elif kind == "D":
                        step_turn_out(what, use)
                    elif kind == "qrows":
                        first, count, _ = Q_ROWS[what]
                        pe.wait_ge(s_keep, (KEPT["qd", 3, 1], KEPT["qm", 3, 0], KEPT["qw", 3, 0])[what])
                        sample_rows(q_s[:, first:first + count, :].rearrange("p t b -> p (t b)"), count * DB, use)
                    elif kind == "kvrows":
                        pe.wait_ge(s_keep, KEPT["vw", 3, 0])
                        sample_rows((v_s if what else k_s)[:, :, :].rearrange("p t b -> p (t b)"), 96, use)
                    elif kind == "soft":
                        soft(*what, use)
                    elif kind == "do":
                        turn_values(*what)
                    elif kind == "fin" and what == 1:
                        pe.wait_ge(s_fin, 1)
                        out_ready(use)
                        nc.tensor.matmul(o_ps[:, 0:64], ones[:, :], SQ, start=True, stop=True).then_inc(s_ofull, 1)
            for s, jobs in enumerate(PLAN):
                if s in LOOPS:
                    with pe.Fori(0, LOOPS[s]) as turn:
                        for k in range(PER_TURN):
                            slot(s + k, PLAN[s + k], turn)
                elif not in_loop(s):
                    slot(s, jobs)

        @block.scalar
        def _(act):
            chain = [0]

            def link(ins):
                chain[0] += 1
                ins.then_inc(s_achain, 1)
                act.wait_ge(s_achain, chain[0])

            def squares(i):
                n = DB if i == 6 else P
                src = x_s_nat if i == 6 else nat[:, i % 4, :]
                act.wait_ge(s_tok[i], 16)
                if i >= 1:
                    act.wait_ge(s_ss, ORDER_OF[i])
                nc.scalar.activation(gate[0:n, 0:D_MODEL], src, ACT.Square, accum_out=tok_ss[0:n, i:i + 1]).then_inc(s_ss, 1)

            def prep_hi(pair, u):
                use = prep_base(pair) + u
                g = gmn if pair == 0 else gn
                act.wait_ge(s_pfull, use + 1)
                if pair == 2:
                    act.wait_ge(s_quarter, 4 * FIRST_IN - 3 + u // 2)
                first = N_MEM if pair == 1 else 0
                for k in range(2):
                    kt = 2 * u + k
                    last = nc.scalar.activation(act_hi[:, kt, first:first + 2 * P], s_ps[:, use % 2, k * 2 * P:(k + 1) * 2 * P],
                                                ACT.Identity, scale=g[:, kt:kt + 1])
                last.then_inc(s_phi, 1)

            def split_hi(q, turn=0):
                act.wait_ge(s_raw[q % WIN_RING], 16 * (q // WIN_RING + 1 + turn))
                if q >= SPLIT_RING:
                    act.wait_ge(s_quarter, q - SPLIT_RING + 1 + PER_TURN * turn)
                nc.scalar.activation(w_hi[:, q % SPLIT_RING, :], w_raw[:, q % WIN_RING, :], ACT.Copy).then_inc(s_hi, 1)

            def evac(n, turn):
                kind, h, c = TILES[n]
                act.wait_ge(s_quarter, 4 * n + 4 + PER_TURN * turn)
                free = s_zfree[n % 2]
                zz = z[n % 2][:, :, 0:HALF]
                two = lambda ap: ap.rearrange("p (a t) -> p a t", a=2)
                if kind == "mk":
                    nc.scalar.activation(mk_T[:, h, :], z[n % 2][:, 0, 0:N_MEM], ACT.Copy).then_inc(free, 1)
                elif kind == "mv":
                    if h >= 1:
                        act.wait_ge(s_tfull, USE["nat", n - 1]["tb"] + 1)
                    nc.scalar.activation(tall[:, 0:N_MEM], z[n % 2][:, 0, 0:N_MEM], ACT.Copy).then_inc(free, 1)
                elif kind[0] == "q":
                    if n == FIRST_IN:
                        act.wait_ge(s_pfull, 3 * N_PREP + 1)
                    dst = cat[:, bass.ds(cat_slot(kind, h, c) * TOK + 2 * TOK * turn, TOK)]
                    nc.scalar.activation(two(dst), zz, ACT.Copy).then_inc(free, 1)
                elif kind[0] == "k":
                    if kind == "kd" and h >= 2:
                        act.wait_ge(s_sfull, USE["A", LAST_STEP["diff", h - 2]]["sb"] + 1)
                    if kind == "kw":
                        act.wait_ge(s_sfull, USE["A", LAST_STEP["diff", 2 + h // 2]]["sb"] + 1)
                    if kind != "kd" or h >= 2:
                        act.wait_ge(s_keep, KEPT["gd", 3, 1] if kind == "kw" else KEPT["gd", h - 1, 1])
                    nc.scalar.activation(two(kT_t[:, key_slot(kind, h, c), :]), zz, ACT.Copy).then_inc(free, 1)
                elif kind[0] == "v":
                    prev = NAT_V[NAT_V.index(n) - 1]
                    act.wait_ge(s_tfull, USE["nat", prev]["tb"] + 1)
                    if TILES[prev][0] != "mv":
                        act.wait_ge(s_keep, KEPT[TILES[prev]])
                    nc.scalar.activation(two(tall[:, :]), zz, ACT.Copy).then_inc(free, 1)
                elif kind[0] == "g":
                    if kind == "gd" and h >= 2:
                        act.wait_ge(s_tfree, USE["D", LAST_STEP["diff", h - 2]]["tb"] + 1)
                    if kind == "gw":
                        if h < 2:
                            act.wait_ge(s_tfree, USE["D", LAST_STEP["diff", 2 + h]]["tb"] + 1)
                        else:
                            act.wait_ge(s_ofree, USE["C", LAST_STEP["dil", h - 2]]["ob"] + 1)
                    if kind == "gm" and h >= 2:
                        act.wait_ge(s_gated, h - 1)
                    if kind in ("gd", "gw"):
                        act.wait_ge(s_keep, KEPT[kind, h, c] - 1)
                    nc.scalar.activation(two(gate_t[:, gate_slot(kind, h, c), :]), zz, ACT.Tanh, scale=0.5).then_inc(s_tanh, 1)
                else:
                    prev = n - 1
                    if n > FIRST_OUT:
                        act.wait_ge(s_tfull, USE["ynat", prev]["tb"] + 1 + 2 * turn)
                        if TILES[prev][2] != 1:
                            act.wait_ge(s_ofull, USE["ynat", prev]["ob"] + 1 + 2 * turn)
                    else:
                        act.wait_ge(s_tfull, USE["nat", NAT_V[-1]]["tb"] + 1)
                        act.wait_ge(s_keep, KEPT["vw", 3, 0])
                    if c == 0:
                        nc.scalar.activation(two(tall[:, :]), zz, ACT.Copy).then_inc(free, 1)
                    elif c == 1:
                        nc.scalar.activation(tall[:, 0:2 * P], z[n % 2][:, 0, 0:2 * P], ACT.Copy).then_inc(free, 1)
                    else:
                        nc.scalar.activation(tall[:, 2 * P:TOK], z[n % 2][:, 1, 0:TOK - 2 * P], ACT.Copy).then_inc(free, 1)

            def natural(n, use):
                kind, h, c = TILES[n]
                act.wait_ge(s_tfull, use["tb"] + 1)
                if kind in ("mk", "kd", "kw"):
                    i = NAT_K.index(n)
                    if i >= 1:
                        act.wait_ge(s_kout, 16 * i)
                    w = N_MEM if kind == "mk" else SEQ
                    nc.scalar.activation(k_nat[:, :, :].rearrange("p t d -> p (t d)")[:, 0:w], t_ps[:, 0:w], ACT.Copy).then_inc(s_tfree, 1)
                elif kind == "mv":
                    nc.scalar.activation(mv_nat[:, :, h * P:(h + 1) * P], t_ps[:, 0:N_MEM].rearrange("p (t d) -> p t d", t=2),
                                         ACT.Copy).then_inc(s_tfree, 1)
                else:
                    if kind == "vd" and h >= 2:
                        act.wait_ge(s_ofull, USE["C", LAST_STEP["diff", h - 2]]["ob"] + 1)
                        act.wait_ge(s_vout[h % 2], 32)
                    if kind == "vw":
                        before = ("diff", 2 + h) if h < 2 else ("dil", h - 2)
                        act.wait_ge(s_ofull, USE["C", LAST_STEP[before]]["ob"] + 1)
                        act.wait_ge(s_vout[h % 2], 64 if h < 2 else 80)
                    nc.scalar.activation(v_nat[:, h % 2, :, c * P:(c + 1) * P], t_ps[:, :].rearrange("p (t d) -> p t d", t=NBLK),
                                         ACT.Copy).then_inc(s_tfree, 1)

            def sum_values(g, b):
                bank, full, free, n = turned_bank((g, b))
                act.wait_ge(full, n + 1)
                for k in range(4):
                    dst = cat_t[:, 3 * H + k, SEQ + b:SEQ + b + 1] if g == MEMORY else o_s[:, 4 * g + k, b:b + 1]
                    turned = bank[:, k * P:(k + 1) * P]
                    last = nc.scalar.activation(turned, turned, ACT.Identity, accum_out=dst)
                last.then_inc(free, 1)

            def step_exp(t):
                kind, h, i, _ = STEPS[t]
                act.wait_ge(s_max, t + 1)
                for c in range(1 if kind == "dil" else 2):
                    w = N_MEM if kind == "mem" else (i + 1) * P
                    src = s_ps[:, c, 0:w] if kind == "mem" else probs[:, c, 0:w]
                    last = nc.scalar.activation(probs[:, c, 0:w], src, ACT.Exp, bias=st_n[:, t % 2, c:c + 1], scale=SCALE,
                                                accum_out=st_l[:, t % 2, c:c + 1])
                last.then_inc(s_exp, 1)

            def step_probs(t):
                kind, h, i, _ = STEPS[t]
                if kind != "diff":
                    act.wait_ge(s_rec, RECS[t] + 1)
                    w = N_MEM if kind == "mem" else (i + 1) * P
                    for c in range(1 if kind == "dil" else 2):
                        last = nc.scalar.activation(probs[:, c, 0:w], probs[:, c, 0:w], ACT.Identity,
                                                    scale=st_r[:, t % 2, c:c + 1])
                    last.then_inc(s_probs, 1)

            def step_turn(t, use):
                kind, h, i, _ = STEPS[t]
                w = SEQ if kind == "mem" else (i + 1) * P
                act.wait_ge(s_tfull, use["tb"] + 1)
                nc.scalar.activation(probs_T[:, 0:w], t_ps[:, 0:w], ACT.Copy).then_inc(s_tfree, 1)

            def norm(half):
                i = 2 * half + 1
                act.wait_ge(s_yrp, half + 1)
                act.wait_ge(s_yg, KT if half == 0 else KT + TWICE)
                nc.scalar.activation(nat[:, i, :], nat[:, i, :], ACT.Copy, scale=y_r[:, i:i + 1]).then_inc(s_ydone[i], 1)

            squares(0)
            squares(1)
            act.wait_ge(s_gm, 16)
            for u in range(N_PREP):
                prep_hi(0, u)
                if u in FIRST_SPLITS:
                    split_hi(FIRST_SPLITS.index(u))
            act.wait_ge(s_lamp, 1)
            nc.scalar.activation(lam_w[:, 2:4], z[1][:, 0, 0:2], ACT.Exp).then_inc(s_lame, 1)
            def slot(s, jobs, turn=0):
                if 2 <= s < QUARTERS - AHEAD:
                    split_hi(s + AHEAD, turn)
                for kind, what, use in jobs:
                    if kind == "evac":
                        evac(what, turn)
                    elif kind == "squares":
                        squares(what)
                    elif kind == "prep":
                        if what == (1, 0):
                            act.wait_ge(s_const, 16 * 8)
                        prep_hi(*what)
                    elif kind == "prep_sample":
                        act.wait_ge(s_phi, 2 * N_PREP + 1)
                        nc.scalar.activation(act_hi[:, :, SAMPLE], tok_s[:, :, :], ACT.Copy).then_inc(s_phi, 1)
                    elif kind == "nat":
                        natural(what, use)
                    elif kind == "A":
                        step_exp(what)
                    elif kind == "do":
                        sum_values(*what)
                    elif kind == "P":
                        step_probs(what)
                    elif kind == "B":
                        step_turn(what, use)
                    elif kind == "C" and STEPS[what][0] == "diff":
                        act.wait_ge(s_ofull, use["ob"] + 1)
                        if what >= 1:
                            act.wait_ge(s_tfull, USE["D", what - 1]["tb"] + 1)
                        nc.scalar.activation(o_nat[:, :], o_ps[:, 0:2 * P], ACT.Square,
                                             accum_out=st_q[:, 0, 0:1]).then_inc(s_osq, 1)
                    elif kind in ("qrows", "kvrows"):
                        act.wait_ge(s_tfull, use["tb"] + 1)
                        n = Q_ROWS[what][1] * DB if kind == "qrows" else 96
                        place = Q_ROWS[what][2] if kind == "qrows" else what
                        if kind == "kvrows":
                            act.wait_ge(s_qdram[2 - what], 16)
                        elif what == 2:
                            act.wait_ge(s_qdram[0], 16)
                        nc.scalar.activation(rows[0:n, place, :], t_ps[0:n, 0:P], ACT.Copy).then_inc(s_tfree, 1)
                    elif kind == "soft" and what[1] == 2:
                        g = what[0]
                        act.wait_ge(s_dsm, 5 * GROUPS.index(g) + 4)
                        s3 = scores_of(g)
                        nc.scalar.activation(s3, s3, ACT.Exp, scale=SCALE)
                        nc.scalar.activation(SNEW[:, 0:32], SNEW[:, 0:32], ACT.Exp, scale=SCALE).then_inc(s_dexp, 1)
                    elif kind == "ynat":
                        e = TILES[what][1]
                        for k, i in enumerate(Y_BLOCKS[TILES[what][2]]):
                            n = P if i < NBLK else DB
                            cols = bass.ds(e * P + 2 * P * turn, P)
                            src = nat[:, i, cols] if i < NBLK else y_s_nat[:, cols]
                            if i < NBLK:
                                act.wait_ge(s_tfree, use["tb"] + 1 + 2 * turn)
                            else:
                                act.wait_ge(s_ofree, use["ob"] + 1 + 2 * turn)
                            if YSQ[what] + k:
                                act.wait_ge(s_ysq, YSQ[what] + k + 10 * turn)
                            nc.scalar.activation(o_nat[0:n, 0:P], src, ACT.Square,
                                                 accum_out=y_ss[0:n, i, bass.ds(e + 2 * turn, 1)]).then_inc(s_ysq, 1)
                    elif kind == "norm":
                        norm(0)
                if IN_END - 3 <= s <= IN_END:
                    if s == IN_END - 3:
                        act.wait_ge(s_tfree, USE["D", LAST_STEP["diff", 3]]["tb"] + 1)
                        act.wait_ge(s_ofree, USE["C", LAST_STEP["dil", 3]]["ob"] + 1)
                        act.wait_ge(s_fin, 3)
                    r = s - (IN_END - 3)
                    act.wait_ge(s_quarter, IN_END - 3 + r)
                    for kt in range(4 * r, 4 * r + 4):
                        if kt >= 3 * H:
                            act.wait_ge(s_gated, kt - 3 * H + 1)
                        nc.scalar.activation(act_hi[:, kt, :], cat_t[:, kt, :], ACT.Copy).then_inc(s_chi, 1)

            for s, jobs in enumerate(PLAN):
                if s in LOOPS:
                    with act.Fori(0, LOOPS[s]) as turn:
                        for k in range(PER_TURN):
                            slot(s + k, PLAN[s + k], turn)
                elif not in_loop(s):
                    slot(s, jobs)
            norm(1)

        @block.vector
        def _(dve):
            chain = [0]

            def link(ins):
                chain[0] += 1
                ins.then_inc(s_chain, 1)
                dve.wait_ge(s_chain, chain[0])

            def scale_tokens(i):
                n = DB if i == 6 else P
                view = x_s_nat if i == 6 else nat[:, i % 4, :]
                dve.wait_ge(s_rr, ORDER_OF[i] + 1)
                nc.vector.tensor_scalar(view, view, tok_r[0:n, i:i + 1], None, ALU.mult).then_inc(s_scaled, 1)

            def prep_lo(pair, u):
                use = prep_base(pair) + u
                g = gmn if pair == 0 else gn
                dve.wait_ge(s_phi, use + 1 + (use > 2 * N_PREP))
                first = N_MEM if pair == 1 else 0
                for k in range(2):
                    kt = 2 * u + k
                    cols = slice(first, first + 2 * P)
                    last = nc.vector.scalar_tensor_tensor(act_lo[:, kt, cols], s_ps[:, use % 2, k * 2 * P:(k + 1) * 2 * P],
                                                          g[:, kt:kt + 1], act_hi[:, kt, cols].bitcast(F32), ALU.mult, ALU.subtract)
                last.then_inc(s_plo, 1)

            def prep_sample():
                use = 2 * N_PREP
                dve.wait_ge(s_pfull, use + 1)
                src = s_ps[:, use % 2, 0:KT * DB].rearrange("p (k b) -> p k b", b=DB)
                nc.vector.tensor_tensor(tok_s[:, :, :], src, gn[:, :].unsqueeze(2).broadcast_to((P, KT, DB)), ALU.mult).then_inc(s_phi, 1)
                dve.wait_ge(s_phi, 2 * N_PREP + 2)
                nc.vector.tensor_tensor(act_lo[:, :, SAMPLE], tok_s[:, :, :], act_hi[:, :, SAMPLE].bitcast(F32), ALU.subtract).then_inc(s_plo, 1)

            def split_lo(q, turn=0):
                dve.wait_ge(s_hi, q + 1 + PER_TURN * turn)
                nc.vector.tensor_tensor(w_lo[:, q % SPLIT_RING, :], w_raw[:, q % WIN_RING, :],
                                        w_hi[:, q % SPLIT_RING, :].bitcast(F32), ALU.subtract).then_inc(s_lo, 1)

            def evac(n):
                kind, h, c = TILES[n]
                if kind[0] != "g":
                    return
                slot = gate_t[:, gate_slot(kind, h, c), :]
                dve.wait_ge(s_tanh, TANHS[n] + 1)
                two = slot.rearrange("p (a t) -> p a t", a=2)
                nc.vector.scalar_tensor_tensor(two, two, 1.0, z[n % 2][:, :, 0:HALF], ALU.add, ALU.mult).then_inc(s_zfree[n % 2], 1)
                if kind == "gm":
                    dve.wait_ge(s_zfree[n % 2], n // 2 + 1)
                    dve.wait_ge(s_ofree, USE["C", LAST_STEP["mem", 3]]["ob"] + 1)
                    _, _, free, last_use = turned_bank((WINDOW, DB - 1))
                    dve.wait_ge(free, last_use + 1)
                    out = cat_t[:, cat_slot(kind, h, c), :]
                    nc.vector.scalar_tensor_tensor(out, out, 0.5, slot, ALU.mult, ALU.mult).then_inc(s_gated, 1)

            def step_max(t, use):
                kind, h, i, _ = STEPS[t]
                tp = t % 2
                w = N_MEM if kind == "mem" else (i + 1) * P
                nc_ = 1 if kind == "dil" else 2
                dve.wait_ge(s_sfull, use["sb"] + 1)
                if kind != "mem":
                    bi = bias_index(kind, h)
                    dve.wait_ge(s_bias[bi % 2], 16 * (bi // 2 + 1))
                for c in range(nc_):
                    if kind == "mem":
                        last = nc.vector.reduce_max(st_m[:, tp, c:c + 1], s_ps[:, c, 0:w], AX_X)
                    else:
                        last = nc.vector.tensor_tensor_reduce(probs[:, c, 0:w], s_ps[:, c, 0:w], bias[:, bi % 2, SEQ - w:SEQ],
                                                              1.0, LOWEST, ALU.add, ALU.max, st_m[:, tp, c:c + 1])
                if kind == "mem":
                    link(last)
                else:
                    last.then_inc(s_sfree, 1)
                    dve.wait_ge(s_sfree, SCORES_READ[t])
                nc.vector.tensor_scalar(st_n[:, tp, 0:nc_], st_m[:, tp, 0:nc_], -SCALE, None, ALU.mult).then_inc(s_max, 1)

            def step_probs(t, use):
                kind, h, i, _ = STEPS[t]
                tp = t % 2
                w = N_MEM if kind == "mem" else (i + 1) * P
                nc_ = 1 if kind == "dil" else 2
                dve.wait_ge(s_exp, t + 1)
                if kind == "mem":
                    nc.vector.reciprocal(st_r[:, tp, 0:2], st_l[:, tp, 0:2]).then_inc(s_rec, 1)
                elif kind == "dil":
                    nc.vector.reciprocal(st_r[:, tp, 0:1], st_l[:, tp, 0:1]).then_inc(s_rec, 1)
                else:
                    link(nc.vector.reciprocal(st_r[:, tp, 0:2], st_l[:, tp, 0:2]))
                    if t == 0:
                        dve.wait_ge(s_neglam, 1)
                    nc.vector.tensor_scalar(st_r[:, tp, 2:3], st_r[:, tp, 1:2], lam_w[:, 5:6], None, ALU.mult)
                    link(nc.vector.tensor_scalar(probs[:, 0, 0:w], probs[:, 0, 0:w], st_r[:, tp, 0:1], None, ALU.mult))
                    nc.vector.scalar_tensor_tensor(probs[:, 0, 0:w], probs[:, 1, 0:w], st_r[:, tp, 2:3], probs[:, 0, 0:w],
                                                   ALU.mult, ALU.add).then_inc(s_probs, 1)

            def step_out(t, use):
                kind, h, i, _ = STEPS[t]
                if kind == "diff":
                    dve.wait_ge(s_orstd, t + 1)
                    nc.vector.tensor_scalar(o_nat[:, :], o_ps[:, 0:2 * P], st_q[:, 1, 0:1], None, ALU.mult).then_inc(s_ofree, 1)
                elif kind == "dil":
                    n = AT["gw", h, 0]
                    dve.wait_ge(s_zfree[n % 2], n // 2 + 1)
                    dve.wait_ge(s_ofull, use["ob"] + 1)
                    cols = slice(i * P, (i + 1) * P)
                    nc.vector.scalar_tensor_tensor(cat_t[:, 2 * H + h, cols], o_ps[:, 0:P], 0.5, gate_t[:, gate_slot("gw", h, 0), cols],
                                                   ALU.mult, ALU.mult).then_inc(s_ofree, 1)
                else:
                    dve.wait_ge(s_ofull, use["ob"] + 1)
                    nc.vector.tensor_copy(cat_t[:, 3 * H + h, 2 * i * P:2 * (i + 1) * P], o_ps[:, 0:2 * P]).then_inc(s_ofree, 1)

            def step_gate(t, use):
                kind, h, i, _ = STEPS[t]
                n = AT["gd", h, 1]
                dve.wait_ge(s_zfree[n % 2], n // 2 + 1)
                dve.wait_ge(s_zfree[(n - 1) % 2], (n - 1) // 2 + 1)
                dve.wait_ge(s_tfull, use["tb"] + 1)
                cols = slice(i * P, (i + 1) * P)
                for c in range(2):
                    last = nc.vector.scalar_tensor_tensor(cat_t[:, 2 * h + c, cols], t_ps[:, c * P:(c + 1) * P], gsub_c[:, c:c + 1],
                                                          gate_t[:, gate_slot("gd", h, c), cols], ALU.mult, ALU.mult)
                last.then_inc(s_tfree, 1)

            done = [0]

            def key_unit(g, b, t):
                i = ROWS.index((g, b))
                slot = done[0] % PAGE_RING
                s3 = scores_of(g)
                dve.wait_ge(s_qbc[i % 2], 16 * (i // 2 + 1))
                dve.wait_ge(s_page[slot], LANDED[done[0]])
                for k in range(4):
                    col = k % 2 * 16 + b * 2 + k // 2 if g < WINDOW else b * H + k
                    seg = pages[:, slot, k * P:(k + 1) * P]
                    last = nc.vector.tensor_tensor_reduce(seg, seg, q_bc[:, i % 2, k * P:(k + 1) * P], 1.0, 0.0,
                                                          ALU.mult, ALU.add, s3[:, t, col:col + 1])
                last.then_inc(s_unit, 1)
                done[0] += 1

            def value_unit(g, b, t):
                i = PAIRS.index((g, b // 2))
                slot = done[0] % PAGE_RING
                acc = v_acc[:, 2 * (i % 2) + b % 2, :]
                if t == 0 and i >= 2:
                    before_g, before_p = PAIRS[i - 2]
                    _, full, _, n = turned_bank((before_g, 2 * before_p + b % 2))
                    dve.wait_ge(full, n + 1)
                dve.wait_ge(s_page[slot], LANDED[done[0]])
                if t:
                    dve.wait_ge(s_unit, UNIT_AT[True, (g, b, t - 1)] + 1)
                n = 2 if g < WINDOW else 4
                for k in range(n):
                    seg = slice(k * 512 // n, (k + 1) * 512 // n)
                    if g < WINDOW:
                        col = 16 * g + b * 2 + k
                        a = dec_a[:, t, col:col + 1]
                    else:
                        a = scores_of(g)[:, t, b * H + k:b * H + k + 1]
                    if t == 0:
                        last = nc.vector.tensor_scalar(acc[:, seg], pages[:, slot, seg], a, None, ALU.mult)
                    else:
                        last = nc.vector.scalar_tensor_tensor(acc[:, seg], pages[:, slot, seg], a, acc[:, seg], ALU.mult, ALU.add)
                last.then_inc(s_unit, 1)
                done[0] += 1

            def soft(g, k, use):
                T = G_TILES[g]
                s3 = scores_of(g)
                snew, mb, m1, l1, lr = SNEW[:, 0:32], MB[:, 0:32], M1[:, 0:32], L1[:, 0:32], LR[:, 0:32]
                over = lambda ap: ap.unsqueeze(1).broadcast_to((P, T, 32))
                if k == 0:
                    dve.wait_ge(s_unit, UNIT_AT[False, (g, DB - 1, T - 1)] + 1)
                    if g < WINDOW:
                        v = s3.rearrange("p t (n h) -> p t n h", h=2)
                        w = bd[:, :, 2 * g:2 * g + 2].unsqueeze(2).broadcast_to((P, T, 16, 2))
                    else:
                        v = s3.rearrange("p t (n h) -> p t n h", h=H)
                        w = bw[:, :, g - WINDOW, :].unsqueeze(2).broadcast_to((P, T, DB, H))
                    link(nc.vector.tensor_tensor(v, v, w, ALU.add))
                    nc.vector.tensor_reduce(m1, s3.rearrange("p t n -> p n t"), AX_X, ALU.max).then_inc(s_dsm, 1)
                    if g < WINDOW:
                        dve.wait_ge(s_keep, KEPT["kd", 2 * g + 1, 1])
                        for c in range(2):
                            prod = PROD[:, c * 16:(c + 1) * 16].rearrange("p (b h) -> p h b", h=2)
                            qv = q_s[:, 4 * g:4 * g + 4, :].rearrange("p (h c) b -> p c h b", c=2)[:, c]
                            kv = k_s[:, 4 * g:4 * g + 4, :].rearrange("p (h c) b -> p c h b", c=2)[:, c]
                            last = nc.vector.tensor_tensor(prod, qv, kv, ALU.mult)
                        last.then_inc(s_dprod, 1)
                    elif g == WINDOW:
                        dve.wait_ge(s_keep, KEPT["kw", 3, 0])
                        prod = PROD[:, 0:32].rearrange("p (b h) -> p h b", h=H)
                        nc.vector.tensor_tensor(prod, q_s[:, 8:12, :], k_s[:, 8:12, :], ALU.mult).then_inc(s_dprod, 1)
                    else:
                        nc.vector.memset(PROD[:, 0:32], 0.0).then_inc(s_dprod, 1)
                if k == 1:
                    dve.wait_ge(s_tfull, use["tb"] + 1)
                    nc.vector.reduce_max(MB[0:32, 0:1], t_ps[0:32, 0:P], AX_X).then_inc(s_tfree, 1)
                    dve.wait_ge(s_tfree, use["tb"] + 1)
                    nc.vector.tensor_scalar(DIAG[0:32, 0:32], ident[0:32, 0:32], MB[0:32, 0:1], None, ALU.mult).then_inc(s_dsm, 1)
                if k == 2:
                    dve.wait_ge(s_ofull, use["ob"] + 1)
                    link(nc.vector.tensor_scalar(snew, o_ps[:, 32:64], NEW_BIAS[g], None, ALU.add))
                    nc.vector.tensor_tensor(mb, o_ps[:, 0:32], snew, ALU.max).then_inc(s_ofree, 1)
                    dve.wait_ge(s_ofree, use["ob"] + 1)
                    nc.vector.tensor_tensor(s3, s3, over(mb), ALU.subtract).then_inc(s_dsm, 1)
                    nc.vector.tensor_tensor(snew, snew, mb, ALU.subtract).then_inc(s_dsm, 1)
                    dve.wait_ge(s_dexp, GROUPS.index(g) + 1)
                    nc.vector.tensor_reduce(l1, s3.rearrange("p t n -> p n t"), AX_X, ALU.add).then_inc(s_dsm, 1)
                if k == 3:
                    dve.wait_ge(s_ofull, use["ob"] + 1)
                    nc.vector.tensor_tensor(lr, o_ps[:, 0:32], snew, ALU.add).then_inc(s_ofree, 1)
                    dve.wait_ge(s_ofree, use["ob"] + 1)
                    link(nc.vector.reciprocal(lr, lr))
                    nc.vector.tensor_tensor(snew, snew, lr, ALU.mult)
                    link(nc.vector.tensor_tensor(s3, s3, over(lr), ALU.mult))
                if k == 4:
                    if g < WINDOW:
                        n = slice(16 * g, 16 * g + 16)
                        nc.vector.scalar_tensor_tensor(dec_a[:, :, n], s3[:, :, 16:32], lam_w[:, 5:6], s3[:, :, 0:16], ALU.mult, ALU.add)
                        link(nc.vector.scalar_tensor_tensor(a_new[:, 0, n], SNEW[:, 16:32], lam_w[:, 5:6], SNEW[:, 0:16], ALU.mult, ALU.add))
                    elif g == WINDOW:
                        link(nc.vector.tensor_copy(a_new[:, 1, :], snew))

            def finish(k, use):
                if k == 0:
                    _, _, free, last_use = turned_bank((WINDOW, DB - 1))
                    dve.wait_ge(free, last_use + 1)
                    dve.wait_ge(s_keep, KEPT["vw", 3, 0])
                    od = o_s[:, 0:8, :]
                    for g in range(2):
                        an = a_new[:, 0, 16 * g:16 * g + 16].rearrange("p (b h) -> p h b", h=2)
                        for c in range(2):
                            vd = v_s[:, 4 * g:4 * g + 4, :].rearrange("p (h c) b -> p c h b", c=2)[:, c]
                            link(nc.vector.tensor_tensor(tmp[:, 0:2, :], vd, an, ALU.mult))
                            o1 = od[:, 4 * g:4 * g + 4, :].rearrange("p (h c) b -> p c h b", c=2)[:, c]
                            link(nc.vector.tensor_tensor(o1, o1, tmp[:, 0:2, :], ALU.add))
                    aw = a_new[:, 1, :].rearrange("p (b h) -> p h b", h=H)
                    link(nc.vector.tensor_tensor(tmp[:, 0:4, :], v_s[:, 8:12, :], aw, ALU.mult))
                    link(nc.vector.tensor_tensor(o_s[:, 8:12, :], o_s[:, 8:12, :], tmp[:, 0:4, :], ALU.add))
                    nc.vector.tensor_tensor(SQ.rearrange("p (t b) -> p t b", b=DB), od, od, ALU.mult).then_inc(s_fin, 1)
                if k == 1:
                    dve.wait_ge(s_ofull, use["ob"] + 1)
                    link(nc.vector.tensor_copy(L1, o_ps[:, 0:64]))
                    l3 = L1.rearrange("p (h c b) -> p h c b", c=2, b=DB)
                    nc.vector.tensor_tensor(M1[:, 0:32].rearrange("p (h b) -> p h b", b=DB), l3[:, :, 0, :], l3[:, :, 1, :],
                                            ALU.add).then_inc(s_ofree, 1)
                if k == 2:
                    dve.wait_ge(s_finp, 1)
                    r3 = M1[:, 32:64].rearrange("p (h b) -> p h b", b=DB)
                    for c in range(2):
                        o1 = o_s[:, 0:8, :].rearrange("p (h c) b -> p c h b", c=2)[:, c]
                        link(nc.vector.tensor_tensor(o1, o1, r3, ALU.mult))
                        link(nc.vector.tensor_scalar(o1, o1, gsub_c[:, c:c + 1], None, ALU.mult))
                    dve.wait_ge(s_keep, KEPT["gw", 3, 0])
                    nc.vector.tensor_tensor(cat_t[:, 0:8, SAMPLE], o_s[:, 0:8, :], g_s[:, 0:8, :], ALU.mult).then_inc(s_fin, 1)
                    nc.vector.scalar_tensor_tensor(cat_t[:, 8:12, SAMPLE], o_s[:, 8:12, :], 0.5, g_s[:, 8:12, :],
                                                   ALU.mult, ALU.mult).then_inc(s_fin, 1)

            def times_g(n, turn=0):
                _, e, c = TILES[n]
                cols = bass.ds(e * P + 2 * P * turn, P)
                if n == FIRST_OUT:
                    dve.wait_ge(s_gf, 16)
                dve.wait_ge(s_ysq, YSQ[n + 1] + 10 * turn)
                blocks = ((0, 4), (0, 2), (2, 4))[c]
                tile = nat[:, blocks[0]:blocks[1], cols]
                g = g_fin[:, cols].unsqueeze(1).broadcast_to((P, blocks[1] - blocks[0], P))
                last = nc.vector.tensor_tensor(tile, tile, g, ALU.mult)
                if c != 1:
                    last = nc.vector.tensor_tensor(y_s_nat[:, cols], y_s_nat[:, cols], g_fin[0:DB, cols], ALU.mult)
                last.then_inc(s_yg, 1)

            def mean(half):
                dve.wait_ge(s_ysq, YSQ[N_TILES - TWICE] if half == 0 else YSQ[N_TILES])
                i, j = ((0, 2), (2, 5))[half]
                nc.vector.tensor_reduce(y_r[:, i:j], y_ss[:, i:j, :], AX_X, ALU.add).then_inc(s_yr, 1)

            def norm(half):
                dve.wait_ge(s_yrp, half + 1)
                dve.wait_ge(s_yg, KT if half == 0 else KT + TWICE)
                i = 2 * half
                nc.vector.tensor_scalar(nat[:, i, :], nat[:, i, :], y_r[:, i:i + 1], None, ALU.mult).then_inc(s_ydone[i], 1)
                if half:
                    nc.vector.tensor_scalar(y_s_nat, y_s_nat, y_r[0:DB, 4:5], None, ALU.mult).then_inc(s_ydone[4], 1)

            nc.vector.memset(ones[:, :], 1.0).then_inc(s_init, 1)
            nc.vector.memset(power[:, :], -0.5).then_inc(s_init, 1)
            nc.vector.memset(y_ss[:, :, :], 0.0)
            scale_tokens(0)
            scale_tokens(1)
            dve.wait_ge(s_gm, 16)
            for u in range(N_PREP):
                prep_lo(0, u)
                if u in FIRST_SPLITS:
                    split_lo(FIRST_SPLITS.index(u))
                if u == 5:
                    dve.wait_ge(s_const, 16 * 8)
                    nc.vector.tensor_tensor(lam_w[:, 0:1], lam_in[:, 0:1], lam_in[:, 1:2], ALU.mult)
                    nc.vector.tensor_tensor(lam_w[:, 1:2], lam_in[:, 2:3], lam_in[:, 3:4], ALU.mult).then_inc(s_lam, 1)
                    nc.vector.tensor_scalar(gsub_c[:, :], gsub[:, :], 0.5 * (1.0 - LAM_INIT), None, ALU.mult)
            dve.wait_ge(s_lame, 1)
            link(nc.vector.tensor_tensor(lam_w[:, 4:5], lam_w[:, 3:4], lam_w[:, 2:3], ALU.subtract))
            nc.vector.tensor_scalar(lam_w[:, 5:6], lam_w[:, 4:5], -LAM_INIT, None, ALU.add).then_inc(s_neglam, 1)
            def slot(s, jobs, turn=0):
                if 2 <= s < QUARTERS - AHEAD:
                    split_lo(s + AHEAD, turn)
                for kind, what, use in jobs:
                    if kind == "evac":
                        evac(what)
                    elif kind == "scale":
                        scale_tokens(what)
                    elif kind == "prep":
                        prep_lo(*what)
                    elif kind == "prep_sample":
                        prep_sample()
                    elif kind == "A":
                        step_max(what, use)
                    elif kind == "P":
                        step_probs(what, use)
                    elif kind == "C":
                        step_out(what, use)
                    elif kind == "D":
                        step_gate(what, use)
                    elif kind == "dk":
                        key_unit(*what)
                    elif kind == "dv":
                        value_unit(*what)
                    elif kind == "soft":
                        soft(*what, use)
                    elif kind == "fin":
                        finish(what, use)
                    elif kind == "ynat":
                        e = TILES[what][1]
                        cols = bass.ds(e * P + 2 * P * turn, P)
                        if e == 0:
                            for i in range(5):
                                dve.wait_ge(s_res[i], 16)
                        dve.wait_ge(s_tfull, use["tb"] + 1 + 2 * turn)
                        c = TILES[what][2]
                        a, b = ((0, 4), (0, 2), (2, 4))[c]
                        nc.vector.tensor_tensor(nat[:, a:b, cols], nat[:, a:b, cols], t_ps[:, a * P:b * P].rearrange("p (t f) -> p t f", f=P),
                                                ALU.add).then_inc(s_tfree, 1)
                        if c != 1:
                            dve.wait_ge(s_ofull, use["ob"] + 1 + 2 * turn)
                            nc.vector.tensor_tensor(y_s_nat[:, cols], y_s_nat[:, cols], o_ps[0:DB, 0:P], ALU.add).then_inc(s_ofree, 1)
                        if what > FIRST_OUT:
                            times_g(what - 1, turn)
                    elif kind == "mean":
                        mean(what)
                    elif kind == "norm":
                        norm(what)
                if IN_END - 3 <= s <= IN_END:
                    for kt in range(4 * (s - IN_END + 3), 4 * (s - IN_END + 3) + 4):
                        dve.wait_ge(s_chi, kt + 1)
                        nc.vector.tensor_tensor(act_lo[:, kt, :], cat_t[:, kt, :], act_hi[:, kt, :].bitcast(F32),
                                                ALU.subtract).then_inc(s_clo, 1)
            for s, jobs in enumerate(PLAN):
                if s in LOOPS:
                    with dve.Fori(0, LOOPS[s]) as turn:
                        for k in range(PER_TURN):
                            slot(s + k, PLAN[s + k], turn)
                elif not in_loop(s):
                    slot(s, jobs)
            mean(1)
            times_g(N_TILES - 1)
            norm(1)

        @block.gpsimd
        def _(pool):
            chain = [0]

            def link(ins):
                chain[0] += 1
                ins.then_inc(s_pchain, 1)
                pool.wait_ge(s_pchain, chain[0])

            def token_rstd(i):
                n = DB if i == 6 else P
                pool.wait_ge(s_ss, ORDER_OF[i] + 1)
                link(nc.gpsimd.tensor_scalar(tok_r[0:n, i:i + 1], tok_ss[0:n, i:i + 1], 1.0 / D_MODEL, EPS, ALU.mult, ALU.add))
                nc.gpsimd.tensor_tensor(tok_r[0:n, i:i + 1], tok_r[0:n, i:i + 1], power[0:n, 0:1], ALU.pow).then_inc(s_rr, 1)

            def keep(n, turn):
                kind, h, c = TILES[n]
                pool.wait_ge(s_zfree[n % 2], n // 2 + 1 + turn)
                if kind[0] == "q":
                    t = cat_slot(kind, h, c)
                    dst = q_s[:, bass.ds(t + 2 * turn, 1), :].rearrange("p a b -> p (a b)")
                    src = cat[:, bass.ds(t * TOK + SEQ + 2 * TOK * turn, DB)]
                elif kind[0] == "k":
                    dst, src = k_s[:, sample_slot(kind, h, c), :], kT_t[:, key_slot(kind, h, c), SAMPLE]
                elif kind[0] == "v":
                    dst, src = v_s[:, sample_slot(kind, h, c), :], tall[:, SAMPLE]
                else:
                    dst, src = g_s[:, sample_slot(kind, h, c), :], gate_t[:, gate_slot(kind, h, c), SAMPLE]
                nc.gpsimd.tensor_copy(dst, src).then_inc(s_keep, 1)

            def y_rstd(half):
                i, j = ((0, 2), (2, 5))[half]
                pool.wait_ge(s_yr, half + 1)
                link(nc.gpsimd.tensor_scalar(y_sum[:, i:j], y_r[:, i:j], 1.0 / D_MODEL, EPS, ALU.mult, ALU.add))
                nc.gpsimd.tensor_tensor(y_r[:, i:j], y_sum[:, i:j], power[:, i:j], ALU.pow).then_inc(s_yrp, 1)

            pool.wait_ge(s_init, 2)
            token_rstd(0)
            token_rstd(1)
            def slot(s, jobs, turn=0):
                for kind, what, use in jobs:
                    if kind == "squares":
                        token_rstd(what)
                    elif kind == "mean":
                        y_rstd(what)
                    elif kind == "evac" and TILES[what] in KEPT:
                        keep(what, turn)
                    elif kind == "C" and STEPS[what][0] == "diff":
                        t = what
                        pool.wait_ge(s_osq, t + 1)
                        link(nc.gpsimd.tensor_scalar(st_q[:, 1, 1:2], st_q[:, 0, 0:1], 1.0 / (2 * P), EPS, ALU.mult, ALU.add))
                        if t >= 1:
                            pool.wait_ge(s_ofree, USE["C", t - 1]["ob"] + 1)
                        nc.gpsimd.tensor_tensor(st_q[:, 1, 0:1], st_q[:, 1, 1:2], power[:, 0:1], ALU.pow).then_inc(s_orstd, 1)
                    elif kind == "fin" and what == 1:
                        pool.wait_ge(s_ofree, use["ob"] + 1)
                        link(nc.gpsimd.tensor_scalar(M1[:, 0:32], M1[:, 0:32], 1.0 / (2 * P), EPS, ALU.mult, ALU.add))
                        nc.gpsimd.tensor_tensor(M1[:, 32:64], M1[:, 0:32], power[:, 0:32], ALU.pow).then_inc(s_finp, 1)
            for s, jobs in enumerate(PLAN):
                if s in LOOPS and s < IN_END:
                    with pool.Fori(0, LOOPS[s]) as turn:
                        for k in range(PER_TURN):
                            slot(s + k, PLAN[s + k], turn)
                elif not in_loop(s):
                    slot(s, jobs)
            y_rstd(1)


_INS = ["x_prompt", "x_sample", "mem_prompt", "cache_k_diff", "cache_v_diff", "page_table", "cache_k_win", "cache_v_win",
        "cache_mem_k", "cache_mem_v", "g_norm", "w_in", "lambda_q1", "lambda_k1", "lambda_q2", "lambda_k2", "g_subln",
        "g_mem_norm", "w_mem_kv", "w_out", "g_final"]
_OUTS = [(1, SEQ, D_MODEL), (DB, 1, D_MODEL), (1, 1, SEQ, H, 2, P), (1, 1, SEQ, H, 2 * P), (1, 1, SEQ, H, P), (1, 1, SEQ, H, P),
         (1, 1, N_MEM, H, P), (1, 1, N_MEM, H, P), (1, DB, 1, H, 2, P), (1, DB, 1, H, 2 * P), (1, DB, 1, H, P), (1, DB, 1, H, P)]


def kernel(**inputs):
    import concourse.bacc as bacc
    from concourse.bass_utils import run_bass_kernel_spmd

    nc = bacc.Bacc("TRN2", target_bir_lowering=False, num_devices=1, dynamic_dma_scratch_size=1024)
    arrays, args = {}, []
    given = {name: np.ascontiguousarray(inputs[name]) for name in _INS}
    given["bias_tables"], given["bias_small"], given["identity"] = constants()
    for name, a in given.items():
        arrays[f"in_{name}_dram"] = a
        args.append(nc.dram_tensor(f"in_{name}_dram", a.shape, mybir.dt.from_np(a.dtype), kind="ExternalInput").ap())
    for i, shape in enumerate(_OUTS):
        args.append(nc.dram_tensor(f"out_{i}_dram", shape, F32, kind="ExternalOutput").ap())
    args.append(nc.dram_tensor("q_rows_dram", (KT * DB, P), F32, kind="Internal").ap())
    hybrid_decoder(nc, *args)
    r = run_bass_kernel_spmd(nc, [arrays], core_ids=[0])
    return tuple(r.results[0][f"out_{i}_dram"] for i in range(len(_OUTS)))
```
